# Optimizing a Trainium2 kernel written in Bass

```python
import jax, jax.numpy as jnp
from jax import lax
import numpy as np

D_MODEL = 1024
BATCH = 1
SEQ = 512
DEPTH = 2

GRID_W = 64
CTX_LEN = 256
NA_HEAD_DIM = 64
NA_HEADS = (D_MODEL // 2) // NA_HEAD_DIM
NA_WIDTH = NA_HEADS * NA_HEAD_DIM
NA_WIN_H = 8
NA_WIN_W = 16
NA_QBLK_W = 16
NA_KBLK_W = 32
RET_HEAD_DIM = 128
RET_HEADS = (D_MODEL // 2) // RET_HEAD_DIM
RET_WIDTH = RET_HEADS * RET_HEAD_DIM
RET_CHUNK = 128
MIX_WIDTH = NA_WIDTH + RET_WIDTH
IN_COLS = 3 * NA_WIDTH + 5 * RET_WIDTH
ROPE_BASE = 10000.0
N_EXPERTS = 32
N_GROUPS = 8
EXPERTS_PER_GROUP = N_EXPERTS // N_GROUPS
TOP_K = 2
D_FF_EXPERT = D_MODEL // 2
MOE_BLOCK = 128
NORM_EPS = 1e-6
NEG_INF = -1e30

kernel_name = 'hybrid_na_retention_moe_dit'

def _rmsnorm(x, w):
    xf = x.astype(jnp.float32)
    y = xf * lax.rsqrt(jnp.mean(xf * xf, axis=-1, keepdims=True) + NORM_EPS)
    return (y * w.astype(jnp.float32)).astype(x.dtype)

def _modulate(x, w, shift, scale):
    return _rmsnorm(x, w) * (1.0 + scale) + shift

def _head_norm(o):
    mu = jnp.mean(o, axis=-1, keepdims=True)
    var = jnp.mean(jnp.square(o - mu), axis=-1, keepdims=True)
    return (o - mu) * lax.rsqrt(var + 1e-5)

def _axial_rope(x):
    B, L, H, d = x.shape
    half = d // 4
    t = jnp.arange(L)
    rows = (t // GRID_W).astype(jnp.float32)
    cols = (t % GRID_W).astype(jnp.float32)
    freqs = ROPE_BASE ** (-jnp.arange(half, dtype=jnp.float32) / half)
    ang = jnp.stack([rows[:, None] * freqs, cols[:, None] * freqs], axis=1)
    cos = jnp.cos(ang)[None, :, None]
    sin = jnp.sin(ang)[None, :, None]
    xr = x.astype(jnp.float32).reshape(B, L, H, 2, 2, half)
    x1, x2 = xr[..., 0, :], xr[..., 1, :]
    out = jnp.stack([x1 * cos - x2 * sin, x1 * sin + x2 * cos], axis=-2)
    return out.reshape(B, L, H, d).astype(x.dtype)

def _na_tables():
    n_cb = GRID_W // NA_QBLK_W
    qcol = np.arange(GRID_W).reshape(n_cb, NA_QBLK_W)
    kstart = np.clip(np.arange(n_cb) * NA_QBLK_W - NA_WIN_W // 2, 0, GRID_W - NA_KBLK_W)
    kcol = kstart[:, None] + np.arange(NA_KBLK_W)
    c0 = np.clip(qcol - NA_WIN_W // 2, 0, GRID_W - NA_WIN_W)
    valid = (kcol[:, None, :] >= c0[:, :, None]) & (kcol[:, None, :] < c0[:, :, None] + NA_WIN_W)
    dc_idx = np.clip(kcol[:, None, :] - qcol[:, :, None] + NA_WIN_W - 1, 0, 2 * NA_WIN_W - 2)
    return kcol, valid, dc_idx

def _neighborhood_attention(q, k, v, k_ctx, v_ctx, rpb):
    B, L, H, d = q.shape
    rows = L // GRID_W
    kh = min(NA_WIN_H, rows)
    kcol, valid, dc_idx = _na_tables()
    n_cb = GRID_W // NA_QBLK_W
    qg = q.reshape(B, rows, n_cb, NA_QBLK_W, H, d)
    kg = k.reshape(B, rows, GRID_W, H, d)
    vg = v.reshape(B, rows, GRID_W, H, d)
    scale = d ** -0.5
    mask = jnp.asarray(valid)[:, :, None, :]
    rpb_c = rpb[:, :, jnp.asarray(dc_idx)]
    n_lat = kh * NA_KBLK_W

    def row(r):
        r0 = jnp.clip(r - kh // 2, 0, rows - kh)
        kr = lax.dynamic_slice_in_dim(kg, r0, kh, axis=1)[:, :, kcol]
        vr = lax.dynamic_slice_in_dim(vg, r0, kh, axis=1)[:, :, kcol]
        qr = qg[:, r]
        s_lat = jnp.einsum('bjqhd,bkjnhd->bhjqkn', qr, kr).astype(jnp.float32) * scale
        dr_idx = r0 + jnp.arange(kh) - r + (NA_WIN_H - 1)
        bias = jnp.transpose(rpb_c[:, dr_idx], (0, 2, 3, 1, 4)).astype(jnp.float32)
        s_lat = jnp.where(mask, s_lat + bias, NEG_INF).reshape(B, H, n_cb, NA_QBLK_W, n_lat)
        s_ctx = jnp.einsum('bjqhd,bmhd->bhjqm', qr, k_ctx).astype(jnp.float32) * scale
        p = jax.nn.softmax(jnp.concatenate([s_lat, s_ctx], axis=-1), axis=-1).astype(v.dtype)
        p_lat = p[..., :n_lat].reshape(B, H, n_cb, NA_QBLK_W, kh, NA_KBLK_W)
        o = (jnp.einsum('bhjqkn,bkjnhd->bjqhd', p_lat, vr)
             + jnp.einsum('bhjqm,bmhd->bjqhd', p[..., n_lat:], v_ctx))
        return o.reshape(B, GRID_W, H, d)

    out = lax.map(row, jnp.arange(rows))
    return jnp.transpose(out, (1, 0, 2, 3, 4)).reshape(B, L, H, d)

def _ctx_attention(q, k, v):
    s = jnp.einsum('bqhd,bkhd->bhqk', q, k).astype(jnp.float32) * (q.shape[-1] ** -0.5)
    p = jax.nn.softmax(s, axis=-1).astype(v.dtype)
    return jnp.einsum('bhqk,bkhd->bqhd', p, v)

def _retention_final_state(k, v, log_g):
    L = k.shape[1]
    w = jnp.exp((L - 1.0 - jnp.arange(L, dtype=jnp.float32))[:, None] * log_g[None, :])
    return jnp.einsum('bmhd,bmhe->bhde', k * w[None, :, :, None], v)

def _retention_chunkwise(q, k, v, log_g, s0):
    B, L, H, d = q.shape
    C = RET_CHUNK
    n = L // C
    pos = jnp.arange(C, dtype=jnp.float32)
    diff = pos[:, None] - pos[None, :]
    intra = jnp.where(diff >= 0, jnp.exp(jnp.maximum(diff, 0.0)[None] * log_g[:, None, None]), 0.0)
    q_dec = jnp.exp((pos[:, None] + 1.0) * log_g[None, :])[None, :, :, None]
    k_dec = jnp.exp((C - 1.0 - pos)[:, None] * log_g[None, :])[None, :, :, None]
    c_dec = jnp.exp(C * log_g)[None, :, None, None]

    def chunks(a):
        return a.reshape(B, n, C, H, a.shape[-1]).swapaxes(0, 1)

    def step(s, blk):
        qb, kb, vb = blk
        scores = jnp.einsum('bihd,bjhd->bhij', qb, kb) * intra
        o = jnp.einsum('bhij,bjhe->bihe', scores, vb) + jnp.einsum('bihd,bhde->bihe', qb, s) * q_dec
        s = s * c_dec + jnp.einsum('bjhd,bjhe->bhde', kb * k_dec, vb)
        return s, o

    _, o = lax.scan(step, s0, (chunks(q), chunks(k), chunks(v)))
    return o.swapaxes(0, 1).reshape(B, L, H, v.shape[-1])

def _bidir_retention(q, k, v, g_f, g_b, log_g, s_f, s_b):
    B, L = q.shape[:2]
    o_f = _retention_chunkwise(q, k, v, log_g[0], s_f)
    o_b = jnp.flip(_retention_chunkwise(jnp.flip(q, 1), jnp.flip(k, 1), jnp.flip(v, 1), log_g[1], s_b), 1)
    o_f = _head_norm(o_f).reshape(B, L, RET_WIDTH).astype(g_f.dtype)
    o_b = _head_norm(o_b).reshape(B, L, RET_WIDTH).astype(g_b.dtype)
    return o_f * jax.nn.silu(g_f) + o_b * jax.nn.silu(g_b)

def _moe(h, router_w, router_bias, w_gate, w_up, w_down):
    T, D = h.shape
    s = jax.nn.sigmoid((h @ router_w).astype(jnp.float32))
    s_sel = (s + router_bias.astype(jnp.float32)).reshape(T, N_GROUPS, EXPERTS_PER_GROUP)
    grp = jnp.argmax(jnp.sum(lax.top_k(s_sel, 2)[0], axis=-1), axis=-1)
    in_grp = jnp.take_along_axis(s_sel, grp[:, None, None], axis=1)[:, 0]
    _, loc = lax.top_k(in_grp, TOP_K)
    eid = grp[:, None] * EXPERTS_PER_GROUP + loc
    gate = jnp.take_along_axis(s, eid, axis=1)
    gate = gate / jnp.sum(gate, axis=-1, keepdims=True)
    A = T * TOP_K
    e_flat = eid.reshape(A)
    tok_flat = jnp.repeat(jnp.arange(T, dtype=jnp.int32), TOP_K)
    order = jnp.argsort(e_flat)
    e_s, tok_s, w_s = e_flat[order], tok_flat[order], gate.reshape(A)[order]
    counts = jax.ops.segment_sum(jnp.ones((A,), jnp.int32), e_flat, num_segments=N_EXPERTS)
    start = jnp.cumsum(counts) - counts
    pcounts = (counts + MOE_BLOCK - 1) // MOE_BLOCK * MOE_BLOCK
    pend = jnp.cumsum(pcounts)
    pstart = pend - pcounts
    pos = pstart[e_s] + (jnp.arange(A, dtype=jnp.int32) - start[e_s])
    nb = (A + MOE_BLOCK - 1) // MOE_BLOCK + N_EXPERTS
    P = nb * MOE_BLOCK
    buf_tok = jnp.full((P,), T, jnp.int32).at[pos].set(tok_s)
    buf_w = jnp.zeros((P,), jnp.float32).at[pos].set(w_s)
    blk_start = jnp.arange(nb, dtype=jnp.int32) * MOE_BLOCK
    blk_exp = jnp.minimum(jnp.sum(blk_start[:, None] >= pend[None, :], axis=1), N_EXPERTS - 1)
    h_pad = jnp.concatenate([h, jnp.zeros((1, D), h.dtype)], axis=0)

    def run(args):
        tok_b, e_b = args
        xb = h_pad[tok_b]
        return (jax.nn.silu(xb @ w_gate[e_b]) * (xb @ w_up[e_b])) @ w_down[e_b]

    y = lax.map(run, (buf_tok.reshape(nb, MOE_BLOCK), blk_exp)).reshape(P, D)
    out = jnp.zeros((T + 1, D), h.dtype).at[buf_tok].add(y * buf_w[:, None].astype(y.dtype))
    return out[:T]

def _layer(x, ctx, c, c_ctx, ada_w, ada_b, norm_mix_w, norm_ffn_w, w_in, na_q_norm, na_k_norm,
           na_rpb, ret_decay, w_out, router_w, router_bias, w_gate, w_up, w_down, last):
    B, L, D = x.shape
    Lc = ctx.shape[1]
    mod = jax.nn.silu(c) @ ada_w + ada_b
    mod_c = jax.nn.silu(c_ctx) @ ada_w + ada_b
    sh_a, sc_a, g_a, sh_f, sc_f, g_f = jnp.split(mod[:, None, :], 6, axis=-1)
    sh_ac, sc_ac, g_ac, sh_fc, sc_fc, g_fc = jnp.split(mod_c, 6)
    splits = list(np.cumsum([NA_WIDTH] * 3 + [RET_WIDTH] * 4))

    def project(h):
        Bx, Lx = h.shape[:2]
        qa, ka, va, qb, kb, vb, gfw, gbw = jnp.split(h @ w_in, splits, axis=-1)
        na = [a.reshape(Bx, Lx, NA_HEADS, NA_HEAD_DIM) for a in (qa, ka, va)]
        rt = [a.reshape(Bx, Lx, RET_HEADS, RET_HEAD_DIM) for a in (qb, kb, vb)]
        na[0] = _rmsnorm(na[0], na_q_norm)
        na[1] = _rmsnorm(na[1], na_k_norm)
        return na, rt, gfw, gbw

    h = _modulate(x, norm_mix_w, sh_a, sc_a)
    hc = _modulate(ctx, norm_mix_w, sh_ac, sc_ac)
    (qa, ka, va), (qb, kb, vb), gfw, gbw = project(h)
    (qac, kac, vac), (qbc, kbc, vbc), gfc, gbc = project(hc)
    ret_scale = RET_HEAD_DIM ** -0.5
    qb = _axial_rope(qb).astype(jnp.float32)
    kb = _axial_rope(kb).astype(jnp.float32) * ret_scale
    vb = vb.astype(jnp.float32)
    qbc = qbc.astype(jnp.float32)
    kbc = kbc.astype(jnp.float32) * ret_scale
    vbc = vbc.astype(jnp.float32)
    log_g = -jnp.exp(ret_decay.astype(jnp.float32))
    s_f = _retention_final_state(kbc, vbc, log_g[0])
    s_b = _retention_final_state(jnp.flip(kbc, 1), jnp.flip(vbc, 1), log_g[1])

    na_lat = _neighborhood_attention(qa, ka, va, kac, vac, na_rpb).reshape(B, L, NA_WIDTH)
    ret_lat = _bidir_retention(qb, kb, vb, gfw, gbw, log_g, s_f, s_b)
    x = x + g_a * (jnp.concatenate([na_lat, ret_lat], axis=-1) @ w_out)
    if not last:
        zero = jnp.zeros_like(s_f)
        na_ctx = _ctx_attention(qac, kac, vac).reshape(B, Lc, NA_WIDTH)
        ret_ctx = _bidir_retention(qbc, kbc, vbc, gfc, gbc, log_g, zero, zero)
        ctx = ctx + g_ac * (jnp.concatenate([na_ctx, ret_ctx], axis=-1) @ w_out)

    tokens = _modulate(x, norm_ffn_w, sh_f, sc_f).reshape(B * L, D)
    if not last:
        tokens_c = _modulate(ctx, norm_ffn_w, sh_fc, sc_fc).reshape(B * Lc, D)
        tokens = jnp.concatenate([tokens, tokens_c], axis=0)
    y = _moe(tokens, router_w, router_bias, w_gate, w_up, w_down)
    x = x + g_f * y[:B * L].reshape(B, L, D)
    if not last:
        ctx = ctx + g_fc * y[B * L:].reshape(B, Lc, D)
    return x, ctx

def setup_inputs(seed: int = 0) -> dict:
    key = jax.random.key(seed)
    ks = jax.random.split(key, 20)
    f32 = jnp.float32
    nrm = lambda k, shape, s: jax.random.normal(k, shape, f32) * s
    base_decay = np.log(-np.log(1.0 - 2.0 ** (-5.0 - np.arange(RET_HEADS)))).astype(np.float32)
    return {
        'x': nrm(ks[0], (BATCH, SEQ, D_MODEL), 1.0),
        'c': nrm(ks[1], (BATCH, D_MODEL), 1.0),
        'ctx': nrm(ks[2], (BATCH, CTX_LEN, D_MODEL), 1.0),
        'c_ctx': nrm(ks[3], (D_MODEL,), 1.0),
        'ada_w': nrm(ks[4], (DEPTH, D_MODEL, 6 * D_MODEL), 0.5 * D_MODEL ** -0.5),
        'ada_b': nrm(ks[5], (DEPTH, 6 * D_MODEL), 0.02),
        'norm_mix_w': 1.0 + nrm(ks[6], (DEPTH, D_MODEL), 0.02),
        'norm_ffn_w': 1.0 + nrm(ks[7], (DEPTH, D_MODEL), 0.02),
        'w_in': nrm(ks[8], (DEPTH, D_MODEL, IN_COLS), D_MODEL ** -0.5),
        'na_q_norm': 1.0 + nrm(ks[9], (DEPTH, NA_HEAD_DIM), 0.02),
        'na_k_norm': 1.0 + nrm(ks[10], (DEPTH, NA_HEAD_DIM), 0.02),
        'na_rpb': nrm(ks[11], (DEPTH, NA_HEADS, 2 * NA_WIN_H - 1, 2 * NA_WIN_W - 1), 0.02),
        'ret_decay': jnp.asarray(base_decay)[None, None, :] + nrm(ks[12], (DEPTH, 2, RET_HEADS), 0.05),
        'w_out': nrm(ks[13], (DEPTH, MIX_WIDTH, D_MODEL), MIX_WIDTH ** -0.5),
        'router_w': nrm(ks[14], (D_MODEL, N_EXPERTS), D_MODEL ** -0.5),
        'router_bias': nrm(ks[15], (N_EXPERTS,), 0.01),
        'exp_w_gate': nrm(ks[16], (DEPTH, N_EXPERTS, D_MODEL, D_FF_EXPERT), D_MODEL ** -0.5),
        'exp_w_up': nrm(ks[17], (DEPTH, N_EXPERTS, D_MODEL, D_FF_EXPERT), D_MODEL ** -0.5),
        'exp_w_down': nrm(ks[18], (DEPTH, N_EXPERTS, D_FF_EXPERT, D_MODEL), D_FF_EXPERT ** -0.5),
    }

def reference(x, c, ctx, c_ctx, ada_w, ada_b, norm_mix_w, norm_ffn_w, w_in, na_q_norm, na_k_norm,
              na_rpb, ret_decay, w_out, router_w, router_bias, exp_w_gate, exp_w_up, exp_w_down):
    for l in range(DEPTH):
        x, ctx = _layer(x, ctx, c, c_ctx, ada_w[l], ada_b[l], norm_mix_w[l], norm_ffn_w[l], w_in[l],
                        na_q_norm[l], na_k_norm[l], na_rpb[l], ret_decay[l], w_out[l],
                        router_w, router_bias, exp_w_gate[l], exp_w_up[l], exp_w_down[l],
                        l == DEPTH - 1)
    return x


_drawn_inputs = setup_inputs


def setup_inputs(seed=0):
    import zlib

    import numpy as np

    out = dict(_drawn_inputs(seed))
    spreads = {}
    factors = {'na_q_norm': 8.0, 'na_k_norm': 8.0, 'na_rpb': 21.483}
    for name, (base, spread) in spreads.items():
        noise = np.random.default_rng([zlib.crc32(name.encode()), seed]).standard_normal(out[name].shape)
        drawn = base * np.exp(spread * noise) if base else spread * noise
        out[name] = __import__('jax').numpy.asarray(drawn.astype(out[name].dtype))
    for name, factor in factors.items():
        out[name] = (out[name] * factor).astype(out[name].dtype)
    return out
```

```python
from contextlib import ExitStack
import math

import numpy as np

import concourse.bass as bass
from concourse import mybir

F32 = mybir.dt.float32
I32 = mybir.dt.int32
ACT = mybir.ActivationFunctionType
ALU = mybir.AluOpType
AX = mybir.AxisListType

P = 128
DEPTH, D, SEQ, CTX = 2, 1024, 512, 256
ROWS, COLS = 8, 64
KD = D // P
LAT = SEQ // P
NT = (SEQ + CTX) // P
TOK = SEQ + CTX
NAH, NAD = 8, 64
RH, RD = 4, 128
CH = 512
WIN_W, KBLK, QBLK = 16, 32, 16
KSPAN = KBLK * ROWS
NE, NG, EPG = 32, 8, 4
FF = 512
NOV = 2 * TOK // P + 2
NBLK = NE + NOV
BIG = 1.0e30
EPS = 1e-6
RET_EPS = 1e-5

K = 256
W_SLOTS = [0, 16 * K]
QA, KA, VA = 32 * K, 44 * K, 56 * K
QB, KB, VB, GF, GB = 74 * K, 86 * K, 98 * K, 110 * K, 122 * K
ARENA = 134 * K
SMALL = 432

KSTART = [0, 8, 24, 32]
BIAS_TYPE = [0, 1, 1, 2]
BIAS_START = [0, -8, -16]
V_TILES = [[0, 1], [6, 7], [7, 8], [2, 3]]
V_PAD = 16


def counted(units, pred):
    n, out = 0, []
    for u in units:
        n += bool(pred(u))
        out.append(n)
    return out


def build(nc, A):
    stack = ExitStack()
    with stack:
        def sb(name, shape, dt=F32):
            return stack.enter_context(nc.sbuf_tensor(name, shape, dt))

        def sem(name):
            return stack.enter_context(nc.semaphore(name))

        def dram(name, shape, dt=F32):
            return nc.dram_tensor(name, shape, dt).ap()

        X = sb("X", [P, NT, D])
        hT = sb("hT", [P, KD, TOK])
        arena = sb("arena", [P, ARENA])
        bc = [sb(f"bc{i}", [P, D]) for i in range(4)]
        ident = sb("ident", [P, P])
        upper = sb("upper", [P, P])
        ones = sb("ones", [P, P])
        tabs = sb("tabs", [P, 768])
        sc32 = sb("sc32", [P, KD, 32])
        rw = sb("rw", [P, KD, NE])
        small = sb("small", [P, SMALL])
        ints = sb("ints", [P, 152], I32)
        idx_slot = [sb(f"idx_slot{s}", [P, 1], I32) for s in range(2)]
        nag = sb("nag", [P, 4, NAD])
        PS = [stack.enter_context(nc.psum_tensor(f"PS{i}", [P, 512], F32)) for i in range(8)]

        used = [0]

        def cut(n):
            used[0] += n
            return small[:, used[0] - n:used[0]]

        neghalf = cut(32)
        ss = cut(8)
        msq = cut(8)
        rstd = cut(8)
        lnscale = cut(1)
        decay = cut(DEPTH * 2 * RH)
        cc = cut(2 * KD)
        cth = cut(2 * KD)
        qk_ss = cut(2 * NAH)
        qk_ms = cut(2 * NAH)
        qk_rs = cut(2 * NAH)
        negmax = cut(4)
        rsum = cut(NT * NAH)
        rinv = cut(NT * NAH)
        bnst = cut(8 * 6)
        mv = cut(8 * 2)
        hvar = cut(8)
        hrstd = cut(8)
        wgt = cut(2 * NT)
        rbias = cut(NE)
        rev8 = cut(NG)
        rev32 = cut(NE)
        ovidx = cut(NOV)
        assert used[0] <= SMALL

        def area(off, shape):
            n = int(np.prod(shape))
            names = "abc"[:len(shape)]
            v = arena[:, off:off + n]
            if len(shape) > 1:
                pat = f"p ({' '.join(names)}) -> p {' '.join(names)}"
                v = v.rearrange(pat, **{names[i]: shape[i] for i in range(len(shape))})
            return v

        ada_w = [area(W_SLOTS[s], (2, 2048)) for s in range(2)]
        win = [area(W_SLOTS[s], (KD, CH)) for s in range(2)]
        qaT, kaT = area(QA, (4, TOK)), area(KA, (4, TOK))
        va = area(VA, (9, CH))
        qbT, kbT = area(QB, (RH, TOK)), area(KB, (RH, TOK))
        vb, gf, gb = area(VB, (NT, CH)), area(GF, (NT, CH)), area(GB, (NT, CH))
        hTf = hT[:, :, :].rearrange("p a b -> p (a b)")
        modsb = hTf[:, 0:1536].rearrange("p (a b) -> p a b", a=3)
        adab = hTf[:, 1536:3072].rearrange("p (a b) -> p a b", a=3)
        normw = area(QB, (D,))
        hrow1 = [area(QB + (1 + i) * D, (D,)) for i in range(2)]
        junk = [area(QB + (3 + i) * D, (D,)) for i in range(2)]
        rowbuf = [bc[2][:, 0:512], bc[2][:, 512:1024]]
        sqbuf = [bc[3][:, 0:512], bc[3][:, 512:1024]]
        cosF = tabs[:, 0:512].rearrange("p (a b) -> p a b", a=4)
        sinF = tabs[:, 512:768].rearrange("p (a b) -> p a b", a=4)
        mask = tabs[:, 0:768].rearrange("p (a b) -> p a b", a=3)
        bias = area(0, (NAH, 3, KSPAN))
        pexp = [area(24 * K + i * 512, (512,)) for i in range(2)]
        pT = [area(28 * K + i * 512, (4, P)) for i in range(2)]
        mix = hTf[:, :].rearrange("p (a b) -> p a b", a=NT)
        delta = area(0, (2, NT, SEQ))
        dec = [area(24 * K + i * 512, (512,)) for i in range(4)]
        Wd = [area(32 * K, (NT, SEQ)), area(44 * K, (NT, SEQ))]
        wo0 = area(56 * K, (KD, CH))
        dctx = bc[3][:, 0:1024].rearrange("p (a b c) -> p a b c", a=2, b=2)
        ofb = [bc[2][:, 0:512], bc[2][:, 512:1024]]
        mixT = area(QB, (KD, TOK))
        wo1 = area(0, (KD, CH))
        otmp = [bc[2][:, 0:512], bc[2][:, 512:1024]]
        wg = [area(s * 48 * K, (KD, FF)) for s in range(2)]
        wu = [area(s * 48 * K + 16 * K, (KD, FF)) for s in range(2)]
        wd = [area(s * 48 * K + 32 * K, (4, D)) for s in range(2)]
        hrow2 = [area(98 * K + t * D, (D,)) for t in range(NT)]
        normw2 = area(122 * K, (D,))
        junk2 = [area(126 * K, (D,)), area(130 * K, (D,))]
        xg = [area(98 * K + s * D, (D,)) for s in range(2)]
        xgT = [area(106 * K + s * D, (KD, P)) for s in range(2)]
        th = [area(114 * K + s * 512, (512,)) for s in range(2)]
        act = [area(118 * K + s * 512, (512,)) for s in range(2)]
        aT = [area(122 * K + s * 512, (4, P)) for s in range(2)]
        yb = [area(126 * K + s * D, (D,)) for s in range(2)]
        y1 = [area(i * D, (D,)) for i in range(2)]
        y2 = [area((2 + i) * D, (D,)) for i in range(2)]
        z1 = [area((4 + i) * D, (D,)) for i in range(2)]
        z2 = [area((6 + i) * D, (D,)) for i in range(2)]
        r_at = [0]

        def rt(shape):
            n = int(np.prod(shape))
            i, o = divmod(r_at[0], D)
            if o + n > D:
                i, o = i + 1, 0
            r_at[0] = i * D + o + n
            v = bc[i][:, o:o + n]
            if len(shape) > 1:
                names = "abc"[:len(shape)]
                v = v.rearrange(f"p ({' '.join(names)}) -> p {' '.join(names)}",
                                **{names[k]: shape[k] for k in range(len(shape))})
            return v

        route_t = {n: rt(shape) for n, shape in dict(
            score=(NT, NE), ssel=(NT, NE), pairs=(NT * NG, 6), gsum=(NT, NG), gmax=(NT,), gcand=(NT, NG),
            gfirst=(NT,), ing=(NT, NG), pen=(NT, NG), ms=(NT, NE), top=(NT,), cand=(NT, NE),
            first0=(NT,), first1=(NT,), oh0=(NT, NE), oh1=(NT, NE), M=(NT, NE), tmp=(NT, NE),
            s0=(NT,), s1=(NT,), rank=(NT,), q=(NT,), r=(NT,), pos=(NT,), ov=(NT,), e=(NT,), blk=(NT,),
            extra=(NE,), zero=(NE,), ovinc=(NE,), ovb=(NE,), ovcmp=(NOV, NE), ovexp=(NOV,), npair=(1,)).items()}

        mod_d = [dram(f"mod_d{l}", (2, 6 * D)) for l in range(DEPTH)]
        h_d = dram("h_d", (TOK, D))
        y_d = dram("y_d", (NBLK * P, D))
        tok_d = [dram(f"tok_d{l}", (P * NBLK, 1), I32) for l in range(DEPTH)]

        const_in = sem("const_in")
        x_in = sem("x_in")
        tok_zero = sem("tok_zero")
        y_zero = sem("y_zero")
        pool_passed = sem("pool_passed")
        out_done = sem("out_done")
        sc_tanh = sem("sc_tanh")
        sc_ready = sem("sc_ready")
        decay_exp = sem("decay_exp")
        dve_step = sem("dve_step")
        act_step = sem("act_step")
        pool_step = sem("pool_step")
        pe_step = sem("pe_step")
        N_CONST = 13

        NAMES = """ada_in0 ada_in1 ada_done adab_zero adab_in mod_rows mod_out
        modb_in ss_done ms_ready rstd_ready hrow_ready tr_done hT_ready
        win0 win1 proj_done act_rel gate_rel qk_ms_ready qk_rs_ready row_ready trow_done trow_evac
        vshift tab_in mask_in bias_in s_done nm_ready p_ready pt_done pt_evac pv_done o_norm
        delta_in lg_ready st_done dec_ready w_mult pvr_done hvar_ready hrstd_ready ret_norm
        wo_in0 wo_in1 gate_in mt_done mt_evac op_done x_upd
        g_in g_ss g_ms g_rs g_row g_tr g_hT h_out logit_done exp_done m_ready rank_done route_ready
        tok_out idx_in
        wg_in0 wg_in1 wu_in0 wu_in1 wd_in0 wd_in1 g_done0 g_done1 u_done0 u_done1 d_done0 d_done1
        idx_cp0 idx_cp1 xg_in0 xg_in1 xg_used0 xg_used1 t_done t_evac
        th_ready gate_step a_ready at_done aT_ready y_done yb_ready y_out0 y_out1
        gb_in yg0 yg1 comb_done""".split()
        POOL_DMA = ("tok_out", "xg_in0", "xg_in1", "yg0", "yg1")
        SEMS = {(None, n): sem(n) for n in NAMES if n not in POOL_DMA}
        SEMS.update({(l, n): sem(f"{n}_{l}") for l in range(DEPTH) for n in POOL_DMA})
        met = sem("met")
        cleared = sem("cleared")

        def S(l, name):
            return SEMS[l if name in POOL_DMA else None, name]

        steps = {"dve": 0, "act": 0, "pool": 0, "pe": 0}
        meetings = {}

        def chain(eng, which, s):
            def link(ins):
                ins.then_inc(s, 1)
                steps[which] += 1
                eng.wait_ge(s, steps[which])
            return link

        def meet(eng, who):
            meetings[who] = meetings.get(who, 0) + 1
            eng.drain().then_inc(met, 1)
            eng.wait_ge(met, 5 * meetings[who])

        def tiles(l):
            return NT if l < DEPTH - 1 else LAT

        KIND = ["norm", "norm", "v", "rope", "rope", "v", "gate", "gate"]

        def proj_units(l):
            full = [1, 2, 4, 5]
            return [(c, t) for c in range(8) for t in range(NT if l < DEPTH - 1 or c in full else LAT)]

        def needs_row(u):
            return KIND[u[0]] in ("norm", "rope")

        def act_reads(u):
            return KIND[u[0]] in ("norm", "v", "gate")

        def dve_reads(u):
            return KIND[u[0]] == "gate"

        def na_units(l):
            out = []
            for j in range(LAT):
                for h in range(NAH):
                    k0 = KSTART[j] * ROWS
                    out.append((j, h, [(k0, KSPAN), (SEQ, CTX)], V_TILES[j] + [4, 5], BIAS_TYPE[j]))
            if l < DEPTH - 1:
                for t in (4, 5):
                    for h in range(NAH):
                        out.append((t, h, [(SEQ, CTX)], [4, 5], None))
            return out

        def ret_groups(l):
            out = [(r, True, range(0, LAT), range(0, NT)) for r in range(RH)]
            if l < DEPTH - 1:
                out += [(r, False, range(LAT, NT), range(LAT, NT)) for r in range(RH)]
            return out

        block = stack.enter_context(nc.Block())

        @block.sync
        def _(sp):
            def const(dst, src):
                sp.dma_start(dst, src).then_inc(const_in, 16)

            const(cc, A["cc"])
            for t in range(NT):
                src = A["x"][t * P:(t + 1) * P, :] if t < LAT else A["ctx"][(t - LAT) * P:(t - LAT + 1) * P, :]
                sp.dma_start(X[:, t, :], src).then_inc(x_in, 16)
            const(ident[:, :], A["ident"])
            const(upper[:, :], A["upper"])
            const(decay, A["ret_decay"].rearrange("a b c -> (a b c)").partition_broadcast(P))
            const(rw[:, :, :], A["router_w"].rearrange("(k p) n -> p k n", p=P))
            const(rbias, A["router_bias"].partition_broadcast(P))
            const(rev8, A["rev8"].partition_broadcast(P))
            const(rev32, A["rev32"].partition_broadcast(P))
            const(ovidx, A["ovidx"].partition_broadcast(P))
            const(ints[:, 0:NE], A["first_blocks"].partition_broadcast(P))
            const(ints[:, 64:64 + NT], A["token_ids"])
            for n, name in enumerate(("na_q_norm", "na_k_norm")):
                const(nag[:, 2 * n:2 * n + 2, :].rearrange("p a b -> p (a b)"),
                      A[name].rearrange("a b -> (a b)").partition_broadcast(P))

            for l in range(DEPTH):
                for j in range(4):
                    for i in range(2):
                        if j == 0 and i == 0:
                            sp.wait_ge(S(l, "adab_zero"), 1)
                        sp.dma_start(adab[32 * j + i:32 * j + i + 1, :, :],
                                     A["ada_b"][l:l + 1].rearrange("a (r j x) -> j a r x", j=4, x=CH)[j])\
                            .then_inc(S(l, "adab_in"), 16)
                for n in range(12):
                    r, kp = divmod(n, 4)
                    if n >= 2:
                        sp.wait_ge(S(l, "ada_done"), n - 1)
                    sp.dma_start(ada_w[n % 2],
                                 A["ada_w"][l].rearrange("(k p) n -> p k n", p=P)[
                                     :, 2 * kp:2 * kp + 2, 2048 * r:2048 * (r + 1)])\
                        .then_inc(S(l, f"ada_in{n % 2}"), 16)
                sp.wait_ge(S(l, "mod_rows"), 3)
                for j in range(4):
                    for i in range(2):
                        sp.dma_start(mod_d[l][i:i + 1, :].rearrange("a (r j x) -> j a r x", j=4, x=CH)[j],
                                     modsb[32 * j + i:32 * j + i + 1, :, :]).then_inc(S(l, "mod_out"), 16)
                sp.wait_ge(S(l, "mod_out"), 128)

                def mod(i, q):
                    return mod_d[l][i, q * D:(q + 1) * D].partition_broadcast(P)

                if l == 0:
                    sp.wait_ge(y_zero, 16 * NOV)
                for n, (i, q) in enumerate(((0, 1), (0, 0), (1, 1), (1, 0))):
                    sp.dma_start(bc[n][:, :], mod(i, q)).then_inc(S(l, "modb_in"), 16)
                sp.dma_start(normw, A["norm_mix_w"][l].partition_broadcast(P)).then_inc(S(l, "modb_in"), 16)
                sp.dma_start(cosF, A["cos_t"]).then_inc(S(l, "tab_in"), 16)
                sp.dma_start(sinF, A["sin_t"]).then_inc(S(l, "tab_in"), 16)

                units = proj_units(l)
                last = [max(i for i, u in enumerate(units) if u[0] == c) + 1 for c in range(8)]
                sp.wait_ge(S(l, "ada_done"), 12)
                for c in range(8):
                    if c >= 2:
                        sp.wait_ge(S(l, "proj_done"), last[c - 2])
                    sp.dma_start(win[c % 2], A["w_in"][l].rearrange("(k p) n -> p k n", p=P)[
                        :, :, c * CH:(c + 1) * CH]).then_inc(S(l, f"win{c % 2}"), 16)
                    if c == 5:
                        n_va = counted(units, act_reads)[last[2] - 1]
                        sp.wait_ge(S(l, "act_rel"), n_va)
                        sp.dma_start(va[0:64, 6:9, :], va[64:128, 0:3, :]).then_inc(S(l, "vshift"), 16)
                        sp.dma_start(va[64:128, 6:9, :], va[0:64, 1:4, :]).then_inc(S(l, "vshift"), 16)
                meet(sp, "sp")

                sp.dma_start(mask, A["na_mask"]).then_inc(S(l, "mask_in"), 16)
                for ty in range(3):
                    for qc in range(QBLK):
                        o = (V_PAD + WIN_W - 1 + BIAS_START[ty] - qc) * ROWS
                        sp.dma_start(bias[qc * ROWS:(qc + 1) * ROWS, :, ty, :],
                                     A["rpb"][l][:, :, o:o + KSPAN]).then_inc(S(l, "bias_in"), 16)
                sp.dma_start(bc[0][:, :], mod(0, 2)).then_inc(S(l, "gate_in"), 16)
                sp.dma_start(bc[1][:, :], mod(1, 2)).then_inc(S(l, "gate_in"), 16)
                meet(sp, "sp")

                sp.dma_start(delta, A["delta"]).then_inc(S(l, "delta_in"), 16)
                sp.dma_start(dctx, A["delta_ctx"]).then_inc(S(l, "delta_in"), 16)
                wo = A["w_out"][l].rearrange("(k p) n -> p k n", p=P)
                sp.dma_start(wo0, wo[:, :, 0:CH]).then_inc(S(l, "wo_in0"), 16)
                meet(sp, "sp")
                sp.dma_start(wo1, wo[:, :, CH:D]).then_inc(S(l, "wo_in1"), 16)
                meet(sp, "sp")

                def expert(s, e):
                    sp.dma_start(wg[s], A["exp_w_gate"][l, e].rearrange("(k p) n -> p k n", p=P))\
                        .then_inc(S(l, f"wg_in{s}"), 16)
                    sp.dma_start(wu[s], A["exp_w_up"][l, e].rearrange("(k p) n -> p k n", p=P))\
                        .then_inc(S(l, f"wu_in{s}"), 16)

                def expert_down(s, e):
                    sp.dma_start(wd[s], A["exp_w_down"][l, e].rearrange("(k p) n -> p k n", p=P))\
                        .then_inc(S(l, f"wd_in{s}"), 16)

                for n, (i, q) in enumerate(((0, 4), (0, 3), (1, 4), (1, 3))):
                    sp.dma_start(bc[n][:, :], mod(i, q)).then_inc(S(l, "g_in"), 16)
                sp.dma_start(normw2, A["norm_ffn_w"][l].partition_broadcast(P)).then_inc(S(l, "g_in"), 16)
                for s in range(2):
                    expert(s, s)
                    expert_down(s, s)
                for t in range(tiles(l)):
                    sp.wait_ge(S(l, "g_row"), t + 1)
                    sp.dma_start(h_d[t * P:(t + 1) * P, :], hrow2[t]).then_inc(S(l, "h_out"), 16)
                sp.wait_ge(S(l, "tok_out"), 32 * tiles(l))
                sp.dma_start(ints[:, 80:80 + NBLK], tok_d[l].rearrange("(p b) a -> p (b a)", p=P))\
                    .then_inc(S(l, "idx_in"), 16)
                sp.wait_ge(S(l, "idx_in"), 16)
                sp.wait_ge(S(l, "h_out"), 16 * tiles(l))
                meet(sp, "sp")

                sp.wait_ge(S(l, "route_ready"), 1)
                n_pairs = sp.value_load(ints[0:1, 79:80], min_val=NE // 2, max_val=NBLK // 2 - 1)
                with sp.Fori(0, n_pairs - 1) as i:
                    for s in range(2):
                        e = sp.value_load(ints[0:1, bass.ds(2 * i + 2 + s, 1)], min_val=0, max_val=NE - 1)
                        sp.wait_ge(S(l, f"g_done{s}"), i + 1)
                        sp.wait_ge(S(l, f"u_done{s}"), i + 1)
                        expert(s, e)
                        sp.wait_ge(S(l, f"d_done{s}"), i + 1)
                        expert_down(s, e)
                meet(sp, "sp")
                sp.dma_start(bc[0][:, :], mod(0, 5)).then_inc(S(l, "gb_in"), 16)
                sp.dma_start(bc[1][:, :], mod(1, 5)).then_inc(S(l, "gb_in"), 16)
                if l == DEPTH - 1:
                    for t in range(LAT):
                        sp.wait_ge(S(l, "comb_done"), t + 1)
                        sp.dma_start(A["out"][t * P:(t + 1) * P, :], X[:, t, :]).then_inc(out_done, 16)
                    sp.wait_ge(out_done, 16 * LAT)
                meet(sp, "sp")
                if l < DEPTH - 1:
                    numbers = [s_.num for (k_, _), s_ in SEMS.items() if k_ is None]
                    sp.sem_clear(range(min(numbers), max(numbers) + 1)).then_inc(cleared, 1)

        @block.gpsimd
        def _(pool):
            link = chain(pool, "pool", pool_step)
            link(pool.memset(ones[:, :], 1.0))
            link(pool.memset(neghalf, -0.5))
            link(pool.memset(lnscale, math.log(RD ** -0.5)))
            link(pool.memset(ints[:, 80:80 + NBLK], 0))
            for l in range(DEPTH):
                pool.dma_start(tok_d[l].rearrange("(p b) a -> p (b a)", p=P), ints[:, 80:80 + NBLK])\
                    .then_inc(tok_zero, 16)
            pool.wait_ge(tok_zero, 32)
            link(pool.memset(bc[0][:, :], 0.0))
            for b in range(NE, NBLK):
                pool.dma_start(y_d[b * P:(b + 1) * P, :], bc[0][:, :]).then_inc(y_zero, 16)
            pool.wait_ge(y_zero, 16 * NOV)

            for l in range(DEPTH):
                pool.wait_ge(S(l, "ms_ready"), 1)
                pool.tensor_tensor(rstd[:, 0:NT], msq[:, 0:NT], neghalf[:, 0:NT], ALU.pow)\
                    .then_inc(S(l, "rstd_ready"), 1)
                n = 0
                for u in proj_units(l):
                    if KIND[u[0]] == "norm":
                        b = n % 2
                        n += 1
                        pool.wait_ge(S(l, "qk_ms_ready"), n)
                        pool.tensor_tensor(qk_rs[:, b * NAH:(b + 1) * NAH], qk_ms[:, b * NAH:(b + 1) * NAH],
                                           neghalf[:, 0:NAH], ALU.pow).then_inc(S(l, "qk_rs_ready"), 1)
                meet(pool, "pool")
                meet(pool, "pool")
                for g in range(len(ret_groups(l))):
                    pool.wait_ge(S(l, "hvar_ready"), g + 1)
                    pool.tensor_tensor(hrstd, hvar, neghalf[:, 0:8], ALU.pow).then_inc(S(l, "hrstd_ready"), 1)
                meet(pool, "pool")
                meet(pool, "pool")
                pool.wait_ge(S(l, "g_ms"), 1)
                pool.tensor_tensor(rstd[:, 0:NT], msq[:, 0:NT], neghalf[:, 0:NT], ALU.pow)\
                    .then_inc(S(l, "g_rs"), 1)
                pool.wait_ge(S(l, "route_ready"), 1)
                for t in range(tiles(l)):
                    for k in range(2):
                        pool.indirect_dma_start(
                            tok_d[l], bass.IndirectOffsetOnAxis(ap=ints[:, 128 + 2 * t + k:129 + 2 * t + k], axis=0),
                            ints[:, 64 + t:65 + t], None).then_inc(S(l, "tok_out"), 16)
                meet(pool, "pool")

                pool.wait_ge(S(l, "idx_in"), 16)

                def gather(s, column, cp_count):
                    pool.tensor_copy(idx_slot[s][:, :], ints[:, column]).then_inc(S(l, f"idx_cp{s}"), 1)
                    pool.wait_ge(S(l, f"idx_cp{s}"), cp_count)
                    pool.sem_inc(pool_passed, 1)
                    pool.indirect_dma_start(xg[s], None, h_d, bass.IndirectOffsetOnAxis(ap=idx_slot[s][:, :], axis=0))\
                        .then_inc(S(l, f"xg_in{s}"), 16)

                n_pairs = pool.value_load(ints[0:1, 79:80], min_val=NE // 2, max_val=NBLK // 2 - 1)
                gather(0, slice(80, 81), 1)
                gather(1, slice(81, 82), 1)
                with pool.Fori(0, n_pairs) as i:
                    for s in range(2):
                        pool.wait_ge(S(l, f"xg_used{s}"), i + 1)
                        gather(s, bass.ds(2 * i + 82 + s, 1), i + 2)
                for s in range(2):
                    pool.wait_ge(S(l, f"y_out{s}"), 16 * n_pairs + 16)
                    pool.wait_ge(S(l, f"xg_in{s}"), 16 * n_pairs + 16)
                pool.sem_inc(pool_passed, 1)
                meet(pool, "pool")
                for t in range(tiles(l)):
                    if t >= 2:
                        pool.wait_ge(S(l, "comb_done"), t - 1)
                    for k, buf in ((0, y1), (1, y2)):
                        pool.indirect_dma_start(
                            buf[t % 2], None, y_d,
                            bass.IndirectOffsetOnAxis(ap=ints[:, 140 + 2 * t + k:141 + 2 * t + k], axis=0))\
                            .then_inc(S(l, f"yg{t % 2}"), 16)
                meet(pool, "pool")
                if l < DEPTH - 1:
                    pool.wait_ge(cleared, 1)
                    pool.drain()

        @block.tensor
        def _(pe):
            pe.wait_ge(const_in, 16 * N_CONST)

            for l in range(DEPTH):
                pe.wait_ge(sc_ready, 1)
                for n in range(12):
                    r, kp = divmod(n, 4)
                    pe.wait_ge(S(l, f"ada_in{n % 2}"), 16 * (n // 2 + 1))
                    for k in range(2):
                        for j in range(4):
                            mm = pe.matmul(PS[r][32 * j:32 * j + 32, :], sc32[:, 2 * kp + k, :],
                                           ada_w[n % 2][:, k, j * CH:(j + 1) * CH],
                                           start=(kp + k == 0), stop=(kp == 3 and k == 1), skip_group_check=True)
                    mm.then_inc(S(l, "ada_done"), 1)

                def rows_to_T(t, row, u0, bank0, ready, done, evac):
                    for half in range(2):
                        u = u0 + half
                        if u >= 4:
                            pe.wait_ge(evac, u - 3)
                        for i in range(4):
                            c = (half * 4 + i) * P
                            mm = pe.transpose(PS[bank0 + u % 4][:, i * P:(i + 1) * P], row[:, c:c + P], ident[:, :])
                        mm.then_inc(done, 1)

                for t in range(NT):
                    pe.wait_ge(S(l, "hrow_ready"), t + 1)
                    rows_to_T(t, hrow1[t % 2], 2 * t, 4, None, S(l, "tr_done"), S(l, "hT_ready"))

                units = proj_units(l)
                n_act, n_dve, n_row = (counted(units, f) for f in (act_reads, dve_reads, needs_row))

                def turn(n):
                    if not needs_row(units[n]):
                        return
                    m = n_row[n] - 1
                    pe.wait_ge(S(l, "row_ready"), m + 1)
                    if m >= 2:
                        pe.wait_ge(S(l, "trow_evac"), m - 1)
                    for i in range(4):
                        mm = pe.transpose(PS[4 + m % 2][:, i * P:(i + 1) * P], rowbuf[m % 2][:, i * P:(i + 1) * P],
                                          ident[:, :])
                    mm.then_inc(S(l, "trow_done"), 1)

                pe.wait_ge(S(l, "hT_ready"), 2 * NT)
                seen = -1
                for n, (c, t) in enumerate(units):
                    if c != seen:
                        pe.wait_ge(S(l, f"win{c % 2}"), 16 * (c // 2 + 1))
                        seen = c
                    if n >= 4:
                        if n_act[n - 4]:
                            pe.wait_ge(S(l, "act_rel"), n_act[n - 4])
                        if n_dve[n - 4]:
                            pe.wait_ge(S(l, "gate_rel"), n_dve[n - 4])
                    for k in range(KD):
                        mm = pe.matmul(PS[n % 4][:, :], hT[:, k, t * P:(t + 1) * P], win[c % 2][:, k, :],
                                       start=(k == 0), stop=(k == KD - 1))
                    mm.then_inc(S(l, "proj_done"), 1)
                    if n >= 2:
                        turn(n - 2)
                turn(len(units) - 2)
                turn(len(units) - 1)
                meet(pe, "pe")

                nu = na_units(l)
                pe.wait_ge(S(l, "vshift"), 32)

                def scores(n):
                    j, h, ranges, _, _ = nu[n]
                    hp = slice((h % 2) * 64, (h % 2) * 64 + 64)
                    if n >= 3:
                        pe.wait_ge(S(l, "p_ready"), n - 2)
                    o = 0
                    for k0, kn in ranges:
                        mm = pe.matmul(PS[n % 3][:, o:o + kn], qaT[hp, h // 2, j * P:(j + 1) * P],
                                       kaT[hp, h // 2, k0:k0 + kn], start=True, stop=True)
                        o += kn
                    mm.then_inc(S(l, "s_done"), 1)

                def turn_p(n):
                    tiles_ = nu[n][3]
                    pe.wait_ge(S(l, "p_ready"), n + 1)
                    if n >= 2:
                        pe.wait_ge(S(l, "pt_evac"), n - 1)
                    for i in range(len(tiles_)):
                        mm = pe.transpose(PS[3 + n % 2][:, i * P:(i + 1) * P], pexp[n % 2][:, i * P:(i + 1) * P],
                                          ident[:, :])
                    mm.then_inc(S(l, "pt_done"), 1)

                def values(n):
                    j, h, _, tiles_, _ = nu[n]
                    pe.wait_ge(S(l, "pt_evac"), n + 1)
                    if h == 0 and j >= 2:
                        pe.wait_ge(S(l, "o_norm"), j - 1)
                    for i, vt in enumerate(tiles_):
                        mm = pe.matmul(PS[5 + j % 2][:, h * NAD:(h + 1) * NAD], pT[n % 2][:, i, :],
                                       va[:, vt, h * NAD:(h + 1) * NAD], start=(i == 0), stop=(i == len(tiles_) - 1))
                    mm.then_inc(S(l, "pv_done"), 1)

                for n in range(len(nu) + 2):
                    if n < len(nu):
                        scores(n)
                    if 1 <= n <= len(nu):
                        turn_p(n - 1)
                    if n >= 2:
                        values(n - 2)
                meet(pe, "pe")

                m = 0
                for g, (r, lat, qts, kts) in enumerate(ret_groups(l)):
                    w = len(qts) * P
                    for a, kt in enumerate(kts):
                        if m >= 2:
                            pe.wait_ge(S(l, "w_mult"), 2 * (m - 1))
                        pe.matmul(PS[m % 2][:, 0:w], kbT[:, r, kt * P:(kt + 1) * P],
                                  qbT[:, r, qts[0] * P:qts[0] * P + w], start=True, stop=True)\
                            .then_inc(S(l, "st_done"), 1)
                        m += 1
                    pe.wait_ge(S(l, "w_mult"), 2 * m)
                    if g >= 2:
                        pe.wait_ge(S(l, "ret_norm"), g - 1)
                    for d in range(2):
                        for i in range(len(qts)):
                            for a, kt in enumerate(kts):
                                mm = pe.matmul(PS[2 + 2 * d + g % 2][:, i * P:(i + 1) * P],
                                               Wd[d][:, a, i * P:(i + 1) * P], vb[:, kt, r * RD:(r + 1) * RD],
                                               start=(a == 0), stop=(a == len(kts) - 1))
                        mm.then_inc(S(l, "pvr_done"), 1)
                meet(pe, "pe")

                nt = tiles(l)
                for t in range(nt):
                    rows_to_T(t, mix[:, t, :], 2 * t, 4, None, S(l, "mt_done"), S(l, "mt_evac"))
                pe.wait_ge(S(l, "mt_evac"), 2 * nt)
                for c, w in enumerate((wo0, wo1)):
                    pe.wait_ge(S(l, f"wo_in{c}"), 16)
                    for t in range(nt):
                        n = c * nt + t
                        if n >= 4:
                            pe.wait_ge(S(l, "x_upd"), n - 3)
                        for k in range(KD):
                            mm = pe.matmul(PS[n % 4][:, :], mixT[:, k, t * P:(t + 1) * P], w[:, k, :],
                                           start=(k == 0), stop=(k == KD - 1))
                        mm.then_inc(S(l, "op_done"), 1)
                meet(pe, "pe")

                for t in range(nt):
                    pe.wait_ge(S(l, "g_row"), t + 1)
                    rows_to_T(t, hrow2[t], 2 * t, 4, None, S(l, "g_tr"), S(l, "g_hT"))
                pe.wait_ge(S(l, "g_hT"), 2 * nt)
                for t in range(nt):
                    for k in range(KD):
                        mm = pe.matmul(PS[0][:, t * NE:(t + 1) * NE], hT[:, k, t * P:(t + 1) * P], rw[:, k, :],
                                       start=(k == 0), stop=(k == KD - 1))
                mm.then_inc(S(l, "logit_done"), 1)
                pe.wait_ge(S(l, "m_ready"), 1)
                for t in range(nt + 1):
                    for t2 in range(min(t, nt - 1) + 1):
                        w = upper if t2 == t else ones
                        mm = pe.matmul(PS[1][:, t * NE:(t + 1) * NE], w[:, :], route_t["M"][:, t2, :],
                                       start=(t2 == 0), stop=(t2 == min(t, nt - 1)))
                mm.then_inc(S(l, "rank_done"), 1)
                meet(pe, "pe")

                pe.wait_ge(S(l, "route_ready"), 1)

                def turn_x(s, half):
                    for i in range(4):
                        c = (half * 4 + i) * P
                        mm = pe.transpose(PS[half][:, i * P:(i + 1) * P], xg[s][:, c:c + P], ident[:, :])
                    return mm

                pe.wait_ge(S(l, "xg_in0"), 16)
                for half in range(2):
                    mm = turn_x(0, half)
                    mm.then_inc(S(l, "t_done"), 1) if half == 0 else mm.then_inc(S(l, "xg_used0"), 1)
                n_pairs = pe.value_load(ints[0:1, 79:80], min_val=NE // 2, max_val=NBLK // 2 - 1)
                with pe.Fori(0, n_pairs) as i:
                    for s in range(2):
                        o = 1 - s
                        pe.wait_ge(S(l, "t_evac"), 4 * i + 2 * s + 2)
                        pe.wait_ge(S(l, f"wg_in{s}"), 16 * i + 16)
                        for k in range(KD):
                            mm = pe.matmul(PS[2][:, :], xgT[s][:, k, :], wg[s][:, k, :], start=(k == 0), stop=(k == KD - 1))
                        mm.then_inc(S(l, f"g_done{s}"), 1)
                        pe.wait_ge(S(l, f"wu_in{s}"), 16 * i + 16)
                        for k in range(KD):
                            mm = pe.matmul(PS[3][:, :], xgT[s][:, k, :], wu[s][:, k, :], start=(k == 0), stop=(k == KD - 1))
                        mm.then_inc(S(l, f"u_done{s}"), 1)
                        pe.wait_ge(S(l, f"xg_in{o}"), 16 * i + 16 + 16 * s)
                        turn_x(o, 0).then_inc(S(l, "t_done"), 1)
                        pe.wait_ge(S(l, "a_ready"), 2 * i + s + 1)
                        for f in range(4):
                            mm = pe.transpose(PS[4][:, f * P:(f + 1) * P], act[s][:, f * P:(f + 1) * P], ident[:, :])
                        mm.then_inc(S(l, "at_done"), 1)
                        turn_x(o, 1).then_inc(S(l, f"xg_used{o}"), 1)
                        pe.wait_ge(S(l, "aT_ready"), 2 * i + s + 1)
                        pe.wait_ge(S(l, f"wd_in{s}"), 16 * i + 16)
                        for c in range(2):
                            for f in range(4):
                                mm = pe.matmul(PS[5 + c][:, :], aT[s][:, f, :], wd[s][:, f, c * CH:(c + 1) * CH],
                                               start=(f == 0), stop=(f == 3))
                            if c == 0:
                                mm.then_inc(S(l, "y_done"), 1)
                        mm.then_inc(S(l, f"d_done{s}"), 1)
                meet(pe, "pe")
                meet(pe, "pe")
                if l < DEPTH - 1:
                    pe.wait_ge(cleared, 1)
                    pe.drain()

        @block.scalar
        def _(act_e):
            link = chain(act_e, "act", act_step)
            act_e.wait_ge(const_in, 16 * N_CONST)
            act_e.activation(cth, cc, ACT.Tanh, scale=0.5).then_inc(sc_tanh, 1)
            act_e.activation(decay, decay, ACT.Exp).then_inc(decay_exp, 1)
            act_e.wait_ge(x_in, 16 * NT)
            for l in range(DEPTH):
                act_e.wait_ge(S(l, "modb_in"), 80)
                for t in range(NT):
                    if t >= 2:
                        act_e.wait_ge(S(l, "ss_done"), t - 1)
                    act_e.activation(junk[t % 2], X[:, t, :], ACT.Square, accum_out=ss[:, t:t + 1])\
                        .then_inc(S(l, "ss_done"), 1)
                for u in range(2 * NT):
                    t, half = divmod(u, 2)
                    act_e.wait_ge(S(l, "tr_done"), u + 1)
                    act_e.activation(hT[:, 4 * half:4 * half + 4, t * P:(t + 1) * P],
                                     PS[4 + u % 4][:, :].rearrange("p (a b) -> p a b", a=4), ACT.Copy)\
                        .then_inc(S(l, "hT_ready"), 1)

                units = proj_units(l)
                n_row = counted(units, needs_row)
                n_norm = counted(units, lambda u: KIND[u[0]] == "norm")

                def evac_row(n):
                    if n < 0 or not needs_row(units[n]):
                        return
                    c, t = units[n]
                    m = n_row[n] - 1
                    dst = {0: qaT, 1: kaT, 3: qbT, 4: kbT}[c]
                    act_e.wait_ge(S(l, "trow_done"), m + 1)
                    act_e.activation(dst[:, :, t * P:(t + 1) * P],
                                     PS[4 + m % 2][:, :].rearrange("p (a b) -> p a b", a=4), ACT.Copy)\
                        .then_inc(S(l, "trow_evac"), 1)

                for n in range(len(units) + 2):
                    if n < len(units):
                        c, t = units[n]
                        kind = KIND[c]
                        if act_reads(units[n]):
                            act_e.wait_ge(S(l, "proj_done"), n + 1)
                        if kind == "norm":
                            m = n_norm[n] - 1
                            if m >= 2:
                                act_e.wait_ge(S(l, "qk_ms_ready"), m - 1)
                            act_e.activation(sqbuf[m % 2], PS[n % 4][:, :], ACT.Square).then_inc(S(l, "act_rel"), 1)
                        elif kind == "v":
                            act_e.activation({2: va, 5: vb}[c][:, t, :], PS[n % 4][:, :], ACT.Copy)\
                                .then_inc(S(l, "act_rel"), 1)
                        elif kind == "gate":
                            act_e.activation({6: gf, 7: gb}[c][:, t, :], PS[n % 4][:, :], ACT.Tanh, scale=0.5)\
                                .then_inc(S(l, "act_rel"), 1)
                    evac_row(n - 2)
                meet(act_e, "act_e")

                nu = na_units(l)

                def evac_p(n):
                    w = len(nu[n][3])
                    act_e.wait_ge(S(l, "pt_done"), n + 1)
                    if n >= 2:
                        act_e.wait_ge(S(l, "pv_done"), n - 1)
                    act_e.activation(pT[n % 2][:, 0:w, :],
                                     PS[3 + n % 2][:, 0:w * P].rearrange("p (a b) -> p a b", a=w), ACT.Copy)\
                        .then_inc(S(l, "pt_evac"), 1)

                for n in range(len(nu) + 1):
                    if n < len(nu):
                        j, h, ranges, _, _ = nu[n]
                        w = sum(k for _, k in ranges)
                        act_e.wait_ge(S(l, "nm_ready"), n + 1)
                        if n >= 2:
                            act_e.wait_ge(S(l, "pt_done"), n - 1)
                        act_e.activation(pexp[n % 2][:, 0:w], PS[n % 3][:, 0:w], ACT.Exp,
                                         bias=negmax[:, n % 4:n % 4 + 1],
                                         accum_out=rsum[:, j * NAH + h:j * NAH + h + 1])\
                            .then_inc(S(l, "p_ready"), 1)
                    if n >= 1:
                        evac_p(n - 1)
                meet(act_e, "act_e")

                act_e.wait_ge(S(l, "delta_in"), 32)
                act_e.wait_ge(S(l, "lg_ready"), 1)
                m = 0
                for r, lat, qts, kts in ret_groups(l):
                    w = len(qts) * P
                    for a in range(len(kts)):
                        for d in range(2):
                            if m >= 4:
                                act_e.wait_ge(S(l, "w_mult"), m - 3)
                            src = delta[:, d, a, :] if lat else dctx[:, d, a, :]
                            lg = decay[:, (l * 2 + d) * RH + r:(l * 2 + d) * RH + r + 1]
                            act_e.activation(dec[m % 4][:, 0:w], src, ACT.Exp, bias=lnscale, scale=lg)\
                                .then_inc(S(l, "dec_ready"), 1)
                            m += 1
                meet(act_e, "act_e")

                nt = tiles(l)
                for u in range(2 * nt):
                    t, half = divmod(u, 2)
                    act_e.wait_ge(S(l, "mt_done"), u + 1)
                    act_e.activation(mixT[:, 4 * half:4 * half + 4, t * P:(t + 1) * P],
                                     PS[4 + u % 4][:, :].rearrange("p (a b) -> p a b", a=4), ACT.Copy)\
                        .then_inc(S(l, "mt_evac"), 1)
                meet(act_e, "act_e")

                for t in range(nt):
                    if t >= 2:
                        act_e.wait_ge(S(l, "g_ss"), t - 1)
                    act_e.activation(junk2[t % 2], X[:, t, :], ACT.Square, accum_out=ss[:, t:t + 1])\
                        .then_inc(S(l, "g_ss"), 1)
                for u in range(2 * nt):
                    t, half = divmod(u, 2)
                    act_e.wait_ge(S(l, "g_tr"), u + 1)
                    act_e.activation(hT[:, 4 * half:4 * half + 4, t * P:(t + 1) * P],
                                     PS[4 + u % 4][:, :].rearrange("p (a b) -> p a b", a=4), ACT.Copy)\
                        .then_inc(S(l, "g_hT"), 1)
                act_e.wait_ge(S(l, "logit_done"), 1)
                act_e.activation(route_t["score"][:, 0:nt, :].rearrange("p a b -> p (a b)"), PS[0][:, 0:nt * NE], ACT.Exp, scale=-1.0)\
                    .then_inc(S(l, "exp_done"), 1)
                meet(act_e, "act_e")

                act_e.wait_ge(S(l, "route_ready"), 1)

                def evac_x(s, half):
                    act_e.activation(xgT[s][:, 4 * half:4 * half + 4, :],
                                     PS[half][:, :].rearrange("p (a b) -> p a b", a=4), ACT.Copy)\
                        .then_inc(S(l, "t_evac"), 1)

                act_e.wait_ge(S(l, "t_done"), 1)
                evac_x(0, 0)
                act_e.wait_ge(S(l, "xg_used0"), 1)
                evac_x(0, 1)
                n_pairs = act_e.value_load(ints[0:1, 79:80], min_val=NE // 2, max_val=NBLK // 2 - 1)
                with act_e.Fori(0, n_pairs) as i:
                    for s in range(2):
                        o = 1 - s
                        act_e.wait_ge(S(l, f"g_done{s}"), i + 1)
                        act_e.activation(th[s], PS[2][:, :], ACT.Tanh, scale=0.5).then_inc(S(l, "th_ready"), 1)
                        act_e.wait_ge(S(l, "t_done"), 2 * i + s + 2)
                        evac_x(o, 0)
                        act_e.wait_ge(S(l, "at_done"), 2 * i + s + 1)
                        act_e.activation(aT[s], PS[4][:, :].rearrange("p (a b) -> p a b", a=4), ACT.Copy)\
                            .then_inc(S(l, "aT_ready"), 1)
                        act_e.wait_ge(S(l, f"xg_used{o}"), i + 1 + s)
                        evac_x(o, 1)
                        act_e.wait_ge(S(l, "yb_ready"), 4 * i + 2 * s + 2)
                        act_e.dma_start(y_d[bass.ds(i * (2 * P) + s * P, P), :], yb[s])\
                            .then_inc(S(l, f"y_out{s}"), 16)
                meet(act_e, "act_e")
                meet(act_e, "act_e")
                if l < DEPTH - 1:
                    act_e.wait_ge(cleared, 1)
                    act_e.drain()

        @block.vector
        def _(dve):
            link = chain(dve, "dve", dve_step)
            def route(l):
                T = tiles(l)
                v = {n: (a[:, 0:T, :] if a.shape[1] == NT and len(a.shape) == 3 else
                         a[:, 0:T * NG, :] if n == "pairs" else a[:, 0:T] if a.shape[1] == NT else a)
                     for n, a in route_t.items()}

                def tt(out, a, b, op):
                    link(dve.tensor_tensor(out, a, b, op))

                def ts(out, a, x, op, y=None, op2=None):
                    link(dve.tensor_scalar(out, a, x, y, op, op2) if op2 is not None
                         else dve.tensor_scalar(out, a, x, None, op))

                def red(out, a, op):
                    link(dve.tensor_reduce(out, a, AX.X, op))

                def over(a, n):
                    return a.unsqueeze(2).broadcast_to([P, T, n])

                def per_token(a, n):
                    return a.unsqueeze(1).broadcast_to([P, T, n])

                dve.wait_ge(S(l, "exp_done"), 1)
                ts(v["score"], v["score"], 1.0, ALU.add)
                link(dve.reciprocal(v["score"], v["score"]))
                tt(v["ssel"], v["score"], per_token(rbias, NE), ALU.add)
                s4 = v["ssel"].rearrange("p t (g e) -> p (t g) e", e=EPG)
                o = 0
                for dist in range(1, EPG):
                    tt(v["pairs"][:, :, o:o + EPG - dist], s4[:, :, 0:EPG - dist], s4[:, :, dist:EPG], ALU.add)
                    o += EPG - dist
                red(v["gsum"].rearrange("p t g -> p (t g)"), v["pairs"], ALU.max)
                red(v["gmax"], v["gsum"], ALU.max)
                tt(v["gcand"], v["gsum"], over(v["gmax"], NG), ALU.is_equal)
                tt(v["gcand"], v["gcand"], per_token(rev8, NG), ALU.mult)
                red(v["gfirst"], v["gcand"], ALU.max)
                tt(v["ing"], per_token(rev8, NG), over(v["gfirst"], NG), ALU.is_equal)
                ts(v["pen"], v["ing"], BIG, ALU.mult, -BIG, ALU.add)
                tt(v["ms"].rearrange("p t (g e) -> p (t g) e", e=EPG), s4,
                   v["pen"].rearrange("p t g -> p (t g)").unsqueeze(2).broadcast_to([P, T * NG, EPG]), ALU.add)
                for k in range(2):
                    oh, first = v[f"oh{k}"], v[f"first{k}"]
                    red(v["top"], v["ms"], ALU.max)
                    tt(v["cand"], v["ms"], over(v["top"], NE), ALU.is_equal)
                    tt(v["cand"], v["cand"], per_token(rev32, NE), ALU.mult)
                    red(first, v["cand"], ALU.max)
                    tt(oh, per_token(rev32, NE), over(first, NE), ALU.is_equal)
                    if k == 0:
                        link(dve.scalar_tensor_tensor(v["ms"], oh, -BIG, v["ms"], ALU.mult, ALU.add))
                dve.tensor_tensor(v["M"], v["oh0"], v["oh1"], ALU.add).then_inc(S(l, "m_ready"), 1)
                for k in range(2):
                    tt(v["tmp"], v["score"], v[f"oh{k}"], ALU.mult)
                    red(v[f"s{k}"], v["tmp"], ALU.add)
                tt(v["top"], v["s0"], v["s1"], ALU.add)
                link(dve.reciprocal(v["top"], v["top"]))
                for k in range(2):
                    tt(wgt.rearrange("p (t k) -> p t k", k=2)[:, 0:T, k], v[f"s{k}"], v["top"], ALU.mult)

                dve.wait_ge(S(l, "rank_done"), 1)
                count = PS[1][:, T * NE:(T + 1) * NE]
                link(dve.memset(v["zero"], 0.0))
                ts(v["extra"], count, float(P), ALU.is_gt)
                for m in range(2, T):
                    link(dve.scalar_tensor_tensor(v["extra"], count, float(m * P), v["extra"], ALU.is_gt, ALU.add))
                link(dve.tensor_tensor_scan(v["ovinc"], v["extra"], v["zero"], 0.0, ALU.add, ALU.add))
                tt(v["ovb"], v["ovinc"], v["extra"], ALU.subtract)
                tt(v["ovcmp"], v["ovinc"].unsqueeze(1).broadcast_to([P, NOV, NE]),
                   ovidx.unsqueeze(2).broadcast_to([P, NOV, NE]), ALU.is_le)
                red(v["ovexp"], v["ovcmp"], ALU.add)
                ts(ints[:, NE:NBLK], v["ovexp"], float(NE - 1), ALU.min)
                nov = v["ovinc"][:, NE - 1:NE]
                ts(v["npair"], nov, 0.0, ALU.is_gt, float(NE // 2), ALU.add)
                for m in range(1, NOV // 2 - 1):
                    link(dve.scalar_tensor_tensor(v["npair"], nov, 2.0 * m, v["npair"], ALU.is_gt, ALU.add))
                link(dve.tensor_copy(ints[:, 79:80], v["npair"]))

                ranks = PS[1][:, 0:T * NE].rearrange("p (t e) -> p t e", e=NE)
                for k in range(2):
                    tt(v["tmp"], v[f"oh{k}"], ranks, ALU.mult)
                    red(v["rank"], v["tmp"], ALU.add)
                    tt(v["tmp"], v[f"oh{k}"], per_token(v["ovb"], NE), ALU.mult)
                    red(v["ov"], v["tmp"], ALU.add)
                    ts(v["q"], v["rank"], float(P), ALU.is_ge)
                    for m in range(2, T):
                        link(dve.scalar_tensor_tensor(v["q"], v["rank"], float(m * P), v["q"], ALU.is_ge, ALU.add))
                    link(dve.scalar_tensor_tensor(v["r"], v["q"], -float(P), v["rank"], ALU.mult, ALU.add))
                    ts(v["pos"], v["q"], 0.0, ALU.is_gt)
                    ts(v["e"], v[f"first{k}"], -1.0, ALU.mult, float(NE), ALU.add)
                    tt(v["blk"], v["ov"], v["q"], ALU.add)
                    ts(v["blk"], v["blk"], float(NE - 1), ALU.add)
                    tt(v["blk"], v["blk"], v["e"], ALU.subtract)
                    tt(v["blk"], v["blk"], v["pos"], ALU.mult)
                    tt(v["blk"], v["blk"], v["e"], ALU.add)
                    link(dve.scalar_tensor_tensor(
                        ints[:, 128:128 + 2 * NT].rearrange("p (t k) -> p t k", k=2)[:, 0:T, k],
                        v["r"], float(NBLK), v["blk"], ALU.mult, ALU.add))
                    i = dve.scalar_tensor_tensor(
                        ints[:, 140:140 + 2 * NT].rearrange("p (t k) -> p t k", k=2)[:, 0:T, k],
                        v["blk"], float(P), v["r"], ALU.mult, ALU.add)
                    if k == 0:
                        link(i)
                i.then_inc(S(l, "route_ready"), 1)

            dve.wait_ge(const_in, 16 * N_CONST)
            link(dve.memset(sc32[:, :, :], 0.0))
            dve.wait_ge(sc_tanh, 1)
            link(dve.scalar_tensor_tensor(cth, cth, 1.0, cc, ALU.add, ALU.mult))
            dve.tensor_scalar(sc32[:, :, 0:2], cth.rearrange("p (k i) -> p k i", i=2), 0.5, None, ALU.mult)\
                .then_inc(sc_ready, 1)
            dve.wait_ge(decay_exp, 1)
            dve.tensor_scalar(decay, decay, -1.0, None, ALU.mult).then_inc(S(0, "lg_ready"), 1)
            link(dve.tensor_scalar(nag[:, 0:2, :], nag[:, 0:2, :], NAD ** -0.5, None, ALU.mult))

            for l in range(DEPTH):
                if l:
                    dve.memset(msq[:, :], 1.0).then_inc(S(l, "lg_ready"), 1)
                dve.memset(adab, 0.0).then_inc(S(l, "adab_zero"), 1)
                dve.wait_ge(S(l, "adab_in"), 128)
                for r in range(3):
                    dve.wait_ge(S(l, "ada_done"), 4 * (r + 1))
                    dve.tensor_tensor(modsb[:, r, :], PS[r][:, :], adab[:, r, :], ALU.add)\
                        .then_inc(S(l, "mod_rows"), 1)
                dve.wait_ge(S(l, "modb_in"), 80)
                for n in (0, 2):
                    link(dve.scalar_tensor_tensor(bc[n][:, :], bc[n][:, :], 1.0, normw, ALU.add, ALU.mult))
                dve.wait_ge(S(l, "ss_done"), NT)
                dve.tensor_scalar(msq[:, 0:NT], ss[:, 0:NT], 1.0 / D, EPS, ALU.mult, ALU.add)\
                    .then_inc(S(l, "ms_ready"), 1)
                dve.wait_ge(S(l, "rstd_ready"), 1)
                for t in range(NT):
                    a, b = (0, 1) if t < LAT else (2, 3)
                    if t >= 2:
                        dve.wait_ge(S(l, "tr_done"), 2 * (t - 1))
                    link(dve.scalar_tensor_tensor(hrow1[t % 2], X[:, t, :], rstd[:, t:t + 1], bc[a][:, :],
                                                  ALU.mult, ALU.mult))
                    dve.tensor_tensor(hrow1[t % 2], hrow1[t % 2], bc[b][:, :], ALU.add)\
                        .then_inc(S(l, "hrow_ready"), 1)

                units = proj_units(l)
                n_act, n_row = counted(units, act_reads), counted(units, needs_row)
                n_norm = counted(units, lambda u: KIND[u[0]] == "norm")

                def row_free(n):
                    m = n_row[n] - 1
                    if m >= 2:
                        dve.wait_ge(S(l, "trow_done"), m - 1)
                    return rowbuf[m % 2]

                def norm_front(n):
                    b = (n_norm[n] - 1) % 2
                    o = slice(b * NAH, (b + 1) * NAH)
                    dve.wait_ge(S(l, "act_rel"), n_act[n])
                    link(dve.tensor_reduce(qk_ss[:, o], sqbuf[b].rearrange("p (h d) -> p h d", h=NAH), AX.X, ALU.add))
                    dve.tensor_scalar(qk_ms[:, o], qk_ss[:, o], 1.0 / NAD, EPS, ALU.mult, ALU.add)\
                        .then_inc(S(l, "qk_ms_ready"), 1)

                def norm_back(n):
                    c = units[n][0]
                    b = (n_norm[n] - 1) % 2
                    row = row_free(n).rearrange("p (h d) -> p h d", h=NAH)
                    dve.wait_ge(S(l, "qk_rs_ready"), n_norm[n])
                    link(dve.tensor_tensor(row, PS[n % 4][:, :].rearrange("p (h d) -> p h d", h=NAH),
                                           qk_rs[:, b * NAH:(b + 1) * NAH].unsqueeze(2)
                                           .broadcast_to([P, NAH, NAD]), ALU.mult))
                    dve.tensor_tensor(row, row, nag[:, 2 * c + l:2 * c + l + 1, :].broadcast_to([P, NAH, NAD]),
                                      ALU.mult).then_inc(S(l, "row_ready"), 1)

                def rope(n):
                    t = units[n][1]
                    row = row_free(n)
                    dve.wait_ge(S(l, "proj_done"), n + 1)
                    if t >= LAT:
                        dve.tensor_copy(row, PS[n % 4][:, :]).then_inc(S(l, "row_ready"), 1)
                        return
                    v = PS[n % 4][:, :].rearrange("p (h a b) -> p h a b", a=4, b=32)
                    q = sqbuf[n % 2].rearrange("p (h a b) -> p h a b", a=4, b=32)
                    link(dve.tensor_tensor(row.rearrange("p (h d) -> p h d", h=RH),
                                           PS[n % 4][:, :].rearrange("p (h d) -> p h d", h=RH),
                                           cosF[:, t:t + 1, :].broadcast_to([P, RH, RD]), ALU.mult))
                    sn = sinF[:, t, :].rearrange("p (a b) -> p a b", a=2)
                    for ax in range(2):
                        s2 = sn[:, ax:ax + 1, :].broadcast_to([P, RH, 32])
                        link(dve.tensor_tensor(q[:, :, 2 * ax, :], v[:, :, 2 * ax + 1, :], s2, ALU.mult))
                        link(dve.tensor_tensor(q[:, :, 2 * ax + 1, :], v[:, :, 2 * ax, :], s2, ALU.mult))
                    for x in (0, 1):
                        i = dve.tensor_tensor(
                            row.rearrange("p (g b) -> p g b", b=32)[:, x::2, :],
                            row.rearrange("p (g b) -> p g b", b=32)[:, x::2, :],
                            sqbuf[n % 2].rearrange("p (g b) -> p g b", b=32)[:, x::2, :],
                            ALU.subtract if x == 0 else ALU.add)
                        if x == 0:
                            link(i)
                    i.then_inc(S(l, "row_ready"), 1)

                dve.wait_ge(S(l, "tab_in"), 32)
                for n in range(len(units) + 1):
                    if n < len(units) and KIND[units[n][0]] == "norm":
                        norm_front(n)
                    if n >= 1 and KIND[units[n - 1][0]] == "norm":
                        norm_back(n - 1)
                    if n < len(units) and KIND[units[n][0]] == "rope":
                        rope(n)
                    if n < len(units) and KIND[units[n][0]] == "gate":
                        c, t = units[n]
                        g = {6: gf, 7: gb}[c][:, t, :]
                        dve.wait_ge(S(l, "act_rel"), n_act[n])
                        dve.scalar_tensor_tensor(g, g, 1.0, PS[n % 4][:, :], ALU.add, ALU.mult)\
                            .then_inc(S(l, "gate_rel"), 1)
                meet(dve, "dve")

                dve.wait_ge(S(l, "mask_in"), 16)
                dve.wait_ge(S(l, "bias_in"), 16 * 3 * QBLK)
                for ty in range(3):
                    link(dve.tensor_tensor(bias[:, :, ty, :], bias[:, :, ty, :],
                                           mask[:, ty:ty + 1, :].broadcast_to([P, NAH, KSPAN]), ALU.add))
                nu = na_units(l)

                def norm_o(j):
                    o = slice(j * NAH, (j + 1) * NAH)
                    dve.wait_ge(S(l, "pv_done"), NAH * (j + 1))
                    link(dve.reciprocal(rinv[:, o], rsum[:, o]))
                    dve.tensor_tensor(mix[:, j, 0:CH].rearrange("p (h d) -> p h d", h=NAH),
                                      PS[5 + j % 2][:, :].rearrange("p (h d) -> p h d", h=NAH),
                                      rinv[:, o].unsqueeze(2).broadcast_to([P, NAH, NAD]), ALU.mult)\
                        .then_inc(S(l, "o_norm"), 1)

                for n, (j, h, ranges, _, ty) in enumerate(nu):
                    w = sum(k for _, k in ranges)
                    dve.wait_ge(S(l, "s_done"), n + 1)
                    if ty is not None:
                        link(dve.tensor_tensor(PS[n % 3][:, 0:KSPAN], PS[n % 3][:, 0:KSPAN], bias[:, h, ty, :], ALU.add))
                    if n >= 4:
                        dve.wait_ge(S(l, "p_ready"), n - 3)
                    dve.tensor_reduce(negmax[:, n % 4:n % 4 + 1], PS[n % 3][:, 0:w], AX.X, ALU.max, negate=True)\
                        .then_inc(S(l, "nm_ready"), 1)
                    if n % NAH == 3 and n > NAH:
                        norm_o(n // NAH - 1)
                norm_o(len(nu) // NAH - 1)
                meet(dve, "dve")

                groups = ret_groups(l)

                def head_norm(g):
                    r, lat, qts, kts = groups[g]
                    n = len(qts)
                    dve.wait_ge(S(l, "pvr_done"), 2 * (g + 1))
                    for d in range(2):
                        for i in range(n):
                            u = d * 4 + i
                            o = PS[2 + 2 * d + g % 2][:, i * P:(i + 1) * P]
                            link(dve.bn_stats(bnst[:, u * 6:u * 6 + 6], o))
                            link(dve.bn_aggr(mv[:, u * 2:u * 2 + 2], bnst[:, u * 6:u * 6 + 6]))
                    dve.tensor_scalar(hvar, mv.rearrange("p (a b) -> p a b", b=2)[:, :, 1], RET_EPS, 4.0,
                                      ALU.add, ALU.mult).then_inc(S(l, "hvar_ready"), 1)
                    dve.wait_ge(S(l, "hrstd_ready"), g + 1)
                    for d in range(2):
                        for i in range(n):
                            u = d * 4 + i
                            o = PS[2 + 2 * d + g % 2][:, i * P:(i + 1) * P]
                            link(dve.tensor_scalar(ofb[d][:, i * P:(i + 1) * P], o, mv[:, 2 * u:2 * u + 1],
                                                   hrstd[:, u:u + 1], ALU.subtract, ALU.mult))
                        v = ofb[d][:, 0:n * P].rearrange("p (a b) -> p a b", a=n)
                        gate = (gf, gb)[d][:, qts[0]:qts[0] + n, r * RD:(r + 1) * RD]
                        link(dve.tensor_tensor(v, v, gate, ALU.mult))
                    dve.tensor_tensor(mix[:, qts[0]:qts[0] + n, CH + r * RD:CH + (r + 1) * RD],
                                      ofb[0][:, 0:n * P].rearrange("p (a b) -> p a b", a=n),
                                      ofb[1][:, 0:n * P].rearrange("p (a b) -> p a b", a=n), ALU.add)\
                        .then_inc(S(l, "ret_norm"), 1)

                link(dve.memset(mv, 0.0))
                m = 0
                for g, (r, lat, qts, kts) in enumerate(groups):
                    w = len(qts) * P
                    if g >= 1:
                        dve.wait_ge(S(l, "pvr_done"), 2 * g)
                    for a in range(len(kts)):
                        for d in range(2):
                            dve.wait_ge(S(l, "st_done"), m // 2 + 1)
                            dve.wait_ge(S(l, "dec_ready"), m + 1)
                            dve.tensor_tensor(Wd[d][:, a, 0:w], PS[(m // 2) % 2][:, 0:w], dec[m % 4][:, 0:w], ALU.mult)\
                                .then_inc(S(l, "w_mult"), 1)
                            m += 1
                    if g >= 1:
                        head_norm(g - 1)
                head_norm(len(groups) - 1)
                meet(dve, "dve")

                nt = tiles(l)
                dve.wait_ge(S(l, "gate_in"), 32)
                for n in range(2 * nt):
                    c, t = divmod(n, nt)
                    dve.wait_ge(S(l, "op_done"), n + 1)
                    link(dve.tensor_tensor(otmp[n % 2], PS[n % 4][:, :],
                                           bc[0 if t < LAT else 1][:, c * CH:(c + 1) * CH], ALU.mult))
                    xs = X[:, t, c * CH:(c + 1) * CH]
                    dve.tensor_tensor(xs, xs, otmp[n % 2], ALU.add).then_inc(S(l, "x_upd"), 1)
                meet(dve, "dve")

                dve.wait_ge(S(l, "g_in"), 80)
                for n in (0, 2):
                    link(dve.scalar_tensor_tensor(bc[n][:, :], bc[n][:, :], 1.0, normw2, ALU.add, ALU.mult))
                dve.wait_ge(S(l, "g_ss"), nt)
                dve.tensor_scalar(msq[:, 0:NT], ss[:, 0:NT], 1.0 / D, EPS, ALU.mult, ALU.add)\
                    .then_inc(S(l, "g_ms"), 1)
                dve.wait_ge(S(l, "g_rs"), 1)
                for t in range(nt):
                    a, b = (0, 1) if t < LAT else (2, 3)
                    link(dve.scalar_tensor_tensor(hrow2[t], X[:, t, :], rstd[:, t:t + 1], bc[a][:, :],
                                                  ALU.mult, ALU.mult))
                    dve.tensor_tensor(hrow2[t], hrow2[t], bc[b][:, :], ALU.add).then_inc(S(l, "g_row"), 1)
                route(l)
                meet(dve, "dve")

                n_pairs = dve.value_load(ints[0:1, 79:80], min_val=NE // 2, max_val=NBLK // 2 - 1)
                for s in range(2):
                    dve.sem_inc(S(l, f"y_out{s}"), 16)
                with dve.Fori(0, n_pairs) as i:
                    for s in range(2):
                        dve.wait_ge(S(l, "th_ready"), 2 * i + s + 1)
                        dve.scalar_tensor_tensor(act[s], th[s], 1.0, PS[2][:, :], ALU.add, ALU.mult)\
                            .then_inc(S(l, "gate_step"), 1)
                        dve.wait_ge(S(l, "gate_step"), 2 * i + s + 1)
                        dve.wait_ge(S(l, f"u_done{s}"), i + 1)
                        dve.scalar_tensor_tensor(act[s], act[s], 0.5, PS[3][:, :], ALU.mult, ALU.mult)\
                            .then_inc(S(l, "a_ready"), 1)
                        dve.wait_ge(S(l, f"y_out{s}"), 16 * i + 16)
                        dve.wait_ge(S(l, "y_done"), 2 * i + s + 1)
                        dve.tensor_copy(yb[s][:, 0:CH], PS[5][:, :]).then_inc(S(l, "yb_ready"), 1)
                        dve.wait_ge(S(l, f"d_done{s}"), i + 1)
                        dve.tensor_copy(yb[s][:, CH:D], PS[6][:, :]).then_inc(S(l, "yb_ready"), 1)
                meet(dve, "dve")

                dve.wait_ge(S(l, "gb_in"), 32)
                for t in range(nt):
                    b = t % 2
                    g = bc[0 if t < LAT else 1][:, :]
                    dve.wait_ge(S(l, f"yg{b}"), 32 * (t // 2 + 1))
                    link(dve.scalar_tensor_tensor(z1[b], y1[b], wgt[:, 2 * t:2 * t + 1], g, ALU.mult, ALU.mult))
                    link(dve.scalar_tensor_tensor(z2[b], y2[b], wgt[:, 2 * t + 1:2 * t + 2], g, ALU.mult, ALU.mult))
                    link(dve.tensor_tensor(z1[b], z1[b], z2[b], ALU.add))
                    dve.tensor_tensor(X[:, t, :], X[:, t, :], z1[b], ALU.add).then_inc(S(l, "comb_done"), 1)
                meet(dve, "dve")
                if l < DEPTH - 1:
                    dve.wait_ge(cleared, 1)
                    dve.drain()


def _constants():
    f = np.float32
    tok = np.arange(SEQ)
    col, row = tok // ROWS, tok % ROWS
    time = row * COLS + col
    freqs = 10000.0 ** (-np.arange(32, dtype=np.float64) / 32)
    ang = np.stack([row[:, None] * freqs, col[:, None] * freqs], axis=1)
    cos = np.repeat(np.cos(ang)[:, :, None, :], 2, axis=2).reshape(LAT, P, RD)
    sin = np.sin(ang).reshape(LAT, P, 64)
    ct = np.arange(CTX)
    fwd = np.concatenate([np.where(time[None] >= time[:, None], time[None] - time[:, None], BIG),
                          time[None] + CTX - ct[:, None]])
    bwd = np.concatenate([np.where(time[None] <= time[:, None], time[:, None] - time[None], BIG),
                          ct[:, None] + SEQ - time[None]])
    cf = np.where(ct[None] >= ct[:, None], ct[None] - ct[:, None], BIG)
    delta = np.stack([fwd, bwd]).reshape(2, NT, P, SEQ).transpose(2, 0, 1, 3)
    dctx = np.stack([cf, cf.T]).reshape(2, 2, P, CTX).transpose(2, 0, 1, 3)
    mask = np.zeros((P, 3, KSPAN))
    for ty, j in ((0, 0), (1, 1), (2, 3)):
        qcol = j * QBLK + np.arange(QBLK)
        c0 = np.clip(qcol - WIN_W // 2, 0, COLS - WIN_W)
        kcol = KSTART[j] + np.arange(KBLK)
        ok = (kcol[None] >= c0[:, None]) & (kcol[None] < c0[:, None] + WIN_W)
        mask[:, ty] = np.repeat(np.repeat(np.where(ok, 0.0, -BIG), ROWS, 0), ROWS, 1)
    return {
        "ident": np.eye(P, dtype=f), "upper": np.triu(np.ones((P, P), f), 1),
        "cos_t": cos.transpose(1, 0, 2).astype(f), "sin_t": sin.transpose(1, 0, 2).astype(f),
        "delta": delta.astype(f), "delta_ctx": dctx.astype(f), "na_mask": mask.astype(f),
        "rev8": (NG - np.arange(NG)).astype(f), "rev32": (NE - np.arange(NE)).astype(f),
        "ovidx": np.arange(NOV).astype(f), "first_blocks": np.arange(NE, dtype=np.int32),
        "token_ids": (np.arange(NT)[None] * P + np.arange(P)[:, None]).astype(np.int32),
    }


def kernel(**inputs):
    import concourse.bacc as bacc
    from concourse.bass_utils import run_bass_kernel_spmd

    x = {k: np.asarray(v) for k, v in inputs.items()}
    arrays = {n: x[n] for n in ("ada_w", "ada_b", "norm_mix_w", "norm_ffn_w", "w_in", "na_q_norm", "na_k_norm",
                                "ret_decay", "w_out", "router_w", "router_bias", "exp_w_gate", "exp_w_up",
                                "exp_w_down")}
    arrays["x"] = x["x"][0].reshape(ROWS, COLS, D).transpose(1, 0, 2).reshape(SEQ, D)
    arrays["ctx"] = x["ctx"][0]
    arrays["cc"] = np.stack([x["c"][0], x["c_ctx"]], -1).reshape(KD, P, 2).transpose(1, 0, 2).reshape(P, 2 * KD)
    rpb = x["na_rpb"]
    win = np.stack([rpb[:, :, ROWS - 1 - q:2 * ROWS - 1 - q, :] for q in range(ROWS)], 1).transpose(0, 1, 2, 4, 3)
    win = np.pad(win, ((0, 0), (0, 0), (0, 0), (V_PAD, V_PAD), (0, 0)))
    arrays["rpb"] = win.reshape(DEPTH, ROWS, NAH, -1)
    arrays.update(_constants())
    arrays = {n: np.ascontiguousarray(a) for n, a in arrays.items()}
    nc = bacc.Bacc("TRN2", target_bir_lowering=False, num_devices=1)
    aps = {n: nc.dram_tensor(f"in_{n}", a.shape, mybir.dt.from_np(a.dtype), kind="ExternalInput").ap()
           for n, a in arrays.items()}
    aps["out"] = nc.dram_tensor("out_x", (SEQ, D), F32, kind="ExternalOutput").ap()
    build(nc, aps)
    r = run_bass_kernel_spmd(nc, [{f"in_{n}": a for n, a in arrays.items()}], core_ids=[0])
    out = r.results[0]["out_x"]
    return out.reshape(COLS, ROWS, D).transpose(1, 0, 2).reshape(1, SEQ, D)
```

```python
from contextlib import ExitStack
import math

import numpy as np

import concourse.bass as bass
from concourse import mybir

F32 = mybir.dt.float32
F32R = mybir.dt.float32r
I32 = mybir.dt.int32
ACT = mybir.ActivationFunctionType
ALU = mybir.AluOpType
AX = mybir.AxisListType

P = 128
DEPTH, D, SEQ, CTX = 2, 1024, 512, 256
ROWS, COLS = 8, 64
KD = D // P
LAT = SEQ // P
NT = (SEQ + CTX) // P
TOK = SEQ + CTX
NAH, NAD = 8, 64
RH, RD = 4, 128
CH = 512
WIN_W, KBLK, QBLK = 16, 32, 16
KSPAN = KBLK * ROWS
NE, NG, EPG = 32, 8, 4
FF = 512
NOV = 2 * TOK // P + 2
NBLK = NE + NOV
UNITS = 12
NO_ROW = 4095
BIG = 1.0e30
EPS = 1e-6
RET_EPS = 1e-5

K = 256
W_SLOTS = [0, 16 * K]
TURN_AT = 7
QA, KA, VA = 32 * K, 44 * K, 56 * K
QB, KB, VB, GF, GB = 74 * K, 86 * K, 98 * K, 110 * K, 122 * K
ARENA = 134 * K
SMALL = 432

KSTART = [0, 8, 24, 32]
BIAS_TYPE = [0, 1, 1, 2]
BIAS_START = [0, -8, -16]
V_TILES = [[0, 1], [6, 7], [7, 8], [2, 3]]
V_PAD = 16


def counted(units, pred):
    n, out = 0, []
    for u in units:
        n += bool(pred(u))
        out.append(n)
    return out


def build(nc, A):
    stack = ExitStack()
    with stack:
        def sb(name, shape, dt=F32):
            return stack.enter_context(nc.sbuf_tensor(name, shape, dt))

        def sem(name):
            return stack.enter_context(nc.semaphore(name))

        def dram(name, shape, dt=F32):
            return nc.dram_tensor(name, shape, dt).ap()

        X = sb("X", [P, NT, D])
        hT = sb("hT", [P, KD, TOK])
        hT_at = nc.sbuf_base - 4 * KD * TOK
        arena = sb("arena", [P, ARENA])
        arena_at = nc.sbuf_base - 4 * ARENA
        bc = [sb(f"bc{i}", [P, D]) for i in range(4)]
        ident = sb("ident", [P, P])
        upper = sb("upper", [P, P])
        ones = sb("ones", [P, P])
        tabs = sb("tabs", [P, 768])
        sc32 = sb("sc32", [P, KD, 32])
        rw = sb("rw", [P, KD, NE])
        small = sb("small", [P, SMALL])
        ints = sb("ints", [P, 152], I32)
        idx_slot = [sb(f"idx_slot{s}", [P, 1], I32) for s in range(2)]
        nag = sb("nag", [P, 4, NAD])
        PS = [stack.enter_context(nc.psum_tensor(f"PS{i}", [P, 512], F32)) for i in range(8)]

        used = [0]

        def cut(n):
            used[0] += n
            return small[:, used[0] - n:used[0]]

        neghalf = cut(32)
        ss = cut(8)
        msq = cut(8)
        rstd = cut(8)
        lnscale = cut(1)
        decay = cut(DEPTH * 2 * RH)
        cc = cut(2 * KD)
        cth = cut(2 * KD)
        qk_ss = cut(2 * NAH)
        qk_ms = cut(2 * NAH)
        qk_rs = cut(2 * NAH)
        negmax = cut(4)
        rsum = cut(NT * NAH)
        rinv = cut(NT * NAH)
        bnst = cut(8 * 6)
        mv = cut(8 * 2)
        hvar = cut(8)
        hrstd = cut(8)
        wgt = cut(2 * NT)
        rbias = cut(NE)
        rev8 = cut(NG)
        rev32 = cut(NE)
        ovidx = cut(NOV)
        assert used[0] <= SMALL

        def area(off, shape):
            n = int(np.prod(shape))
            names = "abc"[:len(shape)]
            v = arena[:, off:off + n]
            if len(shape) > 1:
                pat = f"p ({' '.join(names)}) -> p {' '.join(names)}"
                v = v.rearrange(pat, **{names[i]: shape[i] for i in range(len(shape))})
            return v

        ada_w = [area(110 * K + s * 2048, (4, CH)) for s in range(2)]
        rows = area(126 * K, (4, CH))
        win = [area(W_SLOTS[s], (KD, CH)) for s in range(2)]
        qaT, kaT = area(QA, (4, TOK)), area(KA, (4, TOK))
        va = area(VA, (9, CH))
        qbT, kbT = area(QB, (RH, TOK)), area(KB, (RH, TOK))
        vb, gf, gb = area(VB, (NT, CH)), area(GF, (NT, CH)), area(GB, (NT, CH))
        hTf = hT[:, :, :].rearrange("p a b -> p (a b)")
        normw = area(QB, (D,))
        hrow1 = [area(QB + (1 + i) * D, (D,)) for i in range(2)]
        junk = [area(QB + (3 + i) * D, (D,)) for i in range(2)]
        rowbuf = [area(VB + 1024 + i * 512, (512,)) for i in range(2)]
        sqbuf = [area(VB + 2048 + i * 512, (512,)) for i in range(2)]
        cosF = tabs[:, 0:512].rearrange("p (a b) -> p a b", a=4)
        sinF = tabs[:, 512:768].rearrange("p (a b) -> p a b", a=4)
        mask = tabs[:, 0:768].rearrange("p (a b) -> p a b", a=3)
        bias = [area(h * 3 * KSPAN, (3, KSPAN)) for h in range(5)] \
            + [bc[i][:, 0:3 * KSPAN].rearrange("p (a b) -> p a b", a=3) for i in (2, 3)] + [area(16 * K, (3, KSPAN))]
        pexp = [bc[0][:, 0:512], bc[0][:, 512:1024]]
        pT = [bc[1][:, o:o + 512].rearrange("p (a b) -> p a b", a=4) for o in (0, 512)]
        mix = hTf[:, :].rearrange("p (a b) -> p a b", a=NT)
        delta = [area(20 * K, (3, 2, SEQ)), area(0, (3, 2, SEQ))]
        dec = [area(12 * K + i * 512, (512,)) for i in range(4)]
        Wd = [area(32 * K + i * D, (2, SEQ)) for i in range(3)]
        mix_gate = [area(44 * K + i * D, (D,)) for i in range(2)]
        wo0 = area(56 * K, (KD, CH))
        dctx = bc[3][:, 0:1024].rearrange("p (a b c) -> p a b c", a=2, b=2)
        ofb = [bc[2][:, 0:512], bc[2][:, 512:1024]]
        mixT = area(QB, (KD, TOK))
        wo1 = area(0, (KD, CH))
        otmp = [area(52 * K + i * 512, (512,)) for i in range(2)]
        wg = [area(s * 48 * K, (KD, FF)) for s in range(2)]
        wu = [area(s * 48 * K + 16 * K, (KD, FF)) for s in range(2)]
        wd = [area(s * 48 * K + 32 * K, (4, D)) for s in range(2)]
        hrow2 = [area(98 * K + t * D, (D,)) for t in range(NT)]
        normw2 = area(122 * K, (D,))
        junk2 = [area(126 * K, (D,)), area(130 * K, (D,))]
        xg = [area(96 * K + s * D, (D,)) for s in range(2)]
        yb = area(104 * K, (D,))
        th = area(108 * K, (FF,))
        act = area(110 * K, (FF,))

        def raw(s, u):
            if u < 8:
                return (wg, wu)[u // 4][s][:, 2 * (u % 4):2 * (u % 4) + 2, :]
            return wd[s][:, u - 8, :].rearrange("p (a b) -> p a b", a=2)

        def split(name, at, shape):
            return nc.alloc_sbuf_tensor_at(name, [P] + shape, F32R, offset=at)

        x_hi = split("x_hi", arena_at + 4 * 112 * K, [KD, P])
        x_lo = split("x_lo", arena_at + 4 * 116 * K, [KD, P])
        a_hi = split("a_hi", arena_at + 4 * 120 * K, [4, P])
        a_lo = split("a_lo", arena_at + 4 * 122 * K, [4, P])
        w_hi = [split(f"w_hi{i}", hT_at + 4 * i * D, [2, FF]) for i in range(3)]
        w_lo = [split(f"w_lo{i}", hT_at + 4 * (3 + i) * D, [2, FF]) for i in range(3)]
        y1 = [area(2 * i * D, (D,)) for i in range(NT)]
        y2 = [area((2 * i + 1) * D, (D,)) for i in range(NT)]
        z = [area((2 * NT + i) * D, (D,)) for i in range(2)]
        ffn_gate = [area(124 * K + i * D, (D,)) for i in range(2)]
        assign = ints[:, 80:80 + NBLK]
        token = tabs[:, 0:NBLK].bitcast(I32)
        second = tabs[:, 64:64 + NBLK]
        y_idx = tabs[:, 128:129].bitcast(I32)
        y_place = tabs[:, 192:192 + NBLK + 1].bitcast(I32)
        r_at = [0]

        def rt(shape):
            n = int(np.prod(shape))
            i, o = divmod(r_at[0], D)
            if o + n > D:
                i, o = i + 1, 0
            r_at[0] = i * D + o + n
            v = bc[i][:, o:o + n]
            if len(shape) > 1:
                names = "abc"[:len(shape)]
                v = v.rearrange(f"p ({' '.join(names)}) -> p {' '.join(names)}",
                                **{names[k]: shape[k] for k in range(len(shape))})
            return v

        route_t = {n: rt(shape) for n, shape in dict(
            score=(NT, NE), ssel=(NT, NE), pairs=(NT * NG, 6), gsum=(NT, NG), gmax=(NT,), gcand=(NT, NG),
            gfirst=(NT,), ing=(NT, NG), pen=(NT, NG), ms=(NT, NE), top=(NT,), cand=(NT, NE),
            first0=(NT,), first1=(NT,), oh0=(NT, NE), oh1=(NT, NE), M=(NT, NE), tmp=(NT, NE),
            s0=(NT,), s1=(NT,), rank=(NT,), q=(NT,), r=(NT,), pos=(NT,), ov=(NT,), e=(NT,), blk=(NT,),
            extra=(NE,), zero=(NE,), ovinc=(NE,), ovb=(NE,), ovcmp=(NOV, NE), ovexp=(NOV,), npair=(1,)).items()}

        mod_d = [dram(f"mod_d{l}", (3, P, CH)) for l in range(DEPTH)]
        h_d = dram("h_d", (TOK, D))
        y_d = dram("y_d", (2 * TOK, D))
        tok_d = [dram(f"tok_d{l}", (P * NBLK, 1), I32) for l in range(DEPTH)]

        cc_in = sem("cc_in")
        const_in = sem("const_in")
        x_in = sem("x_in")
        tok_zero = sem("tok_zero")
        pool_passed = sem("pool_passed")
        out_done = sem("out_done")
        sc_tanh = sem("sc_tanh")
        sc_ready = sem("sc_ready")
        decay_exp = sem("decay_exp")
        dve_step = sem("dve_step")
        act_step = sem("act_step")
        pool_step = sem("pool_step")
        pe_step = sem("pe_step")
        N_CONST = 12

        NAMES = """ada_in0 ada_in1 ada_done rows_in mod_rows mod_out
        modb_in next_in ss_done ms_ready rstd_ready hrow_ready tr_done hT_ready
        win0 win1 proj_done act_rel gate_rel qk_ms_ready qk_rs_ready row_ready trow_done trow_evac
        vshift tab_in delta_in2 mask_in bias_in0 bias_in1 bias_in2 bias_ready s_done nm_ready p_ready pt_done pt_evac pv_done o_norm
        delta_in lg_ready st_done dec_ready w_mult w_used_r pvr_done hvar_ready hrstd_ready ret_norm
        wo_in0 wo_in1 gate_in mt_done mt_evac op_done x_upd
        g_in g_ss g_ms g_rs g_row g_tr g_hT h_out logit_done exp_done m_ready rank_done route_ready
        tok_out idx_in
        wg_in0 wg_in1 wu_in0 wu_in1 wd_in0 wd_in1 whi_ready wlo_ready w_used
        idx_cp0 idx_cp1 y_idx_cp xg_in0 xg_in1 xg_used0 xg_used1 xt_done xhi_ready xlo_ready
        th_ready gate_step a_ready at_done ahi_ready alo_ready y_copied yb_free y_out
        gb_in y_in0 y_in1 y_in2 y_in3 y_in4 y_in5 z_first comb_done""".split()
        POOL_DMA = ("tok_out", "xg_in0", "xg_in1", "y_out")
        SEMS = {(None, n): sem(n) for n in NAMES if n not in POOL_DMA}
        SEMS.update({(l, n): sem(f"{n}_{l}") for l in range(DEPTH) for n in POOL_DMA})
        met = sem("met")
        cleared = sem("cleared")

        def S(l, name):
            return SEMS[l if name in POOL_DMA else None, name]

        steps = {"dve": 0, "act": 0, "pool": 0, "pe": 0}
        meetings = {}

        def chain(eng, which, s):
            def link(ins):
                ins.then_inc(s, 1)
                steps[which] += 1
                eng.wait_ge(s, steps[which])
            return link

        def meet(eng, who):
            meetings[who] = meetings.get(who, 0) + 1
            eng.drain().then_inc(met, 1)
            eng.wait_ge(met, 5 * meetings[who])

        def tiles(l):
            return NT if l < DEPTH - 1 else LAT

        KIND = ["norm", "norm", "v", "rope", "rope", "v", "gate", "gate"]

        def proj_units(l):
            full = [1, 2, 4, 5]
            return [(c, t) for c in range(8) for t in range(NT if l < DEPTH - 1 or c in full else LAT)]

        def needs_row(u):
            return KIND[u[0]] in ("norm", "rope")

        def act_reads(u):
            return KIND[u[0]] in ("norm", "v", "gate")

        def dve_reads(u):
            return KIND[u[0]] == "gate"

        def ada_pieces(l):
            own = [(l, r, k) for r in range(0 if l == 0 else 1, 3) for k in range(KD)]
            return own + ([(l + 1, 0, k) for k in range(KD)] if l < DEPTH - 1 else [])

        def ada_start(l):
            return KD if l == 0 else 0

        def after_unit(l, n):
            p = n - TURN_AT + ada_start(l)
            return p if n >= TURN_AT and p < len(ada_pieces(l)) else None

        def part_end(l, q):
            return (q + 1) * KD - 1 - ada_start(l) + TURN_AT

        def na_units(l):
            out = []
            for j in range(LAT):
                for h in range(NAH):
                    k0 = KSTART[j] * ROWS
                    out.append((j, h, [(k0, KSPAN), (SEQ, CTX)], V_TILES[j] + [4, 5], BIAS_TYPE[j]))
            if l < DEPTH - 1:
                for t in (4, 5):
                    for h in range(NAH):
                        out.append((t, h, [(SEQ, CTX)], [4, 5], None))
            return out

        def ret_groups(l):
            out = [(r, True, range(0, LAT), range(0, NT)) for r in range(RH)]
            if l < DEPTH - 1:
                out += [(r, False, range(LAT, NT), range(LAT, NT)) for r in range(RH)]
            return out

        def ret_steps(l):
            return [(g, a, r, qts, kt, a == len(kts) - 1)
                    for g, (r, _, qts, kts) in enumerate(ret_groups(l)) for a, kt in enumerate(kts)]

        def ret_end(l, g):
            return [m for m, x in enumerate(ret_steps(l)) if x[0] == g][-1] + 1

        block = stack.enter_context(nc.Block())

        @block.sync
        def _(sp):
            def const(dst, src):
                sp.dma_start(dst, src).then_inc(const_in, 16)

            def piece(l, p):
                ll, r, k = ada_pieces(l)[p]
                if p >= 2:
                    sp.wait_ge(S(l, "ada_done"), p - 1)
                sp.dma_start(ada_w[p % 2], A["ada_w"][ll][k * P:(k + 1) * P, 2048 * r:2048 * (r + 1)]
                             .rearrange("p (j x) -> p j x", x=CH)).then_inc(S(l, f"ada_in{p % 2}"), 16)

            def store_rows(l, q):
                ll, r, _ = ada_pieces(l)[q * KD]
                sp.wait_ge(S(l, "mod_rows"), q + 1)
                sp.dma_start(mod_d[ll][r], rows[:, q, :]).then_inc(S(l, "mod_out"), 16)

            def load_mod(l, dst, i, q):
                src = mod_d[l][q // 2].rearrange("(j s) x -> s j x", s=32)[i, 2 * (q % 2):2 * (q % 2) + 2, :]
                return sp.dma_start(dst.rearrange("p (a b) -> p a b", a=2), src.partition_broadcast(P))

            sp.dma_start(cc, A["cc"]).then_inc(cc_in, 16)
            sp.dma_start(rows[:, 0, :], A["ada_b"][0]).then_inc(S(0, "rows_in"), 16)
            for t in range(NT):
                src = A["x"][t * P:(t + 1) * P, :] if t < LAT else A["ctx"][(t - LAT) * P:(t - LAT + 1) * P, :]
                if t < ada_start(0):
                    piece(0, t)
                sp.dma_start(X[:, t, :], src).then_inc(x_in, 16)
            for p in range(NT, ada_start(0)):
                piece(0, p)
            const(ident[:, :], A["ident"])
            const(upper[:, :], A["upper"])
            const(decay, A["ret_decay"].rearrange("a b c -> (a b c)").partition_broadcast(P))
            const(rw[:, :, :], A["router_w"].rearrange("(k p) n -> p k n", p=P))
            const(rbias, A["router_bias"].partition_broadcast(P))
            const(rev8, A["rev8"].partition_broadcast(P))
            const(rev32, A["rev32"].partition_broadcast(P))
            const(ovidx, A["ovidx"].partition_broadcast(P))
            const(ints[:, 0:NE], A["first_blocks"].partition_broadcast(P))
            const(ints[:, 64:64 + 2 * NT], A["assign_ids"])
            for n, name in enumerate(("na_q_norm", "na_k_norm")):
                const(nag[:, 2 * n:2 * n + 2, :].rearrange("p a b -> p (a b)"),
                      A[name].rearrange("a b -> (a b)").partition_broadcast(P))

            for l in range(DEPTH):
                w_in = A["w_in"][l].rearrange("(k p) n -> p k n", p=P)

                def load_win(c):
                    sp.dma_start(win[c % 2], w_in[:, :, c * CH:(c + 1) * CH]).then_inc(S(l, f"win{c % 2}"), 16)

                if l == 0:
                    store_rows(0, 0)
                    sp.wait_ge(S(l, "mod_out"), 16)
                    for n, (i, q) in enumerate(((0, 1), (0, 0), (1, 1), (1, 0))):
                        load_mod(0, bc[n][:, :], i, q).then_inc(S(l, "modb_in"), 16)
                    sp.dma_start(normw, A["norm_mix_w"][l].partition_broadcast(P)).then_inc(S(l, "modb_in"), 16)
                load_win(0)
                sp.dma_start(cosF, A["cos_t"]).then_inc(S(l, "tab_in"), 16)
                sp.dma_start(sinF, A["sin_t"]).then_inc(S(l, "tab_in"), 16)
                n_parts = len(ada_pieces(l)) // KD
                q0 = ada_start(l) // KD
                first = 3 * l + (0 if l == 0 else 1) + q0
                sp.dma_start(rows[:, q0:n_parts, :], A["ada_b"][first:first + n_parts - q0]
                             .rearrange("q p x -> p q x")).then_inc(S(l, "rows_in"), 16)
                load_win(1)
                units = proj_units(l)
                last = [max(i for i, u in enumerate(units) if u[0] == c) + 1 for c in range(8)]
                todo = [(last[c - 2], "win", c) for c in range(2, 8)]
                todo += [(max(0, p - 2 - ada_start(l) + TURN_AT), "piece", p)
                         for p in range(ada_start(l), len(ada_pieces(l)))]
                todo += [(part_end(l, q) + 2, "rows", q) for q in range(q0, n_parts)]
                todo += [(last[2] + 2, "vshift", 0), (last[4] + 2, "bias_high", 0), (last[6], "bias_low", 0),
                         (last[7], "bias_top", 0)]
                for _, what, n in sorted(todo, key=lambda x: x[0]):
                    if what == "win":
                        sp.wait_ge(S(l, "proj_done"), last[n - 2])
                        load_win(n)
                    if what == "piece":
                        piece(l, n)
                    if what == "rows":
                        store_rows(l, n)
                    if what == "vshift":
                        sp.wait_ge(S(l, "act_rel"), counted(units, act_reads)[last[2] - 1])
                        sp.dma_start(va[0:64, 6:9, :], va[64:128, 0:3, :]).then_inc(S(l, "vshift"), 16)
                        sp.dma_start(va[64:128, 6:9, :], va[0:64, 1:4, :]).then_inc(S(l, "vshift"), 16)
                    if what == "bias_high":
                        sp.wait_ge(S(l, "trow_done"), sum(needs_row(u) for u in units))
                        sp.dma_start(mask, A["na_mask"]).then_inc(S(l, "mask_in"), 16)
                        for h in (5, 6):
                            sp.dma_start(bias[h], A["rpb"][l][h]).then_inc(S(l, "bias_in0"), 16)
                    if what == "bias_low":
                        sp.wait_ge(S(l, "proj_done"), last[6])
                        for h in range(5):
                            sp.dma_start(bias[h], A["rpb"][l][h]).then_inc(S(l, "bias_in1"), 16)
                    if what == "bias_top":
                        sp.wait_ge(S(l, "proj_done"), last[7])
                        sp.dma_start(bias[7], A["rpb"][l][7]).then_inc(S(l, "bias_in2"), 16)
                        sp.dma_start(delta[0], A["delta"][0]).then_inc(S(l, "delta_in"), 16)
                sp.wait_ge(S(l, "mod_out"), 16 * n_parts)
                meet(sp, "sp")
                meet(sp, "sp")

                sp.dma_start(delta[1], A["delta"][1]).then_inc(S(l, "delta_in2"), 16)
                sp.dma_start(dctx, A["delta_ctx"]).then_inc(S(l, "delta_in2"), 16)
                wo = A["w_out"][l].rearrange("(k p) n -> p k n", p=P)
                sp.dma_start(wo0, wo[:, :, 0:CH]).then_inc(S(l, "wo_in0"), 16)
                for i in range(2):
                    load_mod(l, mix_gate[i], i, 2).then_inc(S(l, "gate_in"), 16)
                meet(sp, "sp")

                sp.dma_start(wo1, wo[:, :, CH:D]).then_inc(S(l, "wo_in1"), 16)
                for n, (i, q) in enumerate(((0, 4), (0, 3), (1, 4), (1, 3))):
                    load_mod(l, bc[n][:, :], i, q).then_inc(S(l, "g_in"), 16)
                sp.dma_start(normw2, A["norm_ffn_w"][l].partition_broadcast(P)).then_inc(S(l, "g_in"), 16)

                def expert_gate(s, e):
                    sp.dma_start(wg[s], A["exp_w_gate"][l, e].rearrange("(k p) n -> p k n", p=P))\
                        .then_inc(S(l, f"wg_in{s}"), 16)

                def expert_up(s, e):
                    sp.dma_start(wu[s], A["exp_w_up"][l, e].rearrange("(k p) n -> p k n", p=P))\
                        .then_inc(S(l, f"wu_in{s}"), 16)

                def expert_down(s, e):
                    sp.dma_start(wd[s], A["exp_w_down"][l, e].rearrange("(k p) n -> p k n", p=P))\
                        .then_inc(S(l, f"wd_in{s}"), 16)

                for t in range(tiles(l)):
                    sp.wait_ge(S(l, "g_row"), t + 1)
                    sp.dma_start(h_d[t * P:(t + 1) * P, :], hrow2[t]).then_inc(S(l, "h_out"), 16)
                sp.wait_ge(S(l, "x_upd"), 2 * tiles(l))
                for s in range(2):
                    expert_gate(s, s)
                    expert_up(s, s)
                    expert_down(s, s)
                sp.wait_ge(S(l, "tok_out"), 32 * tiles(l))
                sp.dma_start(assign, tok_d[l].rearrange("(p b) a -> p (b a)", p=P))\
                    .then_inc(S(l, "idx_in"), 16)
                sp.wait_ge(S(l, "idx_in"), 16)
                sp.wait_ge(S(l, "h_out"), 16 * tiles(l))
                meet(sp, "sp")

                for i in range(2):
                    load_mod(l, ffn_gate[i], i, 5).then_inc(S(l, "gb_in"), 16)
                if l < DEPTH - 1:
                    for n, (i, q) in enumerate(((0, 1), (0, 0), (1, 1), (1, 0))):
                        load_mod(l + 1, bc[n][:, :], i, q).then_inc(S(l, "next_in"), 16)
                sp.wait_ge(S(l, "route_ready"), 1)
                n_pairs = sp.value_load(ints[0:1, 79:80], min_val=NE // 2, max_val=NBLK // 2 - 1)
                with sp.Fori(0, n_pairs - 1) as i:
                    for s in range(2):
                        e = sp.value_load(ints[0:1, bass.ds(2 * i + 2 + s, 1)], min_val=0, max_val=NE - 1)
                        sp.wait_ge(S(l, "wlo_ready"), (2 * i + s) * UNITS + 4)
                        expert_gate(s, e)
                        sp.wait_ge(S(l, "wlo_ready"), (2 * i + s) * UNITS + 8)
                        expert_up(s, e)
                        sp.wait_ge(S(l, "wlo_ready"), (2 * i + s) * UNITS + 12)
                        expert_down(s, e)
                meet(sp, "sp")
                for t in range(tiles(l)):
                    for k, buf in ((0, y1), (1, y2)):
                        sp.dma_start(buf[t], y_d[k * TOK + t * P:k * TOK + (t + 1) * P, :])\
                            .then_inc(S(l, f"y_in{t}"), 16)
                if l < DEPTH - 1:
                    sp.dma_start(normw, A["norm_mix_w"][l + 1].partition_broadcast(P)).then_inc(S(l, "next_in"), 16)
                    sp.wait_ge(S(l, "next_in"), 80)
                if l == DEPTH - 1:
                    for t in range(LAT):
                        sp.wait_ge(S(l, "comb_done"), t + 1)
                        sp.dma_start(A["out"][t * P:(t + 1) * P, :], X[:, t, :]).then_inc(out_done, 16)
                    sp.wait_ge(out_done, 16 * LAT)
                meet(sp, "sp")
                if l < DEPTH - 1:
                    numbers = [s_.num for (k_, _), s_ in SEMS.items() if k_ is None]
                    sp.sem_clear(range(min(numbers), max(numbers) + 1)).then_inc(cleared, 1)

        @block.gpsimd
        def _(pool):
            link = chain(pool, "pool", pool_step)
            link(pool.memset(ones[:, :], 1.0))
            link(pool.memset(neghalf, -0.5))
            link(pool.memset(lnscale, math.log(RD ** -0.5)))
            link(pool.memset(assign, NO_ROW))
            for l in range(DEPTH):
                pool.dma_start(tok_d[l].rearrange("(p b) a -> p (b a)", p=P), assign)\
                    .then_inc(tok_zero, 16)
            pool.wait_ge(tok_zero, 32)

            for l in range(DEPTH):
                pool.wait_ge(S(l, "ms_ready"), 1)
                pool.tensor_tensor(rstd[:, 0:NT], msq[:, 0:NT], neghalf[:, 0:NT], ALU.pow)\
                    .then_inc(S(l, "rstd_ready"), 1)
                n = 0
                for u in proj_units(l):
                    if KIND[u[0]] == "norm":
                        b = n % 2
                        n += 1
                        pool.wait_ge(S(l, "qk_ms_ready"), n)
                        pool.tensor_tensor(qk_rs[:, b * NAH:(b + 1) * NAH], qk_ms[:, b * NAH:(b + 1) * NAH],
                                           neghalf[:, 0:NAH], ALU.pow).then_inc(S(l, "qk_rs_ready"), 1)
                pool.wait_ge(S(l, "mask_in"), 16)
                for what, heads in (("bias_in0", (5, 6)), ("bias_in1", range(5)), ("bias_in2", (7,))):
                    pool.wait_ge(S(l, what), 16 * len(heads))
                    for h in heads:
                        pool.tensor_tensor(bias[h], bias[h], mask, ALU.add).then_inc(S(l, "bias_ready"), 1)
                meet(pool, "pool")
                meet(pool, "pool")
                for g in range(len(ret_groups(l))):
                    pool.wait_ge(S(l, "hvar_ready"), g + 1)
                    pool.tensor_tensor(hrstd, hvar, neghalf[:, 0:8], ALU.pow).then_inc(S(l, "hrstd_ready"), 1)
                meet(pool, "pool")
                for t in range(tiles(l)):
                    pool.wait_ge(S(l, "g_ms"), t + 1)
                    pool.tensor_tensor(rstd[:, t:t + 1], msq[:, t:t + 1], neghalf[:, 0:1], ALU.pow)\
                        .then_inc(S(l, "g_rs"), 1)
                pool.wait_ge(S(l, "route_ready"), 1)
                for t in range(tiles(l)):
                    for k in range(2):
                        pool.indirect_dma_start(
                            tok_d[l], bass.IndirectOffsetOnAxis(ap=ints[:, 128 + 2 * t + k:129 + 2 * t + k], axis=0),
                            ints[:, 64 + 2 * t + k:65 + 2 * t + k], None).then_inc(S(l, "tok_out"), 16)
                meet(pool, "pool")

                for s in range(2):
                    link(pool.memset(xg[s], 0.0))

                def gather(s, column, cp_count):
                    pool.tensor_copy(idx_slot[s][:, :], token[:, column]).then_inc(S(l, f"idx_cp{s}"), 1)
                    pool.wait_ge(S(l, f"idx_cp{s}"), cp_count)
                    pool.sem_inc(pool_passed, 1)
                    pool.indirect_dma_start(xg[s], None, h_d, bass.IndirectOffsetOnAxis(ap=idx_slot[s][:, :], axis=0),
                                            bounds_check=TOK - 1, oob_is_err=False)\
                        .then_inc(S(l, f"xg_in{s}"), 16)

                n_pairs = pool.value_load(ints[0:1, 79:80], min_val=NE // 2, max_val=NBLK // 2 - 1)
                gather(0, slice(0, 1), 1)
                gather(1, slice(1, 2), 1)

                def store(b):
                    pool.tensor_copy(y_idx, y_place[:, bass.ds(b, 1)]).then_inc(S(l, "y_idx_cp"), 1)
                    pool.wait_ge(S(l, "y_idx_cp"), b + 1)
                    pool.wait_ge(S(l, "y_copied"), 2 * b + 2)
                    pool.sem_inc(pool_passed, 1)
                    pool.indirect_dma_start(y_d, bass.IndirectOffsetOnAxis(ap=y_idx, axis=0), yb, None,
                                            bounds_check=2 * TOK - 1, oob_is_err=False)\
                        .then_inc(S(l, "y_out"), 16)
                    pool.wait_ge(S(l, "y_out"), 16 * b + 16)
                    pool.sem_inc(S(l, "yb_free"), 1)

                pool.sem_inc(S(l, "yb_free"), 1)
                with pool.Fori(0, n_pairs) as i:
                    for s in range(2):
                        b = 2 * i + s
                        pool.wait_ge(S(l, f"xg_used{s}"), i + 1)
                        gather(s, bass.ds(b + 2, 1), i + 2)
                        store(b)
                store(2 * n_pairs)
                for s in range(2):
                    pool.wait_ge(S(l, f"xg_in{s}"), 16 * n_pairs + 16)
                pool.sem_inc(pool_passed, 1)
                meet(pool, "pool")
                meet(pool, "pool")
                if l < DEPTH - 1:
                    pool.wait_ge(cleared, 1)
                    pool.drain()

        @block.tensor
        def _(pe):
            for l in range(DEPTH):
                def ada_piece(p):
                    ll, r, k = ada_pieces(l)[p]
                    q = p // KD
                    if k == 0 and q >= 2:
                        pe.wait_ge(S(l, "mod_rows"), q - 1)
                    pe.wait_ge(S(l, f"ada_in{p % 2}"), 16 * (p // 2 + 1))
                    for j in range(4):
                        mm = pe.matmul(PS[6 + q % 2][32 * j:32 * j + 32, :], sc32[:, k, :], ada_w[p % 2][:, j, :],
                                       start=(k == 0), stop=(k == KD - 1), skip_group_check=True)
                    mm.then_inc(S(l, "ada_done"), 1)

                if l == 0:
                    pe.wait_ge(sc_ready, 1)
                for p in range(ada_start(l)):
                    ada_piece(p)
                if l == 0:
                    pe.wait_ge(const_in, 16 * N_CONST)

                def rows_to_T(t, row, banks, done, evac):
                    for half in range(2):
                        u = 2 * t + half
                        if u >= len(banks):
                            pe.wait_ge(evac, u - len(banks) + 1)
                        for i in range(4):
                            c = (half * 4 + i) * P
                            mm = pe.transpose(PS[banks[u % len(banks)]][:, i * P:(i + 1) * P], row[:, c:c + P],
                                              ident[:, :])
                        mm.then_inc(done, 1)

                def turn_h(t):
                    pe.wait_ge(S(l, "hrow_ready"), t + 1)
                    rows_to_T(t, hrow1[t % 2], [6, 7], S(l, "tr_done"), S(l, "hT_ready"))

                units = proj_units(l)
                n_act, n_dve, n_row = (counted(units, f) for f in (act_reads, dve_reads, needs_row))

                n_c0 = sum(c == 0 for c, _ in units)

                def turn(n):
                    if not needs_row(units[n]):
                        return
                    m = n_row[n] - 1
                    pe.wait_ge(S(l, "row_ready"), m + 1)
                    if m >= 2:
                        pe.wait_ge(S(l, "trow_evac"), m - 1)
                    for i in range(4):
                        mm = pe.transpose(PS[4 + m % 2][:, i * P:(i + 1) * P], rowbuf[m % 2][:, i * P:(i + 1) * P],
                                          ident[:, :])
                    mm.then_inc(S(l, "trow_done"), 1)

                turn_h(0)
                turn_h(1)
                seen = -1
                for n, (c, t) in enumerate(units):
                    if c != seen:
                        pe.wait_ge(S(l, f"win{c % 2}"), 16 * (c // 2 + 1))
                        seen = c
                    if c == 0:
                        pe.wait_ge(S(l, "hT_ready"), 2 * t + 2)
                    elif n == n_c0:
                        pe.wait_ge(S(l, "hT_ready"), 2 * NT)
                    if n >= 4:
                        if n_act[n - 4]:
                            pe.wait_ge(S(l, "act_rel"), n_act[n - 4])
                        if n_dve[n - 4]:
                            pe.wait_ge(S(l, "gate_rel"), n_dve[n - 4])
                    for k in range(KD):
                        mm = pe.matmul(PS[n % 4][:, :], hT[:, k, t * P:(t + 1) * P], win[c % 2][:, k, :],
                                       start=(k == 0), stop=(k == KD - 1))
                    mm.then_inc(S(l, "proj_done"), 1)
                    if n >= 2:
                        turn(n - 2)
                    if n + 2 < NT:
                        turn_h(n + 2)
                    if after_unit(l, n) is not None:
                        ada_piece(after_unit(l, n))
                turn(len(units) - 2)
                turn(len(units) - 1)
                meet(pe, "pe")

                nu = na_units(l)
                pe.wait_ge(S(l, "vshift"), 32)

                def scores(n):
                    j, h, ranges, _, _ = nu[n]
                    hp = slice((h % 2) * 64, (h % 2) * 64 + 64)
                    if n >= 3:
                        pe.wait_ge(S(l, "p_ready"), n - 2)
                    o = 0
                    for k0, kn in ranges:
                        mm = pe.matmul(PS[n % 3][:, o:o + kn], qaT[hp, h // 2, j * P:(j + 1) * P],
                                       kaT[hp, h // 2, k0:k0 + kn], start=True, stop=True)
                        o += kn
                    mm.then_inc(S(l, "s_done"), 1)

                def turn_p(n):
                    tiles_ = nu[n][3]
                    pe.wait_ge(S(l, "p_ready"), n + 1)
                    if n >= 2:
                        pe.wait_ge(S(l, "pt_evac"), n - 1)
                    for i in range(len(tiles_)):
                        mm = pe.transpose(PS[3 + n % 2][:, i * P:(i + 1) * P], pexp[n % 2][:, i * P:(i + 1) * P],
                                          ident[:, :])
                    mm.then_inc(S(l, "pt_done"), 1)

                def values(n):
                    j, h, _, tiles_, _ = nu[n]
                    pe.wait_ge(S(l, "pt_evac"), n + 1)
                    if h == 0 and j >= 2:
                        pe.wait_ge(S(l, "o_norm"), j - 1)
                    for i, vt in enumerate(tiles_):
                        mm = pe.matmul(PS[5 + j % 2][:, h * NAD:(h + 1) * NAD], pT[n % 2][:, i, :],
                                       va[:, vt, h * NAD:(h + 1) * NAD], start=(i == 0), stop=(i == len(tiles_) - 1))
                    mm.then_inc(S(l, "pv_done"), 1)

                for n in range(len(nu) + 2):
                    if n < len(nu):
                        scores(n)
                    if 1 <= n <= len(nu):
                        turn_p(n - 1)
                    if n >= 2:
                        values(n - 2)
                meet(pe, "pe")

                steps_r = ret_steps(l)

                def ret_scores(m):
                    g, a, r, qts, kt, _ = steps_r[m]
                    w = len(qts) * P
                    if m >= 2:
                        pe.wait_ge(S(l, "w_mult"), 2 * (m - 1))
                    pe.matmul(PS[m % 2][:, 0:w], kbT[:, r, kt * P:(kt + 1) * P],
                              qbT[:, r, qts[0] * P:qts[0] * P + w], start=True, stop=True)\
                        .then_inc(S(l, "st_done"), 1)

                ret_scores(0)
                for m, (g, a, r, qts, kt, end) in enumerate(steps_r):
                    if m + 1 < len(steps_r):
                        ret_scores(m + 1)
                    pe.wait_ge(S(l, "w_mult"), 2 * m + 2)
                    if a == 0 and g >= 2:
                        pe.wait_ge(S(l, "ret_norm"), g - 1)
                    for d in range(2):
                        for i in range(len(qts)):
                            mm = pe.matmul(PS[2 + 2 * d + g % 2][:, i * P:(i + 1) * P],
                                           Wd[m % 3][:, d, i * P:(i + 1) * P], vb[:, kt, r * RD:(r + 1) * RD],
                                           start=(a == 0 and i == 0), stop=end, skip_group_check=True)
                    mm.then_inc(S(l, "w_used_r"), 1)
                meet(pe, "pe")

                nt = tiles(l)

                def router(t):
                    pe.wait_ge(S(l, "g_row"), t + 1)
                    rows_to_T(t, hrow2[t], [4, 5], S(l, "g_tr"), S(l, "g_hT"))
                    pe.wait_ge(S(l, "g_hT"), 2 * t + 2)
                    for k in range(KD):
                        mm = pe.matmul(PS[6][:, t * NE:(t + 1) * NE], hT[:, k, t * P:(t + 1) * P], rw[:, k, :],
                                       start=(k == 0), stop=(k == KD - 1))
                    mm.then_inc(S(l, "logit_done"), 1)

                for t in range(nt):
                    rows_to_T(t, mix[:, t, :], [4, 5, 6, 7], S(l, "mt_done"), S(l, "mt_evac"))
                pe.wait_ge(S(l, "mt_evac"), 2 * nt)
                for c, w in enumerate((wo0, wo1)):
                    pe.wait_ge(S(l, f"wo_in{c}"), 16)
                    for t in range(nt):
                        n = c * nt + t
                        if n >= 4:
                            pe.wait_ge(S(l, "x_upd"), n - 3)
                        for k in range(KD):
                            mm = pe.matmul(PS[n % 4][:, :], mixT[:, k, t * P:(t + 1) * P], w[:, k, :],
                                           start=(k == 0), stop=(k == KD - 1))
                        mm.then_inc(S(l, "op_done"), 1)
                        if c == 1 and t >= 2:
                            router(t - 2)
                router(nt - 2)
                router(nt - 1)
                pe.wait_ge(S(l, "m_ready"), 1)
                for t in range(nt + 1):
                    for t2 in range(min(t, nt - 1) + 1):
                        w = upper if t2 == t else ones
                        mm = pe.matmul(PS[7][:, t * NE:(t + 1) * NE], w[:, :], route_t["M"][:, t2, :],
                                       start=(t2 == 0), stop=(t2 == min(t, nt - 1)))
                mm.then_inc(S(l, "rank_done"), 1)
                meet(pe, "pe")

                pe.wait_ge(S(l, "route_ready"), 1)

                def turn_x(s, half):
                    for i in range(4):
                        c = (half * 4 + i) * P
                        mm = pe.transpose(PS[half][:, i * P:(i + 1) * P], xg[s][:, c:c + P], ident[:, :])
                    return mm

                def unit(b, u, hi, lo, banks, start, stop):
                    pe.wait_ge(S(l, "whi_ready"), b * UNITS + u + 1)
                    for i, (x, w) in enumerate(((hi, w_hi), (lo, w_hi), (hi, w_lo))):
                        if i == 2:
                            pe.wait_ge(S(l, "wlo_ready"), b * UNITS + u + 1)
                        for k in range(2):
                            one = banks[0] is banks[1]
                            mm = pe.matmul(banks[k][:, :], x[k], w[u % 3][:, k, :],
                                           start=start and i == 0 and (k == 0 or not one),
                                           stop=stop and i == 2 and (k == 1 or not one))
                    mm.then_inc(S(l, "w_used"), 1)

                pe.wait_ge(S(l, "xg_in0"), 16)
                turn_x(0, 0).then_inc(S(l, "xt_done"), 1)
                turn_x(0, 1).then_inc(S(l, "xg_used0"), 1)
                n_pairs = pe.value_load(ints[0:1, 79:80], min_val=NE // 2, max_val=NBLK // 2 - 1)
                with pe.Fori(0, n_pairs) as i:
                    for s in range(2):
                        o = 1 - s
                        b = 2 * i + s
                        pe.wait_ge(S(l, "xhi_ready"), 2 * b + 2)
                        pe.wait_ge(S(l, "xlo_ready"), 2 * b + 2)
                        for u in range(8):
                            bank = PS[2 + u // 4]
                            k = 2 * (u % 4)
                            unit(b, u, [x_hi[:, k + q, :] for q in range(2)], [x_lo[:, k + q, :] for q in range(2)],
                                 [bank, bank], u % 4 == 0, u % 4 == 3)
                        pe.wait_ge(S(l, f"xg_in{o}"), 16 * i + 16 + 16 * s)
                        turn_x(o, 0).then_inc(S(l, "xt_done"), 1)
                        pe.wait_ge(S(l, "a_ready"), b + 1)
                        for f in range(4):
                            mm = pe.transpose(PS[4][:, f * P:(f + 1) * P], act[:, f * P:(f + 1) * P], ident[:, :])
                        mm.then_inc(S(l, "at_done"), 1)
                        turn_x(o, 1).then_inc(S(l, f"xg_used{o}"), 1)
                        pe.wait_ge(S(l, "ahi_ready"), b + 1)
                        pe.wait_ge(S(l, "alo_ready"), b + 1)
                        pe.wait_ge(S(l, "y_copied"), 2 * b + 2)
                        for f in range(4):
                            unit(b, 8 + f, [a_hi[:, f, :]] * 2, [a_lo[:, f, :]] * 2, [PS[5], PS[6]], f == 0, f == 3)
                meet(pe, "pe")
                meet(pe, "pe")
                if l < DEPTH - 1:
                    pe.wait_ge(cleared, 1)
                    pe.drain()

        @block.scalar
        def _(act_e):
            link = chain(act_e, "act", act_step)
            act_e.wait_ge(cc_in, 16)
            act_e.activation(cth, cc, ACT.Tanh, scale=0.5).then_inc(sc_tanh, 1)
            act_e.wait_ge(const_in, 16 * N_CONST)
            act_e.activation(decay, decay, ACT.Exp).then_inc(decay_exp, 1)
            act_e.wait_ge(x_in, 16 * NT)
            for l in range(DEPTH):
                for t in range(NT):
                    if t >= 2:
                        act_e.wait_ge(S(l, "ss_done"), t - 1)
                    act_e.activation(junk[t % 2], X[:, t, :], ACT.Square, accum_out=ss[:, t:t + 1])\
                        .then_inc(S(l, "ss_done"), 1)
                def evac_h(t):
                    for half in range(2):
                        u = 2 * t + half
                        act_e.wait_ge(S(l, "tr_done"), u + 1)
                        act_e.activation(hT[:, 4 * half:4 * half + 4, t * P:(t + 1) * P],
                                         PS[6 + half][:, :].rearrange("p (a b) -> p a b", a=4), ACT.Copy)\
                            .then_inc(S(l, "hT_ready"), 1)

                units = proj_units(l)
                n_row = counted(units, needs_row)
                n_norm = counted(units, lambda u: KIND[u[0]] == "norm")

                def evac_row(n):
                    if n < 0 or not needs_row(units[n]):
                        return
                    c, t = units[n]
                    m = n_row[n] - 1
                    dst = {0: qaT, 1: kaT, 3: qbT, 4: kbT}[c]
                    act_e.wait_ge(S(l, "trow_done"), m + 1)
                    act_e.activation(dst[:, :, t * P:(t + 1) * P],
                                     PS[4 + m % 2][:, :].rearrange("p (a b) -> p a b", a=4), ACT.Copy)\
                        .then_inc(S(l, "trow_evac"), 1)

                evac_h(0)
                evac_h(1)
                for n in range(len(units) + 2):
                    if n < len(units):
                        c, t = units[n]
                        kind = KIND[c]
                        if kind == "gate" and KIND[units[n - 1][0]] != "gate":
                            act_e.wait_ge(S(l, "ada_done"), len(ada_pieces(l)))
                            act_e.wait_ge(S(l, "mod_out"), 16 * (len(ada_pieces(l)) // KD))
                        if act_reads(units[n]):
                            act_e.wait_ge(S(l, "proj_done"), n + 1)
                        if kind == "norm":
                            m = n_norm[n] - 1
                            if m >= 2:
                                act_e.wait_ge(S(l, "qk_ms_ready"), m - 1)
                            act_e.activation(sqbuf[m % 2], PS[n % 4][:, :], ACT.Square).then_inc(S(l, "act_rel"), 1)
                        elif kind == "v":
                            act_e.activation({2: va, 5: vb}[c][:, t, :], PS[n % 4][:, :], ACT.Copy)\
                                .then_inc(S(l, "act_rel"), 1)
                        elif kind == "gate":
                            act_e.activation({6: gf, 7: gb}[c][:, t, :], PS[n % 4][:, :], ACT.Tanh, scale=0.5)\
                                .then_inc(S(l, "act_rel"), 1)
                    evac_row(n - 2)
                    if n + 2 < NT:
                        evac_h(n + 2)
                meet(act_e, "act_e")

                nu = na_units(l)

                def evac_p(n):
                    w = len(nu[n][3])
                    act_e.wait_ge(S(l, "pt_done"), n + 1)
                    if n >= 2:
                        act_e.wait_ge(S(l, "pv_done"), n - 1)
                    act_e.activation(pT[n % 2][:, 0:w, :],
                                     PS[3 + n % 2][:, 0:w * P].rearrange("p (a b) -> p a b", a=w), ACT.Copy)\
                        .then_inc(S(l, "pt_evac"), 1)

                for n in range(len(nu) + 1):
                    if n < len(nu):
                        j, h, ranges, _, _ = nu[n]
                        w = sum(k for _, k in ranges)
                        act_e.wait_ge(S(l, "nm_ready"), n + 1)
                        if n >= 2:
                            act_e.wait_ge(S(l, "pt_done"), n - 1)
                        act_e.activation(pexp[n % 2][:, 0:w], PS[n % 3][:, 0:w], ACT.Exp,
                                         bias=negmax[:, n % 4:n % 4 + 1],
                                         accum_out=rsum[:, j * NAH + h:j * NAH + h + 1])\
                            .then_inc(S(l, "p_ready"), 1)
                    if n >= 1:
                        evac_p(n - 1)
                meet(act_e, "act_e")

                act_e.wait_ge(S(l, "delta_in"), 16)
                act_e.wait_ge(S(l, "lg_ready"), 1)
                for m, (g, a, r, qts, _, _) in enumerate(ret_steps(l)):
                    w = len(qts) * P
                    if m == 3:
                        act_e.wait_ge(S(l, "delta_in2"), 32)
                    for d in range(2):
                        if m >= 2:
                            act_e.wait_ge(S(l, "w_mult"), 2 * m + d - 3)
                        src = delta[a // 3][:, a % 3, d, :] if qts[0] == 0 else dctx[:, d, a, :]
                        lg = decay[:, (l * 2 + d) * RH + r:(l * 2 + d) * RH + r + 1]
                        act_e.activation(dec[(2 * m + d) % 4][:, 0:w], src, ACT.Exp, bias=lnscale, scale=lg)\
                            .then_inc(S(l, "dec_ready"), 1)
                meet(act_e, "act_e")

                nt = tiles(l)
                for u in range(2 * nt):
                    t, half = divmod(u, 2)
                    act_e.wait_ge(S(l, "mt_done"), u + 1)
                    act_e.activation(mixT[:, 4 * half:4 * half + 4, t * P:(t + 1) * P],
                                     PS[4 + u % 4][:, :].rearrange("p (a b) -> p a b", a=4), ACT.Copy)\
                        .then_inc(S(l, "mt_evac"), 1)

                for n in range(nt + 2):
                    if n >= 2:
                        t = n - 2
                        for half in range(2):
                            act_e.wait_ge(S(l, "g_tr"), 2 * t + half + 1)
                            act_e.activation(hT[:, 4 * half:4 * half + 4, t * P:(t + 1) * P],
                                             PS[4 + half][:, :].rearrange("p (a b) -> p a b", a=4), ACT.Copy)\
                                .then_inc(S(l, "g_hT"), 1)
                    if n < nt:
                        act_e.wait_ge(S(l, "x_upd"), nt + n + 1)
                        if n >= 2:
                            act_e.wait_ge(S(l, "g_ss"), n - 1)
                        act_e.activation(junk2[n % 2], X[:, n, :], ACT.Square, accum_out=ss[:, n:n + 1])\
                            .then_inc(S(l, "g_ss"), 1)
                act_e.wait_ge(S(l, "logit_done"), nt)
                act_e.activation(route_t["score"][:, 0:nt, :].rearrange("p a b -> p (a b)"), PS[6][:, 0:nt * NE], ACT.Exp, scale=-1.0)\
                    .then_inc(S(l, "exp_done"), 1)
                meet(act_e, "act_e")

                act_e.wait_ge(S(l, "route_ready"), 1)

                def evac_x(half):
                    act_e.activation(x_hi[:, 4 * half:4 * half + 4, :],
                                     PS[half][:, :].rearrange("p (a b) -> p a b", a=4), ACT.Copy)\
                        .then_inc(S(l, "xhi_ready"), 1)

                act_e.wait_ge(S(l, "xt_done"), 1)
                evac_x(0)
                act_e.wait_ge(S(l, "xg_used0"), 1)
                evac_x(1)
                def evac_y(b):
                    act_e.wait_ge(S(l, "yb_free"), b + 1)
                    for c in range(2):
                        act_e.activation(yb[:, c * CH:(c + 1) * CH], PS[5 + c][:, :], ACT.Copy)\
                            .then_inc(S(l, "y_copied"), 1)

                act_e.sem_inc(S(l, "w_used"), 3)
                n_pairs = act_e.value_load(ints[0:1, 79:80], min_val=NE // 2, max_val=NBLK // 2 - 1)
                with act_e.Fori(0, n_pairs) as i:
                    for s in range(2):
                        o = 1 - s
                        b = 2 * i + s

                        def high(u):
                            if u % 4 == 0:
                                act_e.wait_ge(S(l, ("wg_in", "wu_in", "wd_in")[u // 4] + str(s)), 16 * i + 16)
                            act_e.wait_ge(S(l, "w_used"), b * UNITS + u + 1)
                            act_e.activation(w_hi[u % 3][:, :, :], raw(s, u), ACT.Copy).then_inc(S(l, "whi_ready"), 1)

                        for u in range(3):
                            high(u)
                        evac_y(b)
                        for u in range(3, 7):
                            high(u)
                        act_e.wait_ge(S(l, "w_used"), b * UNITS + 4 + 3)
                        act_e.activation(th, PS[2][:, :], ACT.Tanh, scale=0.5).then_inc(S(l, "th_ready"), 1)
                        for u in range(7, 10):
                            high(u)
                        act_e.wait_ge(S(l, "xt_done"), b + 2)
                        evac_x(0)
                        act_e.wait_ge(S(l, "at_done"), b + 1)
                        act_e.activation(a_hi[:, :, :], PS[4][:, :].rearrange("p (a b) -> p a b", a=4), ACT.Copy)\
                            .then_inc(S(l, "ahi_ready"), 1)
                        act_e.wait_ge(S(l, f"xg_used{o}"), i + 1 + s)
                        evac_x(1)
                        high(10)
                        high(11)
                act_e.wait_ge(S(l, "w_used"), 2 * n_pairs * UNITS + 3)
                evac_y(2 * n_pairs)
                meet(act_e, "act_e")
                act_e.wait_ge(S(l, "y_in0"), 32)
                for t in range(nt):
                    act_e.wait_ge(S(l, f"y_in{t}"), 32)
                    if t >= 2:
                        act_e.wait_ge(S(l, "comb_done"), t - 1)
                    act_e.activation(z[t % 2], y1[t], ACT.Copy, scale=wgt[:, 2 * t:2 * t + 1])\
                        .then_inc(S(l, "z_first"), 1)
                meet(act_e, "act_e")
                if l < DEPTH - 1:
                    act_e.wait_ge(cleared, 1)
                    act_e.drain()

        @block.vector
        def _(dve):
            link = chain(dve, "dve", dve_step)
            def route(l):
                T = tiles(l)
                v = {n: (a[:, 0:T, :] if a.shape[1] == NT and len(a.shape) == 3 else
                         a[:, 0:T * NG, :] if n == "pairs" else a[:, 0:T] if a.shape[1] == NT else a)
                     for n, a in route_t.items()}

                def tt(out, a, b, op):
                    link(dve.tensor_tensor(out, a, b, op))

                def ts(out, a, x, op, y=None, op2=None):
                    link(dve.tensor_scalar(out, a, x, y, op, op2) if op2 is not None
                         else dve.tensor_scalar(out, a, x, None, op))

                def red(out, a, op):
                    link(dve.tensor_reduce(out, a, AX.X, op))

                def over(a, n):
                    return a.unsqueeze(2).broadcast_to([P, T, n])

                def per_token(a, n):
                    return a.unsqueeze(1).broadcast_to([P, T, n])

                dve.wait_ge(S(l, "exp_done"), 1)
                ts(v["score"], v["score"], 1.0, ALU.add)
                link(dve.reciprocal(v["score"], v["score"]))
                tt(v["ssel"], v["score"], per_token(rbias, NE), ALU.add)
                s4 = v["ssel"].rearrange("p t (g e) -> p (t g) e", e=EPG)
                o = 0
                for dist in range(1, EPG):
                    tt(v["pairs"][:, :, o:o + EPG - dist], s4[:, :, 0:EPG - dist], s4[:, :, dist:EPG], ALU.add)
                    o += EPG - dist
                red(v["gsum"].rearrange("p t g -> p (t g)"), v["pairs"], ALU.max)
                red(v["gmax"], v["gsum"], ALU.max)
                tt(v["gcand"], v["gsum"], over(v["gmax"], NG), ALU.is_equal)
                tt(v["gcand"], v["gcand"], per_token(rev8, NG), ALU.mult)
                red(v["gfirst"], v["gcand"], ALU.max)
                tt(v["ing"], per_token(rev8, NG), over(v["gfirst"], NG), ALU.is_equal)
                ts(v["pen"], v["ing"], BIG, ALU.mult, -BIG, ALU.add)
                tt(v["ms"].rearrange("p t (g e) -> p (t g) e", e=EPG), s4,
                   v["pen"].rearrange("p t g -> p (t g)").unsqueeze(2).broadcast_to([P, T * NG, EPG]), ALU.add)
                for k in range(2):
                    oh, first = v[f"oh{k}"], v[f"first{k}"]
                    red(v["top"], v["ms"], ALU.max)
                    tt(v["cand"], v["ms"], over(v["top"], NE), ALU.is_equal)
                    tt(v["cand"], v["cand"], per_token(rev32, NE), ALU.mult)
                    red(first, v["cand"], ALU.max)
                    tt(oh, per_token(rev32, NE), over(first, NE), ALU.is_equal)
                    if k == 0:
                        link(dve.scalar_tensor_tensor(v["ms"], oh, -BIG, v["ms"], ALU.mult, ALU.add))
                dve.tensor_tensor(v["M"], v["oh0"], v["oh1"], ALU.add).then_inc(S(l, "m_ready"), 1)
                for k in range(2):
                    tt(v["tmp"], v["score"], v[f"oh{k}"], ALU.mult)
                    red(v[f"s{k}"], v["tmp"], ALU.add)
                tt(v["top"], v["s0"], v["s1"], ALU.add)
                link(dve.reciprocal(v["top"], v["top"]))
                for k in range(2):
                    tt(wgt.rearrange("p (t k) -> p t k", k=2)[:, 0:T, k], v[f"s{k}"], v["top"], ALU.mult)

                dve.wait_ge(S(l, "rank_done"), 1)
                count = PS[7][:, T * NE:(T + 1) * NE]
                link(dve.memset(v["zero"], 0.0))
                ts(v["extra"], count, float(P), ALU.is_gt)
                for m in range(2, T):
                    link(dve.scalar_tensor_tensor(v["extra"], count, float(m * P), v["extra"], ALU.is_gt, ALU.add))
                link(dve.tensor_tensor_scan(v["ovinc"], v["extra"], v["zero"], 0.0, ALU.add, ALU.add))
                tt(v["ovb"], v["ovinc"], v["extra"], ALU.subtract)
                tt(v["ovcmp"], v["ovinc"].unsqueeze(1).broadcast_to([P, NOV, NE]),
                   ovidx.unsqueeze(2).broadcast_to([P, NOV, NE]), ALU.is_le)
                red(v["ovexp"], v["ovcmp"], ALU.add)
                ts(ints[:, NE:NBLK], v["ovexp"], float(NE - 1), ALU.min)
                nov = v["ovinc"][:, NE - 1:NE]
                ts(v["npair"], nov, 0.0, ALU.is_gt, float(NE // 2), ALU.add)
                for m in range(1, NOV // 2 - 1):
                    link(dve.scalar_tensor_tensor(v["npair"], nov, 2.0 * m, v["npair"], ALU.is_gt, ALU.add))
                link(dve.tensor_copy(ints[:, 79:80], v["npair"]))

                ranks = PS[7][:, 0:T * NE].rearrange("p (t e) -> p t e", e=NE)
                for k in range(2):
                    tt(v["tmp"], v[f"oh{k}"], ranks, ALU.mult)
                    red(v["rank"], v["tmp"], ALU.add)
                    tt(v["tmp"], v[f"oh{k}"], per_token(v["ovb"], NE), ALU.mult)
                    red(v["ov"], v["tmp"], ALU.add)
                    ts(v["q"], v["rank"], float(P), ALU.is_ge)
                    for m in range(2, T):
                        link(dve.scalar_tensor_tensor(v["q"], v["rank"], float(m * P), v["q"], ALU.is_ge, ALU.add))
                    link(dve.scalar_tensor_tensor(v["r"], v["q"], -float(P), v["rank"], ALU.mult, ALU.add))
                    ts(v["pos"], v["q"], 0.0, ALU.is_gt)
                    ts(v["e"], v[f"first{k}"], -1.0, ALU.mult, float(NE), ALU.add)
                    tt(v["blk"], v["ov"], v["q"], ALU.add)
                    ts(v["blk"], v["blk"], float(NE - 1), ALU.add)
                    tt(v["blk"], v["blk"], v["e"], ALU.subtract)
                    tt(v["blk"], v["blk"], v["pos"], ALU.mult)
                    tt(v["blk"], v["blk"], v["e"], ALU.add)
                    i = dve.scalar_tensor_tensor(
                        ints[:, 128:128 + 2 * NT].rearrange("p (t k) -> p t k", k=2)[:, 0:T, k],
                        v["r"], float(NBLK), v["blk"], ALU.mult, ALU.add)
                    if k == 0:
                        link(i)
                i.then_inc(S(l, "route_ready"), 1)

            dve.wait_ge(cc_in, 16)
            link(dve.memset(sc32[:, :, :], 0.0))
            dve.wait_ge(sc_tanh, 1)
            link(dve.scalar_tensor_tensor(cth, cth, 1.0, cc, ALU.add, ALU.mult))
            dve.tensor_scalar(sc32[:, :, 0:2], cth.rearrange("p (k i) -> p k i", i=2), 0.5, None, ALU.mult)\
                .then_inc(sc_ready, 1)
            dve.wait_ge(S(0, "rows_in"), 16)
            dve.wait_ge(S(0, "ada_done"), KD)
            dve.tensor_tensor(rows[:, 0, :], PS[6][:, :], rows[:, 0, :], ALU.add).then_inc(S(0, "mod_rows"), 1)
            dve.wait_ge(const_in, 16 * N_CONST)
            dve.wait_ge(decay_exp, 1)
            dve.tensor_scalar(decay, decay, -1.0, None, ALU.mult).then_inc(S(0, "lg_ready"), 1)
            link(dve.tensor_scalar(nag[:, 0:2, :], nag[:, 0:2, :], NAD ** -0.5, None, ALU.mult))

            for l in range(DEPTH):
                if l:
                    dve.memset(msq[:, :], 1.0).then_inc(S(l, "lg_ready"), 1)
                if l == 0:
                    dve.wait_ge(S(l, "modb_in"), 80)
                for n in (0, 2):
                    link(dve.scalar_tensor_tensor(bc[n][:, :], bc[n][:, :], 1.0, normw, ALU.add, ALU.mult))
                dve.wait_ge(S(l, "ss_done"), NT)
                dve.tensor_scalar(msq[:, 0:NT], ss[:, 0:NT], 1.0 / D, EPS, ALU.mult, ALU.add)\
                    .then_inc(S(l, "ms_ready"), 1)
                dve.wait_ge(S(l, "rstd_ready"), 1)
                for t in range(NT):
                    a, b = (0, 1) if t < LAT else (2, 3)
                    if t >= 2:
                        dve.wait_ge(S(l, "tr_done"), 2 * (t - 1))
                    link(dve.scalar_tensor_tensor(hrow1[t % 2], X[:, t, :], rstd[:, t:t + 1], bc[a][:, :],
                                                  ALU.mult, ALU.mult))
                    dve.tensor_tensor(hrow1[t % 2], hrow1[t % 2], bc[b][:, :], ALU.add)\
                        .then_inc(S(l, "hrow_ready"), 1)

                units = proj_units(l)
                n_act, n_row = counted(units, act_reads), counted(units, needs_row)
                n_norm = counted(units, lambda u: KIND[u[0]] == "norm")

                def row_free(n):
                    m = n_row[n] - 1
                    if m >= 2:
                        dve.wait_ge(S(l, "trow_done"), m - 1)
                    return rowbuf[m % 2]

                def norm_front(n):
                    b = (n_norm[n] - 1) % 2
                    o = slice(b * NAH, (b + 1) * NAH)
                    dve.wait_ge(S(l, "act_rel"), n_act[n])
                    link(dve.tensor_reduce(qk_ss[:, o], sqbuf[b].rearrange("p (h d) -> p h d", h=NAH), AX.X, ALU.add))
                    dve.tensor_scalar(qk_ms[:, o], qk_ss[:, o], 1.0 / NAD, EPS, ALU.mult, ALU.add)\
                        .then_inc(S(l, "qk_ms_ready"), 1)

                def norm_back(n):
                    c = units[n][0]
                    b = (n_norm[n] - 1) % 2
                    row = row_free(n).rearrange("p (h d) -> p h d", h=NAH)
                    dve.wait_ge(S(l, "qk_rs_ready"), n_norm[n])
                    link(dve.tensor_tensor(row, PS[n % 4][:, :].rearrange("p (h d) -> p h d", h=NAH),
                                           qk_rs[:, b * NAH:(b + 1) * NAH].unsqueeze(2)
                                           .broadcast_to([P, NAH, NAD]), ALU.mult))
                    dve.tensor_tensor(row, row, nag[:, 2 * c + l:2 * c + l + 1, :].broadcast_to([P, NAH, NAD]),
                                      ALU.mult).then_inc(S(l, "row_ready"), 1)

                def rope(n):
                    t = units[n][1]
                    row = row_free(n)
                    dve.wait_ge(S(l, "proj_done"), n + 1)
                    if t >= LAT:
                        dve.tensor_copy(row, PS[n % 4][:, :]).then_inc(S(l, "row_ready"), 1)
                        return
                    v = PS[n % 4][:, :].rearrange("p (h a b) -> p h a b", a=4, b=32)
                    q = sqbuf[n % 2].rearrange("p (h a b) -> p h a b", a=4, b=32)
                    link(dve.tensor_tensor(row.rearrange("p (h d) -> p h d", h=RH),
                                           PS[n % 4][:, :].rearrange("p (h d) -> p h d", h=RH),
                                           cosF[:, t:t + 1, :].broadcast_to([P, RH, RD]), ALU.mult))
                    sn = sinF[:, t, :].rearrange("p (a b) -> p a b", a=2)
                    for ax in range(2):
                        s2 = sn[:, ax:ax + 1, :].broadcast_to([P, RH, 32])
                        link(dve.tensor_tensor(q[:, :, 2 * ax, :], v[:, :, 2 * ax + 1, :], s2, ALU.mult))
                        link(dve.tensor_tensor(q[:, :, 2 * ax + 1, :], v[:, :, 2 * ax, :], s2, ALU.mult))
                    for x in (0, 1):
                        i = dve.tensor_tensor(
                            row.rearrange("p (g b) -> p g b", b=32)[:, x::2, :],
                            row.rearrange("p (g b) -> p g b", b=32)[:, x::2, :],
                            sqbuf[n % 2].rearrange("p (g b) -> p g b", b=32)[:, x::2, :],
                            ALU.subtract if x == 0 else ALU.add)
                        if x == 0:
                            link(i)
                    i.then_inc(S(l, "row_ready"), 1)

                dve.wait_ge(S(l, "tab_in"), 32)
                q0 = ada_start(l) // KD
                for n in range(len(units) + 1):
                    for q in range(q0, len(ada_pieces(l)) // KD):
                        if n == part_end(l, q) + 1:
                            dve.wait_ge(S(l, "rows_in"), 16 * (q0 + 1))
                            dve.wait_ge(S(l, "ada_done"), (q + 1) * KD)
                            dve.tensor_tensor(rows[:, q, :], PS[6 + q % 2][:, :], rows[:, q, :], ALU.add)\
                                .then_inc(S(l, "mod_rows"), 1)
                    if n < len(units) and KIND[units[n][0]] == "norm":
                        norm_front(n)
                    if n >= 1 and KIND[units[n - 1][0]] == "norm":
                        norm_back(n - 1)
                    if n < len(units) and KIND[units[n][0]] == "rope":
                        rope(n)
                    if n < len(units) and KIND[units[n][0]] == "gate":
                        c, t = units[n]
                        g = {6: gf, 7: gb}[c][:, t, :]
                        dve.wait_ge(S(l, "act_rel"), n_act[n])
                        dve.scalar_tensor_tensor(g, g, 1.0, PS[n % 4][:, :], ALU.add, ALU.mult)\
                            .then_inc(S(l, "gate_rel"), 1)
                meet(dve, "dve")

                nu = na_units(l)

                def norm_o(j):
                    o = slice(j * NAH, (j + 1) * NAH)
                    dve.wait_ge(S(l, "pv_done"), NAH * (j + 1))
                    link(dve.reciprocal(rinv[:, o], rsum[:, o]))
                    dve.tensor_tensor(mix[:, j, 0:CH].rearrange("p (h d) -> p h d", h=NAH),
                                      PS[5 + j % 2][:, :].rearrange("p (h d) -> p h d", h=NAH),
                                      rinv[:, o].unsqueeze(2).broadcast_to([P, NAH, NAD]), ALU.mult)\
                        .then_inc(S(l, "o_norm"), 1)

                for n, (j, h, ranges, _, ty) in enumerate(nu):
                    w = sum(k for _, k in ranges)
                    dve.wait_ge(S(l, "s_done"), n + 1)
                    if ty is not None:
                        if n < NAH:
                            dve.wait_ge(S(l, "bias_ready"), {7: 8}.get(h, h + 3) if h not in (5, 6) else 2)
                        link(dve.tensor_tensor(PS[n % 3][:, 0:KSPAN], PS[n % 3][:, 0:KSPAN], bias[h][:, ty, :], ALU.add))
                    if n >= 4:
                        dve.wait_ge(S(l, "p_ready"), n - 3)
                    dve.tensor_reduce(negmax[:, n % 4:n % 4 + 1], PS[n % 3][:, 0:w], AX.X, ALU.max, negate=True)\
                        .then_inc(S(l, "nm_ready"), 1)
                    if n % NAH == 3 and n > NAH:
                        norm_o(n // NAH - 1)
                norm_o(len(nu) // NAH - 1)
                meet(dve, "dve")

                groups = ret_groups(l)

                def head_norm(g, part):
                    r, lat, qts, kts = groups[g]
                    n = len(qts)
                    d = part % 2
                    if part == 0:
                        dve.wait_ge(S(l, "w_used_r"), ret_end(l, g))
                    if part == 2:
                        dve.wait_ge(S(l, "hrstd_ready"), g + 1)
                    for i in range(n):
                        u = d * 4 + i
                        o = PS[2 + 2 * d + g % 2][:, i * P:(i + 1) * P]
                        if part < 2:
                            link(dve.bn_stats(bnst[:, u * 6:u * 6 + 6], o))
                            link(dve.bn_aggr(mv[:, u * 2:u * 2 + 2], bnst[:, u * 6:u * 6 + 6]))
                        else:
                            link(dve.tensor_scalar(ofb[d][:, i * P:(i + 1) * P], o, mv[:, 2 * u:2 * u + 1],
                                                   hrstd[:, u:u + 1], ALU.subtract, ALU.mult))
                    if part == 1:
                        dve.tensor_scalar(hvar, mv.rearrange("p (a b) -> p a b", b=2)[:, :, 1], RET_EPS, 4.0,
                                          ALU.add, ALU.mult).then_inc(S(l, "hvar_ready"), 1)
                    if part >= 2:
                        v = ofb[d][:, 0:n * P].rearrange("p (a b) -> p a b", a=n)
                        gate = (gf, gb)[d][:, qts[0]:qts[0] + n, r * RD:(r + 1) * RD]
                        link(dve.tensor_tensor(v, v, gate, ALU.mult))
                    if part == 3:
                        dve.tensor_tensor(mix[:, qts[0]:qts[0] + n, CH + r * RD:CH + (r + 1) * RD],
                                          ofb[0][:, 0:n * P].rearrange("p (a b) -> p a b", a=n),
                                          ofb[1][:, 0:n * P].rearrange("p (a b) -> p a b", a=n), ALU.add)\
                            .then_inc(S(l, "ret_norm"), 1)

                link(dve.memset(mv, 0.0))
                for m, (g, a, r, qts, kt, _) in enumerate(ret_steps(l)):
                    w = len(qts) * P
                    for d in range(2):
                        dve.wait_ge(S(l, "st_done"), m + 1)
                        dve.wait_ge(S(l, "dec_ready"), 2 * m + d + 1)
                        if m >= 3:
                            dve.wait_ge(S(l, "w_used_r"), m - 2)
                        dve.tensor_tensor(Wd[m % 3][:, d, 0:w], PS[m % 2][:, 0:w], dec[(2 * m + d) % 4][:, 0:w],
                                          ALU.mult).then_inc(S(l, "w_mult"), 1)
                    if g >= 1:
                        for part in ({1: [0], 2: [1], 3: [2], 4: [3]} if len(qts) == LAT else {0: [0, 1], 1: [2, 3]})\
                                .get(a, []):
                            head_norm(g - 1, part)
                for part in range(4):
                    head_norm(len(groups) - 1, part)
                meet(dve, "dve")

                nt = tiles(l)
                dve.wait_ge(S(l, "g_in"), 80)
                for n in (0, 2):
                    link(dve.scalar_tensor_tensor(bc[n][:, :], bc[n][:, :], 1.0, normw2, ALU.add, ALU.mult))
                dve.wait_ge(S(l, "gate_in"), 32)

                def ffn_row(t):
                    a, b = (0, 1) if t < LAT else (2, 3)
                    dve.wait_ge(S(l, "g_rs"), t + 1)
                    link(dve.scalar_tensor_tensor(hrow2[t], X[:, t, :], rstd[:, t:t + 1], bc[a][:, :],
                                                  ALU.mult, ALU.mult))
                    dve.tensor_tensor(hrow2[t], hrow2[t], bc[b][:, :], ALU.add).then_inc(S(l, "g_row"), 1)

                for n in range(2 * nt):
                    c, t = divmod(n, nt)
                    dve.wait_ge(S(l, "op_done"), n + 1)
                    link(dve.tensor_tensor(otmp[n % 2], PS[n % 4][:, :],
                                           mix_gate[0 if t < LAT else 1][:, c * CH:(c + 1) * CH], ALU.mult))
                    xs = X[:, t, c * CH:(c + 1) * CH]
                    dve.tensor_tensor(xs, xs, otmp[n % 2], ALU.add).then_inc(S(l, "x_upd"), 1)
                    if c == 1:
                        if t >= 1:
                            ffn_row(t - 1)
                        dve.wait_ge(S(l, "g_ss"), t + 1)
                        dve.tensor_scalar(msq[:, t:t + 1], ss[:, t:t + 1], 1.0 / D, EPS, ALU.mult, ALU.add)\
                            .then_inc(S(l, "g_ms"), 1)
                ffn_row(nt - 1)
                route(l)
                dve.wait_ge(S(l, "idx_in"), 16)
                link(dve.memset(y_place[:, 0:1], NO_ROW))
                link(dve.tensor_copy(y_place[:, 1:NBLK + 1], assign))
                link(dve.tensor_scalar(second, assign, float(TOK), None, ALU.is_ge))
                link(dve.scalar_tensor_tensor(token, second, -float(TOK), assign, ALU.mult, ALU.add))
                meet(dve, "dve")

                n_pairs = dve.value_load(ints[0:1, 79:80], min_val=NE // 2, max_val=NBLK // 2 - 1)

                def low(dst, src, hi, ready):
                    dve.tensor_tensor(dst, src, hi.bitcast(F32), ALU.subtract).then_inc(S(l, ready), 1)

                def low_x(half):
                    o = slice(4 * half, 4 * half + 4)
                    low(x_lo[:, o, :], PS[half][:, :].rearrange("p (a b) -> p a b", a=4), x_hi[:, o, :], "xlo_ready")

                for half in range(2):
                    dve.wait_ge(S(l, "xhi_ready"), half + 1)
                    low_x(half)
                with dve.Fori(0, n_pairs) as i:
                    for s in range(2):
                        b = 2 * i + s

                        def low_w(u):
                            dve.wait_ge(S(l, "whi_ready"), b * UNITS + u + 1)
                            low(w_lo[u % 3][:, :, :], raw(s, u), w_hi[u % 3][:, :, :], "wlo_ready")

                        for u in range(8):
                            low_w(u)
                        dve.wait_ge(S(l, "th_ready"), b + 1)
                        dve.scalar_tensor_tensor(act, th, 1.0, PS[2][:, :], ALU.add, ALU.mult)\
                            .then_inc(S(l, "gate_step"), 1)
                        low_w(8)
                        low_w(9)
                        dve.wait_ge(S(l, "gate_step"), b + 1)
                        dve.wait_ge(S(l, "w_used"), b * UNITS + 8 + 3)
                        dve.scalar_tensor_tensor(act, act, 0.5, PS[3][:, :], ALU.mult, ALU.mult)\
                            .then_inc(S(l, "a_ready"), 1)
                        dve.wait_ge(S(l, "xhi_ready"), 2 * b + 3)
                        low_x(0)
                        dve.wait_ge(S(l, "ahi_ready"), b + 1)
                        low(a_lo[:, :, :], PS[4][:, :].rearrange("p (a b) -> p a b", a=4), a_hi[:, :, :], "alo_ready")
                        dve.wait_ge(S(l, "xhi_ready"), 2 * b + 4)
                        low_x(1)
                        low_w(10)
                        low_w(11)
                meet(dve, "dve")

                dve.wait_ge(S(l, "gb_in"), 32)
                for t in range(nt):
                    v = z[t % 2]
                    dve.wait_ge(S(l, "z_first"), t + 1)
                    link(dve.scalar_tensor_tensor(v, y2[t], wgt[:, 2 * t + 1:2 * t + 2], v, ALU.mult, ALU.add))
                    link(dve.tensor_tensor(v, v, ffn_gate[0 if t < LAT else 1], ALU.mult))
                    dve.tensor_tensor(X[:, t, :], X[:, t, :], v, ALU.add).then_inc(S(l, "comb_done"), 1)
                meet(dve, "dve")
                if l < DEPTH - 1:
                    dve.wait_ge(cleared, 1)
                    dve.drain()


def _constants():
    f = np.float32
    tok = np.arange(SEQ)
    col, row = tok // ROWS, tok % ROWS
    time = row * COLS + col
    freqs = 10000.0 ** (-np.arange(32, dtype=np.float64) / 32)
    ang = np.stack([row[:, None] * freqs, col[:, None] * freqs], axis=1)
    cos = np.repeat(np.cos(ang)[:, :, None, :], 2, axis=2).reshape(LAT, P, RD)
    sin = np.sin(ang).reshape(LAT, P, 64)
    ct = np.arange(CTX)
    fwd = np.concatenate([np.where(time[None] >= time[:, None], time[None] - time[:, None], BIG),
                          time[None] + CTX - ct[:, None]])
    bwd = np.concatenate([np.where(time[None] <= time[:, None], time[:, None] - time[None], BIG),
                          ct[:, None] + SEQ - time[None]])
    cf = np.where(ct[None] >= ct[:, None], ct[None] - ct[:, None], BIG)
    delta = np.stack([fwd, bwd]).reshape(2, NT, P, SEQ).transpose(2, 0, 1, 3)
    dctx = np.stack([cf, cf.T]).reshape(2, 2, P, CTX).transpose(2, 0, 1, 3)
    mask = np.zeros((P, 3, KSPAN))
    for ty, j in ((0, 0), (1, 1), (2, 3)):
        qcol = j * QBLK + np.arange(QBLK)
        c0 = np.clip(qcol - WIN_W // 2, 0, COLS - WIN_W)
        kcol = KSTART[j] + np.arange(KBLK)
        ok = (kcol[None] >= c0[:, None]) & (kcol[None] < c0[:, None] + WIN_W)
        mask[:, ty] = np.repeat(np.repeat(np.where(ok, 0.0, -BIG), ROWS, 0), ROWS, 1)
    return {
        "ident": np.eye(P, dtype=f), "upper": np.triu(np.ones((P, P), f), 1),
        "cos_t": cos.transpose(1, 0, 2).astype(f), "sin_t": sin.transpose(1, 0, 2).astype(f),
        "delta": np.stack([delta[:, :, 3 * i:3 * i + 3].transpose(0, 2, 1, 3) for i in range(2)]).astype(f), "delta_ctx": dctx.astype(f), "na_mask": mask.astype(f),
        "rev8": (NG - np.arange(NG)).astype(f), "rev32": (NE - np.arange(NE)).astype(f),
        "ovidx": np.arange(NOV).astype(f), "first_blocks": np.arange(NE, dtype=np.int32),
        "assign_ids": (np.arange(2)[None, None] * TOK + np.arange(NT)[None, :, None] * P + np.arange(P)[:, None, None])
        .reshape(P, 2 * NT).astype(np.int32),
    }


def kernel(**inputs):
    import concourse.bacc as bacc
    from concourse.bass_utils import run_bass_kernel_spmd

    x = {k: np.asarray(v) for k, v in inputs.items()}
    arrays = {n: x[n] for n in ("ada_w", "norm_mix_w", "norm_ffn_w", "w_in", "na_q_norm", "na_k_norm",
                                "ret_decay", "w_out", "router_w", "router_bias", "exp_w_gate", "exp_w_up",
                                "exp_w_down")}
    arrays["x"] = x["x"][0].reshape(ROWS, COLS, D).transpose(1, 0, 2).reshape(SEQ, D)
    arrays["ctx"] = x["ctx"][0]
    arrays["cc"] = np.stack([x["c"][0], x["c_ctx"]], -1).reshape(KD, P, 2).transpose(1, 0, 2).reshape(P, 2 * KD)
    rpb = x["na_rpb"]
    win = np.stack([rpb[:, :, ROWS - 1 - q:2 * ROWS - 1 - q, :] for q in range(ROWS)], 2).transpose(0, 1, 2, 4, 3)
    win = np.pad(win, ((0, 0), (0, 0), (0, 0), (V_PAD, V_PAD), (0, 0)))
    win = np.stack([np.stack([win[:, :, :, (o := V_PAD + WIN_W - 1 + b - q):o + KBLK] for b in BIAS_START], 3)
                    for q in range(QBLK)], 2)
    arrays["rpb"] = win.reshape(DEPTH, NAH, P, 3, KSPAN)
    ada_b = np.zeros((DEPTH, 3, 4, 32, CH), np.float32)
    ada_b[:, :, :, 0:2] = x["ada_b"].reshape(DEPTH, 3, 4, 1, CH)
    arrays["ada_b"] = ada_b.reshape(DEPTH * 3, P, CH)
    arrays.update(_constants())
    arrays = {n: np.ascontiguousarray(a) for n, a in arrays.items()}
    nc = bacc.Bacc("TRN2", target_bir_lowering=False, num_devices=1)
    aps = {n: nc.dram_tensor(f"in_{n}", a.shape, mybir.dt.from_np(a.dtype), kind="ExternalInput").ap()
           for n, a in arrays.items()}
    aps["out"] = nc.dram_tensor("out_x", (SEQ, D), F32, kind="ExternalOutput").ap()
    build(nc, aps)
    r = run_bass_kernel_spmd(nc, [{f"in_{n}": a for n, a in arrays.items()}], core_ids=[0])
    out = r.results[0]["out_x"]
    return out.reshape(COLS, ROWS, D).transpose(1, 0, 2).reshape(1, SEQ, D)
```

```python
from contextlib import ExitStack
import math

import numpy as np

import concourse.bass as bass
from concourse import mybir

F32 = mybir.dt.float32
F32R = mybir.dt.float32r
I32 = mybir.dt.int32
ACT = mybir.ActivationFunctionType
ALU = mybir.AluOpType
AX = mybir.AxisListType

P = 128
DEPTH, D, SEQ, CTX = 2, 1024, 512, 256
ROWS, COLS = 8, 64
KD = D // P
LAT = SEQ // P
NT = (SEQ + CTX) // P
TOK = SEQ + CTX
NAH, NAD = 8, 64
RH, RD = 4, 128
CH = 512
WIN_W, KBLK, QBLK = 16, 32, 16
KSPAN = KBLK * ROWS
NE, NG, EPG = 32, 8, 4
FF = 512
NOV = 2 * TOK // P + 2
NBLK = NE + NOV
UNITS = 12
NO_ROW = 4095
BIG = 1.0e30
EPS = 1e-6
RET_EPS = 1e-5

K = 256
HC = 256
N_STEPS = 32
PIECES_AT = 10
TURNS_AT = 6
QA, KA, VA = 48 * K, 60 * K, 72 * K
QB, KB, VB, GF = 84 * K, 96 * K, 108 * K, 120 * K
ARENA = 134 * K
SMALL = 444

KSTART = [0, 8, 24, 32]
BIAS_TYPE = [0, 1, 1, 2]
BIAS_START = [0, -8, -16]
V_TILES = [[0, 1], [6, 7], [7, 8], [2, 3]]
V_PAD = 16
S_BANKS = [0, 1, 2, 7]
OUT_BANKS = [0, 1, 6, 7]


def counted(units, pred):
    n, out = 0, []
    for u in units:
        n += bool(pred(u))
        out.append(n)
    return out


def build(nc, A):
    stack = ExitStack()
    with stack:
        def sb(name, shape, dt=F32):
            return stack.enter_context(nc.sbuf_tensor(name, shape, dt))

        def sem(name):
            return stack.enter_context(nc.semaphore(name))

        def dram(name, shape, dt=F32):
            return nc.dram_tensor(name, shape, dt).ap()

        X = sb("X", [P, NT, D])
        hT = sb("hT", [P, KD, TOK])
        hT_at = nc.sbuf_base - 4 * KD * TOK
        arena = sb("arena", [P, ARENA])
        arena_at = nc.sbuf_base - 4 * ARENA
        bcs = sb("bc", [P, 4 * D])
        bc = [bcs[:, i * D:(i + 1) * D] for i in range(4)]
        ident = sb("ident", [P, P])
        upper = sb("upper", [P, P])
        ones = sb("ones", [P, P])
        tabs = sb("tabs", [P, 768])
        sc32 = sb("sc32", [P, KD, 32])
        rw = sb("rw", [P, KD, NE])
        small = sb("small", [P, SMALL])
        ints = sb("ints", [P, 128], I32)
        idx_slot = [sb(f"idx_slot{s}", [P, 1], I32) for s in range(2)]
        nag = sb("nag", [P, 4, NAD])
        PS = [stack.enter_context(nc.psum_tensor(f"PS{i}", [P, 512], F32)) for i in range(8)]

        used = [0]

        def cut(n):
            used[0] += n
            return small[:, used[0] - n:used[0]]

        neghalf = cut(32)
        ss = cut(8)
        msq = cut(8)
        rstd = cut(8)
        lnscale = cut(1)
        decay = cut(DEPTH * 2 * RH)
        cc = cut(2 * KD)
        cth = cut(2 * KD)
        qk_ss = cut(2 * NAH)
        qk_ms = cut(2 * NAH)
        qk_rs = cut(2 * NAH)
        negmax = cut(4)
        rsum = cut(NT * NAH)
        rinv = cut(NT * NAH)
        bnst = cut(8 * 6)
        mv = cut(8 * 2)
        hvar = cut(8)
        hrstd = cut(8)
        wgt = cut(2 * NT)
        rbias = cut(NE)
        rev8 = cut(NG)
        rev32 = cut(NE)
        ovidx = cut(NOV)
        less_none = cut(2 * NT)
        assert used[0] <= SMALL

        def area(off, shape):
            n = int(np.prod(shape))
            names = "abc"[:len(shape)]
            v = arena[:, off:off + n]
            if len(shape) > 1:
                pat = f"p ({' '.join(names)}) -> p {' '.join(names)}"
                v = v.rearrange(pat, **{names[i]: shape[i] for i in range(len(shape))})
            return v

        def split(name, at, shape):
            return nc.alloc_sbuf_tensor_at(name, [P] + shape, F32R, offset=at)

        h_hi = split("h_hi", hT_at, [KD, TOK])
        h_lo = split("h_lo", arena_at + 4 * 24 * K, [KD, TOK])
        wc = [area(i * 8 * K, (4, HC)) for i in range(3)]
        wc_lo = [split(f"wc_lo{i}", arena_at + 4 * i * 8 * K, [4, HC]) for i in range(3)]
        wc_hi = [split(f"wc_hi{i}", arena_at + 4 * (i * 8 + 4) * K, [4, HC]) for i in range(3)]
        ada_w = [area(GF, (4, CH)), bcs[:, 0:2048].rearrange("p (a b) -> p a b", a=4)]
        ada_first = [area(at, (2, 4, CH)) for at in (24 * K, QA, QA + 16 * K, 104 * K)]
        rows = area(128 * K, (3, CH))
        qaT, kaT = area(QA, (4, TOK)), area(KA, (4, TOK))
        va, va_shift = area(VA, (NT, CH)), area(30 * K, (3, CH))
        qbT, kbT = area(QB, (RH, TOK)), area(KB, (RH, TOK))
        vb, gf = area(VB, (NT, CH)), area(GF, (NT, CH))
        gb = bcs[:, 0:NT * CH].rearrange("p (a b) -> p a b", a=NT)
        hTf = hT[:, :, :].rearrange("p a b -> p (a b)")
        normw = area(QB, (D,))
        hrow1 = [area(QB + (1 + i) * D, (D,)) for i in range(2)]
        junk = [area(QB + (3 + i) * D, (D,)) for i in range(2)]
        rowbuf = [area(VB + i * 512, (512,)) for i in range(2)]
        sqbuf = [area(VB + 1024 + i * 512, (512,)) for i in range(2)]
        cosF = tabs[:, 0:512].rearrange("p (a b) -> p a b", a=4)
        sinF = tabs[:, 512:768].rearrange("p (a b) -> p a b", a=4)
        mask = tabs[:, 0:768].rearrange("p (a b) -> p a b", a=3)
        bias = [bc[3][:, 0:3 * KSPAN].rearrange("p (a b) -> p a b", a=3)] \
            + [area((h - 1) * 3 * KSPAN, (3, KSPAN)) for h in range(1, NAH)]
        diag = [area(21 * K + i * P, (P,)) for i in range(2)]
        pexp = [area(22 * K + i * 512, (512,)) for i in range(2)]
        pT = [area(26 * K + i * 512, (4, P)) for i in range(2)]
        mixT_na = hTf[:, 0:4 * TOK].rearrange("p (a b) -> p a b", a=4)
        q_pad = [hTf[:, 4 * TOK + i * 2 * TOK:4 * TOK + (i + 1) * 2 * TOK].rearrange("p (a b) -> p a b", a=2)
                 for i in range(2)]
        mix = hTf[:, 4 * TOK:8 * TOK].rearrange("p (a b) -> p a b", a=NT)
        delta = [area(36 * K, (3, 2, SEQ)), area(0, (3, 2, SEQ))]
        dec = [area(12 * K + i * 512, (512,)) for i in range(4)]
        Wd = [area(20 * K + i * D, (2, SEQ)) for i in range(3)]
        mix_gate = [area(52 * K + i * D, (D,)) for i in range(2)]
        wo0 = area(60 * K, (KD, CH))
        dctx = area(32 * K, (2, 2, CTX))
        ofb = [area(48 * K + i * 512, (512,)) for i in range(2)]
        mixT = area(QB, (4, TOK))
        hT2 = area(16 * K, (KD, TOK))
        wo1 = area(0, (KD, CH))
        otmp = [area(76 * K + i * 512, (512,)) for i in range(2)]
        wg = [area(s * 48 * K, (KD, FF)) for s in range(2)]
        wu = [area(s * 48 * K + 16 * K, (KD, FF)) for s in range(2)]
        wd = [area(s * 48 * K + 32 * K, (4, D)) for s in range(2)]
        hrow2 = [area(98 * K + t * D, (D,)) for t in range(NT)]
        normw2 = area(122 * K, (D,))
        junk2 = [area(126 * K, (D,)), area(130 * K, (D,))]
        xg = [area(96 * K + s * D, (D,)) for s in range(2)]
        yb = [area(104 * K, (D,)), area(124 * K, (D,))]
        th = area(108 * K, (FF,))
        act = area(110 * K, (FF,))

        def raw(s, u):
            if u < 8:
                return (wg, wu)[u // 4][s][:, 2 * (u % 4):2 * (u % 4) + 2, :]
            return wd[s][:, u - 8, :].rearrange("p (a b) -> p a b", a=2)

        x_hi = split("x_hi", arena_at + 4 * 112 * K, [KD, P])
        x_lo = split("x_lo", arena_at + 4 * 116 * K, [KD, P])
        a_hi = split("a_hi", arena_at + 4 * 120 * K, [4, P])
        a_lo = split("a_lo", arena_at + 4 * 122 * K, [4, P])
        w_hi = [split(f"w_hi{i}", hT_at + 4 * i * D, [2, FF]) for i in range(3)]
        w_lo = [split(f"w_lo{i}", hT_at + 4 * (3 + i) * D, [2, FF]) for i in range(3)]
        y_at = [QA + i * D for i in range(9)] + [104 * K, 116 * K, 120 * K]
        y1 = [area(y_at[2 * i], (D,)) for i in range(NT)]
        y2 = [area(y_at[2 * i + 1], (D,)) for i in range(NT)]
        ffn_gate = [area(124 * K + i * D, (D,)) for i in range(2)]
        assign = ints[:, 80:80 + NBLK]
        token = tabs[:, 0:NBLK].bitcast(I32)
        second = tabs[:, 64:64 + NBLK]
        y_idx = [tabs[:, 128 + s:129 + s].bitcast(I32) for s in range(2)]
        y_place = tabs[:, 192:192 + NBLK + 1].bitcast(I32)
        r_at = [0]

        def rt(shape):
            n = int(np.prod(shape))
            i, o = divmod(r_at[0], D)
            if o + n > D:
                i, o = i + 1, 0
            r_at[0] = i * D + o + n
            v = bc[i][:, o:o + n]
            if len(shape) > 1:
                names = "abc"[:len(shape)]
                v = v.rearrange(f"p ({' '.join(names)}) -> p {' '.join(names)}",
                                **{names[k]: shape[k] for k in range(len(shape))})
            return v

        route_t = {n: rt(shape) for n, shape in dict(
            score=(NT, NE), ssel=(NT, NE), pairs=(NT * NG, 6), gsum=(NT, NG), gmax=(NT,), gcand=(NT, NG),
            gfirst=(NT,), ing=(NT, NG), pen=(NT, NG), ms=(NT, NE), top=(NT,), cand=(NT, NE), M=(NT, NE),
            before=(NT + 1, NE), extra=(NE,), zero=(NE,), ovinc=(NE,), ovb=(NE,), count=(NE,), ovcmp=(NOV, NE),
            ovexp=(NOV,), npair=(1,), oh=(2 * NT, NE), tmp=(2 * NT, NE), first=(2 * NT,), s=(2 * NT,),
            rank=(2 * NT,), full=(2 * NT,), q=(2 * NT,), r=(2 * NT,), pos=(2 * NT,), ov=(2 * NT,), e=(2 * NT,),
            blk=(2 * NT,), qcmp=(2 * NT, NT - 1)).items()}
        route_t["in_blk"] = area(128 * K, (2 * NT, NBLK))
        in_row = area(122 * K, (2 * NT, P))
        row_no, blk_no = tabs[:, 256:256 + P], tabs[:, 256 + P:256 + P + NBLK]

        mod_d = [dram(f"mod_d{l}", (3, P, CH)) for l in range(DEPTH)]
        h_d = dram("h_d", (TOK, D))
        y_d = dram("y_d", (2 * TOK, D))

        cc_in = sem("cc_in")
        ada_first_in = [sem(f"ada_first_in{i}") for i in range(4)]
        ident_in = sem("ident_in")
        const_in = sem("const_in")
        x_in0, x_in1, x_in2 = sem("x_in0"), sem("x_in1"), sem("x_in2")
        pool_passed = sem("pool_passed")
        out_done = sem("out_done")
        sc_tanh = sem("sc_tanh")
        lg_ready = sem("lg_ready")
        sc_ready = sem("sc_ready")
        decay_exp = sem("decay_exp")
        dve_step = sem("dve_step")
        act_step = sem("act_step")
        pool_step = sem("pool_step")
        pe_step = sem("pe_step")
        N_CONST = 11

        NAMES = """ada_in0 ada_in1 ada_done rows_in mod_rows mod_out
        modb_in modc_in next_in ss_done ms_ready rstd_ready hrow_scaled hrow_ready tr_done hT_ready
        wc_in0 wc_in1 wc_in2 wch_ready wcl_ready hlo_ready slot_done act_rel gate_rel
        qk_ms_ready qk_rs_ready row_ready trow_done trow_evac
        vshift tab_in delta_in2 mask_in bias_in0 bias_in1 bias_in2 bias_ready s_done nm_ready
        qz_first qz_more p_ready diag_ready pt_done pt_evac pv_done o_evac
        delta_in st_done dec_ready w_mult w_used_r pvr_done hvar_ready hrstd_ready head_normed head_gated ret_norm
        wo_in0 wo_in1 gate_in mt_done mt_evac op_done x_upd
        g_in g_ss g_ms g_rs g_row g_tr g_hT h_out logit_done exp_done m_ready rank_done route_ready
        numbers_in places_ready places_done token_ready
        wg_in0 wg_in1 wu_in0 wu_in1 wd_in0 wd_in1 whi_ready wlo_ready w_used
        idx_cp0 idx_cp1 y_idx_cp xg_in0 xg_in1 xg_used0 xg_used1 xt_done xhi_ready xlo_ready
        th_ready gate_step a_ready at_done ahi_ready alo_ready y_copied yb_free y_out
        gb_in y_in0 y_in1 y_in2 y_in3 y_in4 y_in5 z_first z_gated comb_done""".split()
        KEPT = ("xg_in0", "xg_in1", "y_out", "gb_in", "next_in", "y_in0", "y_in1", "y_in2", "y_in3", "y_in4",
                "y_in5", "z_first", "z_gated", "comb_done")
        SEMS = {(None, n): sem(n) for n in NAMES if n not in KEPT}
        SEMS.update({(l, n): sem(f"{n}_{l}") for l in range(DEPTH) for n in KEPT})
        met = sem("met")
        cleared = sem("cleared")

        def S(l, name):
            return SEMS[l if name in KEPT else None, name]

        steps = {"dve": 0, "act": 0, "pool": 0, "pe": 0}
        meetings = {}

        def chain(eng, which, s):
            def link(ins):
                ins.then_inc(s, 1)
                steps[which] += 1
                eng.wait_ge(s, steps[which])
            return link

        def meet(eng, who):
            meetings[who] = meetings.get(who, 0) + 1
            eng.drain().then_inc(met, 1)
            eng.wait_ge(met, 5 * meetings[who])

        def tiles(l):
            return NT if l < DEPTH - 1 else LAT

        KIND = ["norm", "norm", "v", "rope", "rope", "v", "gate", "gate"]

        def proj_pairs(l, c):
            return 3 if l < DEPTH - 1 or c in (1, 2, 4, 5) else 2

        def proj_slots(l):
            return [(w, p) for p in range(proj_pairs(l, 0)) for w in range(3)] \
                + [(w, p) for w in range(3, N_STEPS) for p in range(proj_pairs(l, w // 4))]

        def step_end(l, w):
            return max(s for s, x in enumerate(proj_slots(l)) if x[0] == w)

        def step_start(l, w):
            return min(s for s, x in enumerate(proj_slots(l)) if x[0] == w)

        def split_at(l):
            return {step_end(l, w - 3) + 2: w for w in range(3, N_STEPS)}

        def turns_at(l):
            with_row = [n for n, u in enumerate(proj_units(l)) if needs_row(u)]
            return {max(proj_units(l)[n][3] + 2, TURNS_AT + m): n for m, n in enumerate(with_row)}

        def proj_units(l):
            return [(w // 4, p, w // 2 % 2, s) for s, (w, p) in enumerate(proj_slots(l)) if w % 2]

        def unit_at(l):
            return {u[3]: n for n, u in enumerate(proj_units(l))}

        def proj_bank(u):
            return PS[3 * u[2] + u[1]]

        def last_in_bank(l, w, p):
            return max([n for n, u in enumerate(proj_units(l)) if u[1] == p and u[2] == w // 2 % 2
                        and 4 * u[0] + 2 * u[2] + 1 < w], default=None)

        def needs_row(u):
            return KIND[u[0]] in ("norm", "rope")

        def act_reads(u):
            return KIND[u[0]] in ("norm", "v", "gate")

        def dve_reads(u):
            return KIND[u[0]] == "gate"

        def ada_pieces(l):
            own = [(l, r, k) for r in range(0 if l == 0 else 1, 3) for k in range(KD)]
            return own + ([(l + 1, 0, k) for k in range(KD)] if l < DEPTH - 1 else [])

        def ada_start(l):
            return KD if l == 0 else 0

        def after_slot(l, s):
            p = (s - PIECES_AT) // 2 + ada_start(l)
            return p if s >= PIECES_AT and s % 2 == 0 and p < len(ada_pieces(l)) else None

        def piece_slot(l, p):
            return PIECES_AT + 2 * (p - ada_start(l))

        def na_units(l):
            out = []
            for hp in range(NAH // 2):
                for j in range(LAT):
                    for e in range(2):
                        out.append((hp, j, e, [(KSTART[j] * ROWS, KSPAN), (SEQ, CTX)], V_TILES[j] + [4, 5],
                                    BIAS_TYPE[j]))
                if l < DEPTH - 1:
                    for t in (4, 5):
                        for e in range(2):
                            out.append((hp, t, e, [(SEQ, CTX)], [4, 5], None))
            return out

        def na_outputs(l):
            nu = na_units(l)
            out = []
            for hp in range(NAH // 2):
                for t0, n in ((0, LAT),) + (((LAT, 2),) if l < DEPTH - 1 else ()):
                    out.append((hp, t0, n, max(i for i, u in enumerate(nu) if u[0] == hp and t0 <= u[1] < t0 + n)))
            return out

        def v_rows(vt):
            return va[:, vt, :] if vt < NT else va_shift[:, vt - NT, :]

        def na_bank(l, n):
            return [i for i, x in enumerate(na_outputs(l)) if n <= x[3]][0]

        def ret_groups(l):
            out = []
            for r in range(RH):
                out.append((r, True, range(0, LAT), range(0, NT)))
                if l < DEPTH - 1:
                    out.append((r, False, range(LAT, NT), range(LAT, NT)))
            return out

        def ret_bank(g, d):
            return PS[2 + 2 * (g % 3) + d]

        def ret_steps(l):
            return [(g, a, r, qts, kt, a == len(kts) - 1)
                    for g, (r, _, qts, kts) in enumerate(ret_groups(l)) for a, kt in enumerate(kts)]

        def ret_end(l, g):
            return [m for m, x in enumerate(ret_steps(l)) if x[0] == g][-1] + 1

        def last_groups(l):
            return 2 if l < DEPTH - 1 else 1

        def normed(group, d):
            r, _, qts, _ = group
            n = len(qts)
            at = (slice(None), slice(qts[0], qts[0] + n), slice(r * RD, (r + 1) * RD))
            return ofb[d][:, 0:n * P].rearrange("p (a b) -> p a b", a=n), (gf, gb)[d][at], mix[at]

        block = stack.enter_context(nc.Block())

        @block.sync
        def _(sp):
            def const(dst, src):
                sp.dma_start(dst, src).then_inc(const_in, 16)

            def piece(l, p):
                ll, r, k = ada_pieces(l)[p]
                if p >= 2:
                    sp.wait_ge(S(l, "ada_done"), p - 1)
                if p % 2 and p in (ada_start(l), ada_start(l) + 1) and p >= ada_start(l):
                    sp.wait_ge(S(l, "hrow_ready"), NT)
                sp.dma_start(ada_w[p % 2], A["ada_w"][ll][k * P:(k + 1) * P, 2048 * r:2048 * (r + 1)]
                             .rearrange("p (j x) -> p j x", x=CH)).then_inc(S(l, f"ada_in{p % 2}"), 16)

            def store_rows(l, q):
                ll, r, _ = ada_pieces(l)[q * KD]
                sp.wait_ge(S(l, "mod_rows"), q + 1)
                sp.dma_start(mod_d[ll][r], rows[:, q % 3, :]).then_inc(S(l, "mod_out"), 16)

            def load_mod(l, dst, i, q):
                src = mod_d[l][q // 2].rearrange("(j s) x -> s j x", s=32)[i, 2 * (q % 2):2 * (q % 2) + 2, :]
                return sp.dma_start(dst.rearrange("p (a b) -> p a b", a=2), src.partition_broadcast(P))

            def load_w(l, w):
                sp.dma_start(wc[w % 3], A["w_in"][l, w]).then_inc(S(l, f"wc_in{w % 3}"), 16)

            sp.dma_start(cc, A["cc"]).then_inc(cc_in, 16)
            sp.dma_start(rows[:, 0, :], A["ada_b"][0]).then_inc(S(0, "rows_in"), 16)
            for i in range(4):
                sp.dma_start(ada_first[i].rearrange("p k j x -> p k (j x)"),
                             A["ada_w"][0][2 * i * P:(2 * i + 2) * P, 0:2048].rearrange("(k p) n -> p k n", p=P))\
                    .then_inc(ada_first_in[i], 16)

            def load_x(tiles_, ready):
                for t in tiles_:
                    src = A["x"][t * P:(t + 1) * P, :] if t < LAT else A["ctx"][(t - LAT) * P:(t - LAT + 1) * P, :]
                    sp.dma_start(X[:, t, :], src).then_inc(ready, 16)

            load_x((0, 1), x_in0)
            sp.dma_start(normw, A["norm_mix_w"][0].partition_broadcast(P)).then_inc(S(0, "modb_in"), 16)
            sp.dma_start(ident[:, :], A["ident"]).then_inc(ident_in, 16)
            store_rows(0, 0)
            load_w(0, 0)
            sp.wait_ge(S(0, "mod_out"), 16)
            for n, (i, q) in enumerate(((0, 1), (0, 0))):
                load_mod(0, bc[n], i, q).then_inc(S(0, "modb_in"), 16)
            load_x((2, 3), x_in1)
            load_w(0, 1)
            load_w(0, 2)
            load_x((4, 5), x_in2)
            for n, (i, q) in enumerate(((1, 1), (1, 0))):
                load_mod(0, bc[2 + n], i, q).then_inc(S(0, "modc_in"), 16)
            const(upper[:, :], A["upper"])
            const(decay, A["ret_decay"].rearrange("a b c -> (a b c)").partition_broadcast(P))
            const(rw[:, :, :], A["router_w"].rearrange("(k p) n -> p k n", p=P))
            const(rbias, A["router_bias"].partition_broadcast(P))
            const(rev8, A["rev8"].partition_broadcast(P))
            const(rev32, A["rev32"].partition_broadcast(P))
            const(ovidx, A["ovidx"].partition_broadcast(P))
            const(ints[:, 0:NE], A["first_blocks"].partition_broadcast(P))
            const(less_none, A["assign_ids"])
            for n, name in enumerate(("na_q_norm", "na_k_norm")):
                const(nag[:, 2 * n:2 * n + 2, :].rearrange("p a b -> p (a b)"),
                      A[name].rearrange("a b -> (a b)").partition_broadcast(P))

            for l in range(DEPTH):
                sp.dma_start(cosF, A["cos_t"]).then_inc(S(l, "tab_in"), 16)
                sp.dma_start(sinF, A["sin_t"]).then_inc(S(l, "tab_in"), 16)
                n_parts = len(ada_pieces(l)) // KD
                q0 = ada_start(l) // KD
                if l:
                    sp.wait_ge(S(l - 1, "comb_done"), tiles(l - 1))
                first = 3 * l + (0 if l == 0 else 1)
                for q in range(q0, n_parts):
                    sp.dma_start(rows[:, q % 3, :], A["ada_b"][first + q]).then_inc(S(l, "rows_in"), 16)
                units, slots = proj_units(l), proj_slots(l)
                end = {w: step_end(l, w) for w in range(N_STEPS)}
                todo = [(end[w - 3] + 1, "weights", w) for w in range(3, N_STEPS)]
                todo += [(piece_slot(l, max(p - 2, ada_start(l))), "piece", p)
                         for p in range(ada_start(l), len(ada_pieces(l)))]
                todo += [(piece_slot(l, (q + 1) * KD - 1) + 2, "rows", q) for q in range(q0, n_parts)]
                todo += [(end[19] + 6, "bias_first", 0)]
                for _, what, n in sorted(todo, key=lambda x: x[0]):
                    if what == "weights":
                        sp.wait_ge(S(l, "slot_done"), end[n - 3] + 1)
                        load_w(l, n)
                    if what == "piece":
                        piece(l, n)
                    if what == "rows":
                        store_rows(l, n)
                    if what == "bias_first":
                        sp.wait_ge(S(l, "trow_done"), sum(needs_row(u) for u in units))
                        sp.dma_start(mask, A["na_mask"]).then_inc(S(l, "mask_in"), 16)
                        sp.dma_start(bias[0], A["rpb"][l][0]).then_inc(S(l, "bias_in0"), 16)
                sp.wait_ge(S(l, "slot_done"), len(slots))
                sp.dma_start(bias[1], A["rpb"][l][1]).then_inc(S(l, "bias_in1"), 16)
                meet(sp, "sp")
                sp.dma_start(va_shift[0:64, :, :], va[64:128, 0:3, :]).then_inc(S(l, "vshift"), 16)
                sp.dma_start(va_shift[64:128, :, :], va[0:64, 1:4, :]).then_inc(S(l, "vshift"), 16)
                for h in range(2, NAH):
                    sp.dma_start(bias[h], A["rpb"][l][h]).then_inc(S(l, "bias_in2"), 16)
                sp.dma_start(delta[0], A["delta"][0]).then_inc(S(l, "delta_in"), 16)
                meet(sp, "sp")

                sp.dma_start(delta[1], A["delta"][1]).then_inc(S(l, "delta_in2"), 16)
                sp.dma_start(dctx, A["delta_ctx"]).then_inc(S(l, "delta_in2"), 16)
                sp.dma_start(tabs[:, 256:256 + P + NBLK], A["numbers"].partition_broadcast(P))\
                    .then_inc(S(l, "numbers_in"), 16)
                wo = A["w_out"][l].rearrange("(k p) n -> p k n", p=P)
                sp.dma_start(wo0, wo[:, :, 0:CH]).then_inc(S(l, "wo_in0"), 16)
                for i in range(2):
                    load_mod(l, mix_gate[i], i, 2).then_inc(S(l, "gate_in"), 16)

                sp.wait_ge(S(l, "w_mult"), 2 * len(ret_steps(l)))
                sp.dma_start(wo1, wo[:, :, CH:D]).then_inc(S(l, "wo_in1"), 16)
                sp.wait_ge(S(l, "ret_norm"), len(ret_groups(l)))
                for n, (i, q) in enumerate(((0, 4), (0, 3), (1, 4), (1, 3))):
                    load_mod(l, bc[n][:, :], i, q).then_inc(S(l, "g_in"), 16)
                sp.dma_start(normw2, A["norm_ffn_w"][l].partition_broadcast(P)).then_inc(S(l, "g_in"), 16)

                def expert_gate(s, e):
                    sp.dma_start(wg[s], A["exp_w_gate"][l, e].rearrange("(k p) n -> p k n", p=P))\
                        .then_inc(S(l, f"wg_in{s}"), 16)

                def expert_up(s, e):
                    sp.dma_start(wu[s], A["exp_w_up"][l, e].rearrange("(k p) n -> p k n", p=P))\
                        .then_inc(S(l, f"wu_in{s}"), 16)

                def expert_down(s, e):
                    sp.dma_start(wd[s], A["exp_w_down"][l, e].rearrange("(k p) n -> p k n", p=P))\
                        .then_inc(S(l, f"wd_in{s}"), 16)

                for t in range(tiles(l)):
                    sp.wait_ge(S(l, "g_row"), t + 1)
                    sp.dma_start(h_d[t * P:(t + 1) * P, :], hrow2[t]).then_inc(S(l, "h_out"), 16)
                sp.wait_ge(S(l, "logit_done"), tiles(l))
                for s in range(2):
                    expert_gate(s, s)
                    expert_up(s, s)
                    if s == 0:
                        expert_down(s, s)
                sp.wait_ge(S(l, "h_out"), 16 * tiles(l))
                meet(sp, "sp")
                expert_down(1, 1)

                sp.wait_ge(S(l, "route_ready"), 1)
                n_pairs = sp.value_load(ints[0:1, 79:80], min_val=NE // 2, max_val=NBLK // 2 - 1)
                with sp.Fori(0, n_pairs - 1) as i:
                    for s in range(2):
                        e = sp.value_load(ints[0:1, bass.ds(2 * i + 2 + s, 1)], min_val=0, max_val=NE - 1)
                        sp.wait_ge(S(l, "wlo_ready"), (2 * i + s) * UNITS + 4)
                        expert_gate(s, e)
                        sp.wait_ge(S(l, "wlo_ready"), (2 * i + s) * UNITS + 8)
                        expert_up(s, e)
                        sp.wait_ge(S(l, "wlo_ready"), (2 * i + s) * UNITS + 12)
                        expert_down(s, e)
                sp.wait_ge(S(l, "y_out"), 32 * n_pairs + 16)
                for i in range(2):
                    load_mod(l, ffn_gate[i], i, 5).then_inc(S(l, "gb_in"), 16)
                if l < DEPTH - 1:
                    for n, (i, q) in enumerate(((0, 1), (0, 0), (1, 1), (1, 0))):
                        load_mod(l + 1, bc[n][:, :], i, q).then_inc(S(l, "next_in"), 16)
                meet(sp, "sp")
                if l < DEPTH - 1:
                    numbers = [s_.num for (k_, _), s_ in SEMS.items() if k_ is None]
                    sp.sem_clear(range(min(numbers), max(numbers) + 1)).then_inc(cleared, 1)
                    sp.dma_start(normw, A["norm_mix_w"][l + 1].partition_broadcast(P)).then_inc(S(l, "next_in"), 16)
                for t in range(tiles(l)):
                    for k, buf in ((0, y1), (1, y2)):
                        sp.dma_start(buf[t], y_d[k * TOK + t * P:k * TOK + (t + 1) * P, :])\
                            .then_inc(S(l, f"y_in{t}"), 16)
                    if l < DEPTH - 1 and 1 <= t <= 3:
                        load_w(l + 1, t - 1)
                if l == DEPTH - 1:
                    for t in range(LAT):
                        sp.wait_ge(S(l, "comb_done"), t + 1)
                        sp.dma_start(A["out"][t * P:(t + 1) * P, :], X[:, t, :]).then_inc(out_done, 16)
                    sp.wait_ge(out_done, 16 * LAT)

        @block.gpsimd
        def _(pool):
            link = chain(pool, "pool", pool_step)
            link(pool.memset(ones[:, :], 1.0))
            link(pool.memset(neghalf, -0.5))
            link(pool.memset(lnscale, math.log(RD ** -0.5)))
            for l in range(DEPTH):
                def shift_row(t):
                    pool.wait_ge(S(l, "hrow_scaled"), t + 1)
                    pool.tensor_tensor(hrow1[t % 2], hrow1[t % 2], bc[1 if t < LAT else 3][:, :], ALU.add)\
                        .then_inc(S(l, "hrow_ready"), 1)

                for t in range(NT):
                    if l:
                        pool.wait_ge(S(l - 1, "z_gated"), t + 1)
                        pool.tensor_tensor(X[:, t, :], X[:, t, :], y1[t], ALU.add)\
                            .then_inc(S(l - 1, "comb_done"), 1)
                    if t >= 1:
                        shift_row(t - 1)
                    pool.wait_ge(S(l, "ms_ready"), t + 1)
                    pool.tensor_tensor(rstd[:, t:t + 1], msq[:, t:t + 1], neghalf[:, 0:1], ALU.pow)\
                        .then_inc(S(l, "rstd_ready"), 1)
                shift_row(NT - 1)
                n = 0
                for u in proj_units(l):
                    if KIND[u[0]] == "norm":
                        b = n % 2
                        n += 1
                        pool.wait_ge(S(l, "qk_ms_ready"), n)
                        pool.tensor_tensor(qk_rs[:, b * NAH:(b + 1) * NAH], qk_ms[:, b * NAH:(b + 1) * NAH],
                                           neghalf[:, 0:NAH], ALU.pow).then_inc(S(l, "qk_rs_ready"), 1)
                pool.wait_ge(S(l, "mask_in"), 16)

                def mask_bias(what, heads):
                    pool.wait_ge(S(l, what), 16 * len(heads))
                    for h in heads:
                        pool.tensor_tensor(bias[h], bias[h], mask, ALU.add).then_inc(S(l, "bias_ready"), 1)

                mask_bias("bias_in0", (0,))
                meet(pool, "pool")
                mask_bias("bias_in1", (1,))
                pool.wait_ge(S(l, "bias_ready"), 2)
                nu = na_units(l)
                link(pool.memset(q_pad[1][64:128, 0, :], 0.0))
                link(pool.memset(q_pad[1][0:64, 1, :], 0.0))
                for hp in range(1, NAH // 2):
                    if hp >= 2:
                        pool.wait_ge(S(l, "s_done"), max(i for i, u in enumerate(nu) if u[0] == hp - 2) + 1)
                    pool.tensor_copy(q_pad[hp % 2][0:64, 0, :], qaT[0:64, hp, :]).then_inc(S(l, "qz_more"), 1)
                    pool.tensor_copy(q_pad[hp % 2][64:128, 1, :], qaT[64:128, hp, :]).then_inc(S(l, "qz_more"), 1)
                    if hp == 1:
                        pool.wait_ge(S(l, "qz_more"), 2)
                        mask_bias("bias_in2", range(2, NAH))
                        pool.wait_ge(S(l, "bias_ready"), NAH)
                meet(pool, "pool")
                groups = ret_groups(l)
                for g in range(len(groups)):
                    pool.wait_ge(S(l, "hvar_ready"), g + 1)
                    pool.tensor_tensor(hrstd, hvar, neghalf[:, 0:8], ALU.pow).then_inc(S(l, "hrstd_ready"), 1)
                    if g < len(groups) - last_groups(l):
                        for d in range(2):
                            v, gate, _ = normed(groups[g], d)
                            pool.wait_ge(S(l, "head_normed"), 2 * g + d + 1)
                            pool.tensor_tensor(v, v, gate, ALU.mult).then_inc(S(l, "head_gated"), 1)
                        pool.wait_ge(S(l, "head_gated"), 2 * g + 2)
                        (a, _, out), (b, _, _) = normed(groups[g], 0), normed(groups[g], 1)
                        pool.tensor_tensor(out, a, b, ALU.add).then_inc(S(l, "ret_norm"), 1)
                for t in range(tiles(l)):
                    pool.wait_ge(S(l, "g_ms"), t + 1)
                    pool.tensor_tensor(rstd[:, t:t + 1], msq[:, t:t + 1], neghalf[:, 0:1], ALU.pow)\
                        .then_inc(S(l, "g_rs"), 1)
                pool.wait_ge(S(l, "logit_done"), tiles(l))
                pool.wait_ge(S(l, "h_out"), 16 * tiles(l))
                for s in range(2):
                    link(pool.memset(xg[s], 0.0))

                def gather(s, column, cp_count):
                    pool.tensor_copy(idx_slot[s][:, :], token[:, column]).then_inc(S(l, f"idx_cp{s}"), 1)
                    pool.wait_ge(S(l, f"idx_cp{s}"), cp_count)
                    pool.sem_inc(pool_passed, 1)
                    pool.indirect_dma_start(xg[s], None, h_d, bass.IndirectOffsetOnAxis(ap=idx_slot[s][:, :], axis=0),
                                            bounds_check=TOK - 1, oob_is_err=False)\
                        .then_inc(S(l, f"xg_in{s}"), 16)

                pool.wait_ge(S(l, "token_ready"), 1)
                gather(0, slice(0, 1), 1)
                gather(1, slice(1, 2), 1)
                meet(pool, "pool")
                n_pairs = pool.value_load(ints[0:1, 79:80], min_val=NE // 2, max_val=NBLK // 2 - 1)

                def store(column, s, count):
                    pool.tensor_copy(y_idx[s], y_place[:, column]).then_inc(S(l, "y_idx_cp"), 1)
                    pool.wait_ge(S(l, "y_idx_cp"), count)
                    pool.sem_inc(pool_passed, 1)
                    pool.indirect_dma_start(y_d, bass.IndirectOffsetOnAxis(ap=y_idx[s], axis=0), yb[s], None,
                                            bounds_check=2 * TOK - 1, oob_is_err=False)\
                        .then_inc(S(l, "y_out"), 16)

                def store_last(b, s):
                    pool.wait_ge(S(l, "y_out"), 16 * b + 16)
                    pool.sem_inc(S(l, "yb_free"), 1)
                    pool.wait_ge(S(l, "y_copied"), 2 * b + 2)
                    store(bass.ds(b, 1), s, b + 2)

                store(slice(0, 1), 1, 1)
                pool.sem_inc(S(l, "yb_free"), 1)
                with pool.Fori(0, n_pairs) as i:
                    for s in range(2):
                        b = 2 * i + s
                        pool.wait_ge(S(l, f"xg_used{s}"), i + 1)
                        gather(s, bass.ds(b + 2, 1), i + 2)
                        store_last(b, s)
                store_last(2 * n_pairs, 0)
                pool.wait_ge(S(l, "y_out"), 32 * n_pairs + 32)
                for s in range(2):
                    pool.wait_ge(S(l, f"xg_in{s}"), 16 * n_pairs + 16)
                pool.sem_inc(pool_passed, 1)
                meet(pool, "pool")
                if l < DEPTH - 1:
                    pool.wait_ge(cleared, 1)
                    pool.drain()

        @block.tensor
        def _(pe):
            for l in range(DEPTH):
                def ada_piece(p):
                    ll, r, k = ada_pieces(l)[p]
                    q = p // KD
                    if k == 0 and q >= 1:
                        pe.wait_ge(S(l, "mod_rows"), q)
                    if p < ada_start(l):
                        w = ada_first[p // 2][:, p % 2]
                        pe.wait_ge(ada_first_in[p // 2], 16)
                    else:
                        w = ada_w[p % 2]
                        pe.wait_ge(S(l, f"ada_in{p % 2}"), 16 * ((p - ada_start(l)) // 2 + 1))
                    for j in range(4):
                        mm = pe.matmul(PS[7][32 * j:32 * j + 32, :], sc32[:, k, :], w[:, j, :],
                                       start=(k == 0), stop=(k == KD - 1), skip_group_check=True)
                    mm.then_inc(S(l, "ada_done"), 1)

                if l == 0:
                    pe.wait_ge(sc_ready, 1)
                for p in range(ada_start(l)):
                    ada_piece(p)
                if l == 0:
                    pe.wait_ge(ident_in, 16)

                def rows_to_T(t, row, banks, done, evacs):
                    for half in range(2):
                        u = 2 * t + half
                        if u >= len(banks):
                            for evac in evacs:
                                pe.wait_ge(evac, u - len(banks) + 1)
                        for i in range(4):
                            c = (half * 4 + i) * P
                            mm = pe.transpose(PS[banks[u % len(banks)]][:, i * P:(i + 1) * P], row[:, c:c + P],
                                              ident[:, :])
                        mm.then_inc(done, 1)

                def turn_h(t):
                    pe.wait_ge(S(l, "hrow_ready"), t + 1)
                    rows_to_T(t, hrow1[t % 2], [6, 7], S(l, "tr_done"), [S(l, "hT_ready"), S(l, "hlo_ready")])

                units, slots, at, turns, splits = proj_units(l), proj_slots(l), unit_at(l), turns_at(l), split_at(l)
                n_act, n_dve, n_row = (counted(units, f) for f in (act_reads, dve_reads, needs_row))

                def turn(n):
                    m = n_row[n] - 1
                    pe.wait_ge(S(l, "row_ready"), m + 1)
                    if m >= 1:
                        pe.wait_ge(S(l, "trow_evac"), m)
                    for i in range(4):
                        f, tile = divmod(i, 2)
                        o = tile * HC + f * P
                        mm = pe.transpose(PS[6][:, i * P:(i + 1) * P], rowbuf[m % 2][:, o:o + P], ident[:, :])
                    mm.then_inc(S(l, "trow_done"), 1)

                turn_h(0)
                turn_h(1)
                for s, (w, p) in enumerate(slots):
                    if s == step_start(l, w):
                        pe.wait_ge(S(l, "wch_ready"), w + 1)
                        pe.wait_ge(S(l, "wcl_ready"), w + 1)
                    if w == 0:
                        pe.wait_ge(S(l, "hT_ready"), 4 * p + 4)
                        pe.wait_ge(S(l, "hlo_ready"), 4 * p + 4)
                    before = last_in_bank(l, w, p) if w % 2 == 0 else None
                    if before is not None:
                        if n_act[before]:
                            pe.wait_ge(S(l, "act_rel"), n_act[before])
                        if n_dve[before]:
                            pe.wait_ge(S(l, "gate_rel"), n_dve[before])
                    bank = PS[3 * (w // 2 % 2) + p]
                    for tile in range(2):
                        t = 2 * p + tile
                        for k in range(4):
                            kk = 4 * (w % 2) + k
                            for i, (x, y) in enumerate(((h_hi, wc_hi), (h_lo, wc_hi), (h_hi, wc_lo))):
                                mm = pe.matmul(bank[:, tile * HC:(tile + 1) * HC], x[:, kk, t * P:(t + 1) * P],
                                               y[w % 3][:, k, :], start=(kk == 0 and i == 0 and tile == 0),
                                               stop=(kk == KD - 1 and i == 2), skip_group_check=True)
                    mm.then_inc(S(l, "slot_done"), 1)
                    if s == TURNS_AT - 1:
                        pe.wait_ge(S(l, "hT_ready"), 2 * NT)
                        pe.wait_ge(S(l, "hlo_ready"), 2 * NT)
                    if s in turns:
                        turn(turns[s])
                    if s in (0, 1, 3, 4):
                        turn_h({0: 2, 1: 3, 3: 4, 4: 5}[s])
                    if after_slot(l, s) is not None:
                        ada_piece(after_slot(l, s))
                meet(pe, "pe")

                nu = na_units(l)
                pe.wait_ge(S(l, "vshift"), 32)

                def scores(n):
                    hp, j, e, ranges, _, _ = nu[n]
                    if n == 0:
                        pe.wait_ge(S(l, "qz_first"), 1)
                    elif hp > nu[n - 1][0]:
                        pe.wait_ge(S(l, "qz_more"), 2 * hp)
                    if n >= 4:
                        pe.wait_ge(S(l, "p_ready"), n - 3)
                    o = 0
                    for k0, kn in ranges:
                        mm = pe.matmul(PS[S_BANKS[n % 4]][:, o:o + kn], q_pad[hp % 2][:, e, j * P:(j + 1) * P],
                                       kaT[:, hp, k0:k0 + kn], start=True, stop=True)
                        o += kn
                    mm.then_inc(S(l, "s_done"), 1)

                def turn_p(n):
                    tiles_ = nu[n][4]
                    pe.wait_ge(S(l, "diag_ready"), n + 1)
                    if n >= 2:
                        pe.wait_ge(S(l, "pt_evac"), n - 1)
                    for i in range(len(tiles_)):
                        mm = pe.matmul(PS[3 + n % 2][:, i * P:(i + 1) * P], pexp[n % 2][:, i * P:(i + 1) * P],
                                       diag[n % 2], start=True, stop=True)
                    mm.then_inc(S(l, "pt_done"), 1)

                def values(n):
                    hp, j, _, _, tiles_, _ = nu[n]
                    pe.wait_ge(S(l, "pt_evac"), n + 2)
                    o = na_bank(l, n)
                    if o >= 2 and (n == 0 or na_bank(l, n - 1) < o):
                        pe.wait_ge(S(l, "o_evac"), o - 1)
                    for i, vt in enumerate(tiles_):
                        for e in range(2):
                            h = 2 * hp + e
                            mm = pe.matmul(PS[5 + o % 2][64 * e:64 * e + 64, (j % LAT) * P:(j % LAT + 1) * P],
                                           v_rows(vt)[:, h * NAD:(h + 1) * NAD], pT[e][:, i, :],
                                           start=(i == 0), stop=(i == len(tiles_) - 1), skip_group_check=True)
                    mm.then_inc(S(l, "pv_done"), 1)

                for n in range(len(nu) + 3):
                    if n < len(nu):
                        scores(n)
                    if 2 <= n <= len(nu) + 1:
                        turn_p(n - 2)
                    if n >= 4 and n % 2 == 0:
                        values(n - 4)
                meet(pe, "pe")

                steps_r = ret_steps(l)

                def ret_scores(m):
                    g, a, r, qts, kt, _ = steps_r[m]
                    w = len(qts) * P
                    if m >= 2:
                        pe.wait_ge(S(l, "w_mult"), 2 * (m - 1))
                    pe.matmul(PS[m % 2][:, 0:w], kbT[:, r, kt * P:(kt + 1) * P],
                              qbT[:, r, qts[0] * P:qts[0] * P + w], start=True, stop=True)\
                        .then_inc(S(l, "st_done"), 1)

                ret_scores(0)
                for m, (g, a, r, qts, kt, end) in enumerate(steps_r):
                    if m + 1 < len(steps_r):
                        ret_scores(m + 1)
                    pe.wait_ge(S(l, "w_mult"), 2 * m + 2)
                    if a == 0 and g >= 3:
                        pe.wait_ge(S(l, "head_normed"), 2 * (g - 2))
                    for d in range(2):
                        for i in range(len(qts)):
                            mm = pe.matmul(ret_bank(g, d)[:, i * P:(i + 1) * P],
                                           Wd[m % 3][:, d, i * P:(i + 1) * P], vb[:, kt, r * RD:(r + 1) * RD],
                                           start=(a == 0 and i == 0), stop=end, skip_group_check=True)
                    mm.then_inc(S(l, "w_used_r"), 1)

                nt = tiles(l)

                def router(t):
                    pe.wait_ge(S(l, "g_row"), t + 1)
                    rows_to_T(t, hrow2[t], [2, 3], S(l, "g_tr"), [S(l, "g_hT")])
                    pe.wait_ge(S(l, "g_hT"), 2 * t + 2)
                    for k in range(KD):
                        mm = pe.matmul(PS[4][:, t * NE:(t + 1) * NE], hT2[:, k, t * P:(t + 1) * P], rw[:, k, :],
                                       start=(k == 0), stop=(k == KD - 1))
                    mm.then_inc(S(l, "logit_done"), 1)

                def project_out(c, t, ks):
                    for k in ks:
                        mm = pe.matmul(PS[OUT_BANKS[(c * nt + t) % 4]][:, :],
                                       (mixT_na, mixT)[k // 4][:, k % 4, t * P:(t + 1) * P], (wo0, wo1)[c][:, k, :],
                                       start=(k == 0), stop=(k == KD - 1))
                    return mm

                pe.wait_ge(S(l, "w_mult"), 2 * len(steps_r))
                pe.wait_ge(S(l, "head_normed"), 2 * (len(ret_groups(l)) - 2))
                pe.wait_ge(S(l, "wo_in0"), 16)
                for t in range(LAT):
                    project_out(0, t, range(4))
                pe.wait_ge(S(l, "ret_norm"), len(ret_groups(l)))
                for t in range(nt):
                    if t >= 4:
                        pe.wait_ge(S(l, "mt_evac"), t - 3)
                    for i in range(4):
                        mm = pe.transpose(PS[2 + t % 4][:, i * P:(i + 1) * P], mix[:, t, i * P:(i + 1) * P],
                                          ident[:, :])
                    mm.then_inc(S(l, "mt_done"), 1)
                for c in range(2):
                    if c == 1:
                        pe.wait_ge(S(l, "wo_in1"), 16)
                    for t in range(nt):
                        n = c * nt + t
                        if c == 0:
                            pe.wait_ge(S(l, "mt_evac"), t + 1)
                        if n >= 4:
                            pe.wait_ge(S(l, "x_upd"), n - 3)
                        project_out(c, t, range(4 if n < LAT else 0, KD)).then_inc(S(l, "op_done"), 1)
                        if c == 1 and t >= 2:
                            router(t - 2)
                router(nt - 2)
                router(nt - 1)
                pe.wait_ge(S(l, "m_ready"), 1)
                cols = PS[5][:, 0:(nt + 1) * NE]
                pe.matmul(cols, ones[:, :], route_t["before"][:, 0:nt + 1, :].rearrange("p t e -> p (t e)"),
                          start=True, stop=False, skip_group_check=True)
                pe.matmul(PS[5][:, 0:nt * NE], upper[:, :], route_t["M"][:, 0:nt, :].rearrange("p t e -> p (t e)"),
                          start=False, stop=True, skip_group_check=True).then_inc(S(l, "rank_done"), 1)
                pe.wait_ge(S(l, "places_ready"), 1)
                for j in range(2 * nt):
                    mm = pe.matmul(PS[0][:, 0:NBLK], in_row[:, j, :], route_t["in_blk"][:, j, :],
                                   start=(j == 0), stop=(j == 2 * nt - 1))
                mm.then_inc(S(l, "places_done"), 1)
                meet(pe, "pe")

                pe.wait_ge(S(l, "route_ready"), 1)

                def turn_x(s, half):
                    for i in range(4):
                        c = (half * 4 + i) * P
                        mm = pe.transpose(PS[half][:, i * P:(i + 1) * P], xg[s][:, c:c + P], ident[:, :])
                    return mm

                def unit(b, u, hi, lo, banks, start, stop):
                    pe.wait_ge(S(l, "whi_ready"), b * UNITS + u + 1)
                    products = [(hi, w_hi), (lo, w_hi), (hi, w_lo)]
                    if u >= 8:
                        products = [(hi, w_hi), (hi, w_lo), (lo, w_hi)]
                    for i, (x, w) in enumerate(products):
                        if w is w_lo:
                            pe.wait_ge(S(l, "wlo_ready"), b * UNITS + u + 1)
                        if u == 8 and i == 2:
                            pe.wait_ge(S(l, "alo_ready"), b + 1)
                        for k in range(2):
                            one = banks[0] is banks[1]
                            mm = pe.matmul(banks[k][:, :], x[k], w[u % 3][:, k, :],
                                           start=start and i == 0 and (k == 0 or not one),
                                           stop=stop and i == 2 and (k == 1 or not one))
                    mm.then_inc(S(l, "w_used"), 1)

                pe.wait_ge(S(l, "xg_in0"), 16)
                turn_x(0, 0).then_inc(S(l, "xt_done"), 1)
                turn_x(0, 1).then_inc(S(l, "xg_used0"), 1)
                n_pairs = pe.value_load(ints[0:1, 79:80], min_val=NE // 2, max_val=NBLK // 2 - 1)
                with pe.Fori(0, n_pairs) as i:
                    for s in range(2):
                        o = 1 - s
                        b = 2 * i + s
                        pe.wait_ge(S(l, "xhi_ready"), 2 * b + 2)
                        pe.wait_ge(S(l, "xlo_ready"), 2 * b + 2)
                        for u in range(8):
                            bank = PS[2 + u // 4]
                            k = 2 * (u % 4)
                            unit(b, u, [x_hi[:, k + q, :] for q in range(2)], [x_lo[:, k + q, :] for q in range(2)],
                                 [bank, bank], u % 4 == 0, u % 4 == 3)
                        pe.wait_ge(S(l, f"xg_in{o}"), 16 * i + 16 + 16 * s)
                        turn_x(o, 0).then_inc(S(l, "xt_done"), 1)
                        pe.wait_ge(S(l, "a_ready"), b + 1)
                        for f in range(4):
                            mm = pe.transpose(PS[4][:, f * P:(f + 1) * P], act[:, f * P:(f + 1) * P], ident[:, :])
                        mm.then_inc(S(l, "at_done"), 1)
                        turn_x(o, 1).then_inc(S(l, f"xg_used{o}"), 1)
                        pe.wait_ge(S(l, "ahi_ready"), b + 1)
                        pe.wait_ge(S(l, "y_copied"), 2 * b + 2)
                        for f in range(4):
                            unit(b, 8 + f, [a_hi[:, f, :]] * 2, [a_lo[:, f, :]] * 2, [PS[5], PS[6]], f == 0, f == 3)
                meet(pe, "pe")
                if l < DEPTH - 1:
                    pe.wait_ge(cleared, 1)
                    pe.drain()

        @block.scalar
        def _(act_e):
            link = chain(act_e, "act", act_step)
            act_e.wait_ge(cc_in, 16)
            act_e.activation(cth, cc, ACT.Tanh, scale=0.5).then_inc(sc_tanh, 1)

            def evac_h(l, t):
                for half in range(2):
                    u = 2 * t + half
                    act_e.wait_ge(S(l, "tr_done"), u + 1)
                    act_e.activation(h_hi[:, 4 * half:4 * half + 4, t * P:(t + 1) * P],
                                     PS[6 + half][:, :].rearrange("p (a b) -> p a b", a=4), ACT.Copy)\
                        .then_inc(S(l, "hT_ready"), 1)

            def high_w(l, w):
                act_e.wait_ge(S(l, f"wc_in{w % 3}"), 16 * (w // 3 + 1))
                act_e.activation(wc_hi[w % 3][:, :, :], wc[w % 3], ACT.Copy).then_inc(S(l, "wch_ready"), 1)

            def front(l, t):
                if t >= 1:
                    squares(l, t - 1)
                if t == 2:
                    high_w(l, 0)
                    high_w(l, 1)
                if t == 3:
                    high_w(l, 2)
                ahead = 3 if l == 0 else 2
                if 0 <= t - ahead <= NT - 3:
                    evac_h(l, t - ahead)

            def squares(l, t):
                if l == 0 and t % 2 == 0:
                    act_e.wait_ge((x_in0, x_in1, x_in2)[t // 2], 32)
                if t >= 2:
                    act_e.wait_ge(S(l, "ss_done"), t - 1)
                act_e.activation(junk[t % 2], X[:, t, :], ACT.Square, accum_out=ss[:, t:t + 1])\
                    .then_inc(S(l, "ss_done"), 1)

            for l in range(DEPTH):
                if l == 0:
                    for t in range(NT + 1):
                        front(0, t)
                    act_e.wait_ge(const_in, 16 * N_CONST)
                    act_e.activation(decay, decay, ACT.Exp).then_inc(decay_exp, 1)
                units, slots, at, turns, splits = proj_units(l), proj_slots(l), unit_at(l), turns_at(l), split_at(l)
                n_row = counted(units, needs_row)
                n_norm = counted(units, lambda u: KIND[u[0]] == "norm")

                def evac_row(n):
                    c, p, half, _ = units[n]
                    m = n_row[n] - 1
                    dst = {0: qaT, 1: kaT, 3: qbT, 4: kbT}[c]
                    act_e.wait_ge(S(l, "trow_done"), m + 1)
                    act_e.activation(dst[:, 2 * half:2 * half + 2, 2 * p * P:(2 * p + 2) * P],
                                     PS[6][:, :].rearrange("p (a b) -> p a b", a=2), ACT.Copy)\
                        .then_inc(S(l, "trow_evac"), 1)

                for s in range(len(slots) + 2):
                    if s in at:
                        n = at[s]
                        c, p, half, _ = units[n]
                        kind = KIND[c]
                        bank = proj_bank(units[n])
                        two = bank[:, :].rearrange("p (a b) -> p a b", a=2)
                        cols = slice(half * HC, (half + 1) * HC)
                        if kind == "gate" and KIND[units[n - 1][0]] != "gate":
                            act_e.wait_ge(S(l, "ada_done"), len(ada_pieces(l)))
                            act_e.wait_ge(S(l, "mod_out"), 16 * (len(ada_pieces(l)) // KD))
                        if act_reads(units[n]):
                            act_e.wait_ge(S(l, "slot_done"), s + 1)
                        if kind == "norm":
                            m = n_norm[n] - 1
                            if m >= 2:
                                act_e.wait_ge(S(l, "qk_ms_ready"), m - 1)
                            act_e.activation(sqbuf[m % 2], bank[:, :], ACT.Square).then_inc(S(l, "act_rel"), 1)
                        elif kind == "v":
                            act_e.activation({2: va, 5: vb}[c][:, 2 * p:2 * p + 2, cols], two, ACT.Copy)\
                                .then_inc(S(l, "act_rel"), 1)
                        elif kind == "gate":
                            act_e.activation({6: gf, 7: gb}[c][:, 2 * p:2 * p + 2, cols], two, ACT.Tanh, scale=0.5)\
                                .then_inc(S(l, "act_rel"), 1)
                    if s in turns:
                        evac_row(turns[s])
                    if s in (3, 4):
                        evac_h(l, s + 1)
                    if s in splits:
                        act_e.wait_ge(S(l, "slot_done"), s - 1)
                        high_w(l, splits[s])
                meet(act_e, "act_e")

                nu = na_units(l)

                def evac_p(n):
                    w = len(nu[n][4])
                    act_e.wait_ge(S(l, "pt_done"), n + 1)
                    if n >= 2:
                        act_e.wait_ge(S(l, "pv_done"), n // 2)
                    act_e.activation(pT[n % 2][:, 0:w, :],
                                     PS[3 + n % 2][:, 0:w * P].rearrange("p (a b) -> p a b", a=w), ACT.Copy)\
                        .then_inc(S(l, "pt_evac"), 1)

                for n in range(len(nu) + 6):
                    if 2 <= n < len(nu) + 2:
                        evac_p(n - 2)
                    if n < len(nu):
                        hp, j, e, ranges, _, _ = nu[n]
                        w = sum(k for _, k in ranges)
                        act_e.wait_ge(S(l, "nm_ready"), n + 1)
                        if n >= 2:
                            act_e.wait_ge(S(l, "pt_done"), n - 1)
                        act_e.activation(pexp[n % 2][:, 0:w], PS[S_BANKS[n % 4]][:, 0:w], ACT.Exp,
                                         bias=negmax[:, n % 4:n % 4 + 1], accum_out=rsum[:, n:n + 1])\
                            .then_inc(S(l, "p_ready"), 1)
                    for o, (hp, t0, w, last_unit) in enumerate(na_outputs(l)):
                        if n == last_unit + 5:
                            act_e.wait_ge(S(l, "pv_done"), (last_unit + 1) // 2)
                            act_e.activation(mixT_na[:, hp, t0 * P:(t0 + w) * P], PS[5 + o % 2][:, 0:w * P], ACT.Copy)\
                                .then_inc(S(l, "o_evac"), 1)
                meet(act_e, "act_e")

                act_e.wait_ge(S(l, "delta_in"), 16)
                act_e.wait_ge(lg_ready, 1)
                for m, (g, a, r, qts, _, _) in enumerate(ret_steps(l)):
                    w = len(qts) * P
                    if m == 3:
                        act_e.wait_ge(S(l, "delta_in2"), 32)
                    for d in range(2):
                        if m >= 2:
                            act_e.wait_ge(S(l, "w_mult"), 2 * m + d - 3)
                        src = delta[a // 3][:, a % 3, d, :] if qts[0] == 0 else dctx[:, d, a, :]
                        lg = decay[:, (l * 2 + d) * RH + r:(l * 2 + d) * RH + r + 1]
                        act_e.activation(dec[(2 * m + d) % 4][:, 0:w], src, ACT.Exp, bias=lnscale, scale=lg)\
                            .then_inc(S(l, "dec_ready"), 1)

                nt = tiles(l)
                for t in range(nt):
                    act_e.wait_ge(S(l, "mt_done"), t + 1)
                    act_e.activation(mixT[:, :, t * P:(t + 1) * P],
                                     PS[2 + t % 4][:, :].rearrange("p (a b) -> p a b", a=4), ACT.Copy)\
                        .then_inc(S(l, "mt_evac"), 1)

                for n in range(nt + 2):
                    if n >= 2:
                        t = n - 2
                        for half in range(2):
                            act_e.wait_ge(S(l, "g_tr"), 2 * t + half + 1)
                            act_e.activation(hT2[:, 4 * half:4 * half + 4, t * P:(t + 1) * P],
                                             PS[2 + half][:, :].rearrange("p (a b) -> p a b", a=4), ACT.Copy)\
                                .then_inc(S(l, "g_hT"), 1)
                    if n < nt:
                        act_e.wait_ge(S(l, "x_upd"), nt + n + 1)
                        if n >= 2:
                            act_e.wait_ge(S(l, "g_ss"), n - 1)
                        act_e.activation(junk2[n % 2], X[:, n, :], ACT.Square, accum_out=ss[:, n:n + 1])\
                            .then_inc(S(l, "g_ss"), 1)
                act_e.wait_ge(S(l, "logit_done"), nt)
                act_e.activation(route_t["score"][:, 0:nt, :].rearrange("p a b -> p (a b)"),
                                 PS[4][:, 0:nt * NE], ACT.Exp, scale=-1.0)\
                    .then_inc(S(l, "exp_done"), 1)
                meet(act_e, "act_e")

                act_e.wait_ge(S(l, "route_ready"), 1)

                def evac_x(half):
                    act_e.activation(x_hi[:, 4 * half:4 * half + 4, :],
                                     PS[half][:, :].rearrange("p (a b) -> p a b", a=4), ACT.Copy)\
                        .then_inc(S(l, "xhi_ready"), 1)

                act_e.wait_ge(S(l, "xt_done"), 1)
                evac_x(0)
                act_e.wait_ge(S(l, "xg_used0"), 1)
                evac_x(1)
                def evac_y(b, s):
                    act_e.wait_ge(S(l, "yb_free"), b + 1)
                    for c in range(2):
                        act_e.activation(yb[s][:, c * CH:(c + 1) * CH], PS[5 + c][:, :], ACT.Copy)\
                            .then_inc(S(l, "y_copied"), 1)

                act_e.sem_inc(S(l, "w_used"), 3)
                n_pairs = act_e.value_load(ints[0:1, 79:80], min_val=NE // 2, max_val=NBLK // 2 - 1)
                with act_e.Fori(0, n_pairs) as i:
                    for s in range(2):
                        o = 1 - s
                        b = 2 * i + s

                        def high(u):
                            if u % 4 == 0:
                                act_e.wait_ge(S(l, ("wg_in", "wu_in", "wd_in")[u // 4] + str(s)), 16 * i + 16)
                            act_e.wait_ge(S(l, "w_used"), b * UNITS + u + 1)
                            act_e.activation(w_hi[u % 3][:, :, :], raw(s, u), ACT.Copy).then_inc(S(l, "whi_ready"), 1)

                        for u in range(3):
                            high(u)
                        evac_y(b, s)
                        for u in range(3, 7):
                            high(u)
                        act_e.wait_ge(S(l, "w_used"), b * UNITS + 4 + 3)
                        act_e.activation(th, PS[2][:, :], ACT.Tanh, scale=0.5).then_inc(S(l, "th_ready"), 1)
                        for u in range(7, 10):
                            high(u)
                        act_e.wait_ge(S(l, "xt_done"), b + 2)
                        evac_x(0)
                        act_e.wait_ge(S(l, "at_done"), b + 1)
                        act_e.activation(a_hi[:, :, :], PS[4][:, :].rearrange("p (a b) -> p a b", a=4), ACT.Copy)\
                            .then_inc(S(l, "ahi_ready"), 1)
                        act_e.wait_ge(S(l, f"xg_used{o}"), i + 1 + s)
                        evac_x(1)
                        high(10)
                        high(11)
                act_e.wait_ge(S(l, "w_used"), 2 * n_pairs * UNITS + 3)
                evac_y(2 * n_pairs, 0)
                meet(act_e, "act_e")
                if l < DEPTH - 1:
                    act_e.wait_ge(cleared, 1)
                    act_e.drain()
                for t in range(nt + 1):
                    if t < nt:
                        act_e.wait_ge(S(l, f"y_in{t}"), 32)
                        act_e.activation(y1[t], y1[t], ACT.Copy, scale=wgt[:, 2 * t:2 * t + 1])\
                            .then_inc(S(l, "z_first"), 1)
                    if l < DEPTH - 1:
                        if t >= 1:
                            act_e.wait_ge(S(l, "comb_done"), t)
                        front(l + 1, t)

        @block.vector
        def _(dve):
            link = chain(dve, "dve", dve_step)
            def route(l):
                T = tiles(l)
                v = {}
                for n, a in route_t.items():
                    per = {NT: T, NT + 1: T + 1, 2 * NT: 2 * T, NT * NG: T * NG}.get(a.shape[1], a.shape[1])
                    v[n] = a[:, 0:per, :] if len(a.shape) == 3 else a[:, 0:per]

                def tt(out, a, b, op):
                    link(dve.tensor_tensor(out, a, b, op))

                def ts(out, a, x, op, y=None, op2=None):
                    link(dve.tensor_scalar(out, a, x, y, op, op2) if op2 is not None
                         else dve.tensor_scalar(out, a, x, None, op))

                def red(out, a, op):
                    link(dve.tensor_reduce(out, a, AX.X, op))

                def over(a, n):
                    return a.unsqueeze(2).broadcast_to([P, a.shape[1], n])

                def per_token(a, n, times=T):
                    return a.unsqueeze(1).broadcast_to([P, times, n])

                def two(a):
                    return a.unsqueeze(1).broadcast_to([P, 2, T, NE])

                def kte(a):
                    return a.rearrange("p (k t) e -> p k t e", k=2)

                dve.wait_ge(S(l, "exp_done"), 1)
                ts(v["score"], v["score"], 1.0, ALU.add)
                link(dve.reciprocal(v["score"], v["score"]))
                tt(v["ssel"], v["score"], per_token(rbias, NE), ALU.add)
                s4 = v["ssel"].rearrange("p t (g e) -> p (t g) e", e=EPG)
                o = 0
                for dist in range(1, EPG):
                    tt(v["pairs"][:, :, o:o + EPG - dist], s4[:, :, 0:EPG - dist], s4[:, :, dist:EPG], ALU.add)
                    o += EPG - dist
                red(v["gsum"].rearrange("p t g -> p (t g)"), v["pairs"], ALU.max)
                red(v["gmax"], v["gsum"], ALU.max)
                tt(v["gcand"], v["gsum"], over(v["gmax"], NG), ALU.is_equal)
                tt(v["gcand"], v["gcand"], per_token(rev8, NG), ALU.mult)
                red(v["gfirst"], v["gcand"], ALU.max)
                tt(v["ing"], per_token(rev8, NG), over(v["gfirst"], NG), ALU.is_equal)
                ts(v["pen"], v["ing"], BIG, ALU.mult, -BIG, ALU.add)
                tt(v["ms"].rearrange("p t (g e) -> p (t g) e", e=EPG), s4,
                   v["pen"].rearrange("p t g -> p (t g)").unsqueeze(2).broadcast_to([P, T * NG, EPG]), ALU.add)
                for k in range(2):
                    oh, first = v["oh"][:, k * T:(k + 1) * T, :], v["first"][:, k * T:(k + 1) * T]
                    red(v["top"], v["ms"], ALU.max)
                    tt(v["cand"], v["ms"], over(v["top"], NE), ALU.is_equal)
                    tt(v["cand"], v["cand"], per_token(rev32, NE), ALU.mult)
                    red(first, v["cand"], ALU.max)
                    tt(oh, per_token(rev32, NE), over(first, NE), ALU.is_equal)
                    if k == 0:
                        link(dve.scalar_tensor_tensor(v["ms"], oh, -BIG, v["ms"], ALU.mult, ALU.add))
                tt(v["M"], v["oh"][:, 0:T, :], v["oh"][:, T:2 * T, :], ALU.add)
                link(dve.memset(v["before"][:, 0, :], 0.0))
                for t in range(T):
                    i = dve.tensor_tensor(v["before"][:, t + 1, :], v["before"][:, t, :], v["M"][:, t, :], ALU.add)
                    if t < T - 1:
                        link(i)
                i.then_inc(S(l, "m_ready"), 1)
                tt(kte(v["tmp"]), kte(v["oh"]), two(v["score"]), ALU.mult)
                red(v["s"], v["tmp"], ALU.add)
                tt(v["top"], v["s"][:, 0:T], v["s"][:, T:2 * T], ALU.add)
                link(dve.reciprocal(v["top"], v["top"]))
                for k in range(2):
                    tt(wgt.rearrange("p (t k) -> p t k", k=2)[:, 0:T, k], v["s"][:, k * T:(k + 1) * T], v["top"],
                       ALU.mult)
                ts(v["e"], v["first"], -1.0, ALU.mult, float(NE), ALU.add)

                dve.wait_ge(S(l, "rank_done"), 1)
                ranks = PS[5][:, 0:T * NE].rearrange("p (t e) -> p t e", e=NE)
                tt(kte(v["tmp"]), kte(v["oh"]), two(ranks), ALU.mult)
                red(v["rank"], v["tmp"], ALU.add)
                ts(v["count"], PS[5][:, T * NE:(T + 1) * NE], 1.0 / P, ALU.mult)
                beyond = v["tmp"].rearrange("p a e -> p (a e)")[:, 0:NE * (T - 1)].rearrange("p (e m) -> p e m", e=NE)
                tt(beyond, over(v["count"], T - 1), per_token(ovidx[:, 1:T], T - 1, NE), ALU.is_gt)
                red(v["extra"], beyond, ALU.add)
                link(dve.memset(v["zero"], 0.0))
                link(dve.tensor_tensor_scan(v["ovinc"], v["extra"], v["zero"], 0.0, ALU.add, ALU.add))
                tt(v["ovb"], v["ovinc"], v["extra"], ALU.subtract)
                tt(v["tmp"], v["oh"], per_token(v["ovb"], NE, 2 * T), ALU.mult)
                red(v["ov"], v["tmp"], ALU.add)
                ts(v["full"], v["rank"], 1.0 / P, ALU.mult)
                qcmp = v["qcmp"][:, :, 0:T - 1]
                tt(qcmp, over(v["full"], T - 1), per_token(ovidx[:, 1:T], T - 1, 2 * T), ALU.is_ge)
                red(v["q"], qcmp, ALU.add)
                link(dve.scalar_tensor_tensor(v["r"], v["q"], -float(P), v["rank"], ALU.mult, ALU.add))
                ts(v["pos"], v["q"], 0.0, ALU.is_gt)
                link(dve.scalar_tensor_tensor(v["blk"], v["ov"], float(NE - 1), v["q"], ALU.add, ALU.add))
                tt(v["blk"], v["blk"], v["e"], ALU.subtract)
                tt(v["blk"], v["blk"], v["pos"], ALU.mult)
                tt(v["blk"], v["blk"], v["e"], ALU.add)
                dve.wait_ge(S(l, "numbers_in"), 16)
                tt(v["in_blk"], over(v["blk"], NBLK), per_token(blk_no, NBLK, 2 * T), ALU.is_equal)
                numbers = less_none.rearrange("p (k t) -> p k t", k=2)[:, :, 0:T].unsqueeze(3)\
                    .broadcast_to([P, 2, T, NBLK])
                tt(kte(v["in_blk"]), kte(v["in_blk"]), numbers, ALU.mult)
                dve.tensor_tensor(in_row[:, 0:2 * T, :], over(v["r"], P), per_token(row_no, P, 2 * T), ALU.is_equal)\
                    .then_inc(S(l, "places_ready"), 1)
                tt(v["ovcmp"], v["ovinc"].unsqueeze(1).broadcast_to([P, NOV, NE]),
                   ovidx.unsqueeze(2).broadcast_to([P, NOV, NE]), ALU.is_le)
                red(v["ovexp"], v["ovcmp"], ALU.add)
                dve.wait_ge(S(l, "places_done"), 1)
                ts(assign, PS[0][:, 0:NBLK], float(NO_ROW), ALU.add)
                ts(second, assign, float(TOK), ALU.is_ge)
                dve.scalar_tensor_tensor(token, second, -float(TOK), assign, ALU.mult, ALU.add)\
                    .then_inc(S(l, "token_ready"), 1)
                link(dve.memset(y_place[:, 0:1], NO_ROW))
                link(dve.tensor_copy(y_place[:, 1:NBLK + 1], assign))
                ts(ints[:, NE:NBLK], v["ovexp"], float(NE - 1), ALU.min)
                nov = v["ovinc"][:, NE - 1:NE]
                ts(v["npair"], nov, 0.0, ALU.is_gt, float(NE // 2), ALU.add)
                for m in range(1, NOV // 2 - 1):
                    link(dve.scalar_tensor_tensor(v["npair"], nov, 2.0 * m, v["npair"], ALU.is_gt, ALU.add))
                dve.tensor_copy(ints[:, 79:80], v["npair"]).then_inc(S(l, "route_ready"), 1)

            dve.wait_ge(cc_in, 16)
            link(dve.memset(sc32[:, :, :], 0.0))
            dve.wait_ge(sc_tanh, 1)
            link(dve.scalar_tensor_tensor(cth, cth, 1.0, cc, ALU.add, ALU.mult))
            dve.tensor_scalar(sc32[:, :, 0:2], cth.rearrange("p (k i) -> p k i", i=2), 0.5, None, ALU.mult)\
                .then_inc(sc_ready, 1)
            dve.wait_ge(S(0, "rows_in"), 16)
            dve.wait_ge(S(0, "ada_done"), KD)
            dve.tensor_tensor(rows[:, 0, :], PS[7][:, :], rows[:, 0, :], ALU.add).then_inc(S(0, "mod_rows"), 1)

            def scale_norm_weight(streams):
                for i in streams:
                    n = 2 * i
                    link(dve.scalar_tensor_tensor(bc[n][:, :], bc[n][:, :], 1.0, normw, ALU.add, ALU.mult))

            def mean_square(l, t):
                dve.wait_ge(S(l, "ss_done"), t + 1)
                dve.tensor_scalar(msq[:, t:t + 1], ss[:, t:t + 1], 1.0 / D, EPS, ALU.mult, ALU.add)\
                    .then_inc(S(l, "ms_ready"), 1)

            def mixer_row(l, t):
                dve.wait_ge(S(l, "rstd_ready"), t + 1)
                if t >= 2:
                    dve.wait_ge(S(l, "tr_done"), 2 * (t - 1))
                dve.scalar_tensor_tensor(hrow1[t % 2], X[:, t, :], rstd[:, t:t + 1], bc[0 if t < LAT else 2][:, :],
                                         ALU.mult, ALU.mult).then_inc(S(l, "hrow_scaled"), 1)

            def low_h(l, t):
                for half in range(2):
                    o = (slice(None), slice(4 * half, 4 * half + 4), slice(t * P, (t + 1) * P))
                    dve.wait_ge(S(l, "hT_ready"), 2 * t + half + 1)
                    dve.tensor_tensor(h_lo[o], PS[6 + half][:, :].rearrange("p (a b) -> p a b", a=4),
                                      h_hi[o].bitcast(F32), ALU.subtract).then_inc(S(l, "hlo_ready"), 1)

            def low_wc(l, w):
                dve.wait_ge(S(l, "wch_ready"), w + 1)
                dve.tensor_tensor(wc_lo[w % 3][:, :, :], wc[w % 3], wc_hi[w % 3][:, :, :].bitcast(F32), ALU.subtract)\
                    .then_inc(S(l, "wcl_ready"), 1)

            def front(l, t):
                if l and t >= 1:
                    mean_square(l, t - 1)
                if l and t in (2, 3, 4):
                    low_wc(l, t - 2)
                if t >= 1:
                    mixer_row(l, t - 1)
                if l == 0:
                    mean_square(l, t)
                    if t in (2, 3, 4):
                        low_wc(l, t - 2)
                if t in ((2, 3) if l == 0 else (2, 3, 4)):
                    low_h(l, t - 2)

            def front_end(l):
                if l:
                    mean_square(l, NT - 1)
                else:
                    low_h(l, 2)
                mixer_row(l, NT - 1)

            for l in range(DEPTH):
                if l == 0:
                    dve.wait_ge(S(l, "modb_in"), 48)
                    scale_norm_weight((0,))
                    for t in range(NT):
                        if t == LAT:
                            dve.wait_ge(S(l, "modc_in"), 32)
                            scale_norm_weight((1,))
                        front(l, t)
                    front_end(l)

                units, slots, at, turns, splits = proj_units(l), proj_slots(l), unit_at(l), turns_at(l), split_at(l)
                n_act, n_row = counted(units, act_reads), counted(units, needs_row)
                n_norm = counted(units, lambda u: KIND[u[0]] == "norm")

                def row_free(n):
                    m = n_row[n] - 1
                    if m >= 2:
                        dve.wait_ge(S(l, "trow_done"), m - 1)
                    return rowbuf[m % 2]

                def norm_front(n):
                    b = (n_norm[n] - 1) % 2
                    o = slice(b * NAH, (b + 1) * NAH)
                    dve.wait_ge(S(l, "act_rel"), n_act[n])
                    link(dve.tensor_reduce(qk_ss[:, o], sqbuf[b].rearrange("p (h d) -> p h d", h=NAH), AX.X, ALU.add))
                    dve.tensor_scalar(qk_ms[:, o], qk_ss[:, o], 1.0 / NAD, EPS, ALU.mult, ALU.add)\
                        .then_inc(S(l, "qk_ms_ready"), 1)

                def norm_back(n):
                    c = units[n][0]
                    b = (n_norm[n] - 1) % 2
                    row = row_free(n).rearrange("p (h d) -> p h d", h=NAH)
                    dve.wait_ge(S(l, "qk_rs_ready"), n_norm[n])
                    link(dve.tensor_tensor(row, proj_bank(units[n])[:, :].rearrange("p (h d) -> p h d", h=NAH),
                                           qk_rs[:, b * NAH:(b + 1) * NAH].unsqueeze(2)
                                           .broadcast_to([P, NAH, NAD]), ALU.mult))
                    dve.tensor_tensor(row, row, nag[:, 2 * c + l:2 * c + l + 1, :].broadcast_to([P, NAH, NAD]),
                                      ALU.mult).then_inc(S(l, "row_ready"), 1)

                def rope(n):
                    _, p, _, slot = units[n]
                    t = 2 * p
                    row = row_free(n)
                    bank = proj_bank(units[n])
                    dve.wait_ge(S(l, "slot_done"), slot + 1)
                    if t >= LAT:
                        dve.tensor_copy(row, bank[:, :]).then_inc(S(l, "row_ready"), 1)
                        return
                    v = bank[:, :].rearrange("p (t h a b) -> p t h a b", t=2, h=2, a=4)
                    q = sqbuf[n % 2].rearrange("p (t h a b) -> p t h a b", t=2, h=2, a=4)
                    link(dve.tensor_tensor(row.rearrange("p (t h d) -> p t h d", t=2, h=2),
                                           bank[:, :].rearrange("p (t h d) -> p t h d", t=2, h=2),
                                           cosF[:, t:t + 2, :].unsqueeze(2).broadcast_to([P, 2, 2, RD]), ALU.mult))
                    sn = sinF[:, t:t + 2, :].rearrange("p t (a b) -> p t a b", a=2)
                    for ax in range(2):
                        s2 = sn[:, :, ax:ax + 1, :].broadcast_to([P, 2, 2, 32])
                        link(dve.tensor_tensor(q[:, :, :, 2 * ax, :], v[:, :, :, 2 * ax + 1, :], s2, ALU.mult))
                        link(dve.tensor_tensor(q[:, :, :, 2 * ax + 1, :], v[:, :, :, 2 * ax, :], s2, ALU.mult))
                    for x in (0, 1):
                        i = dve.tensor_tensor(
                            row.rearrange("p (g b) -> p g b", b=32)[:, x::2, :],
                            row.rearrange("p (g b) -> p g b", b=32)[:, x::2, :],
                            sqbuf[n % 2].rearrange("p (g b) -> p g b", b=32)[:, x::2, :],
                            ALU.subtract if x == 0 else ALU.add)
                        if x == 0:
                            link(i)
                    i.then_inc(S(l, "row_ready"), 1)

                if l == 0:
                    dve.wait_ge(const_in, 16 * N_CONST)
                    dve.wait_ge(decay_exp, 1)
                    dve.tensor_scalar(decay, decay, -1.0, None, ALU.mult).then_inc(lg_ready, 1)
                    link(dve.tensor_scalar(nag[:, 0:2, :], nag[:, 0:2, :], NAD ** -0.5, None, ALU.mult))
                dve.wait_ge(S(l, "tab_in"), 32)
                q0 = ada_start(l) // KD
                n_parts = len(ada_pieces(l)) // KD
                for s in range(len(slots) + 1):
                    for q in range(q0, n_parts):
                        if s == piece_slot(l, (q + 1) * KD - 1) + 1:
                            dve.wait_ge(S(l, "rows_in"), 16 * n_parts)
                            dve.wait_ge(S(l, "ada_done"), (q + 1) * KD)
                            dve.tensor_tensor(rows[:, q % 3, :], PS[7][:, :], rows[:, q % 3, :], ALU.add)\
                                .then_inc(S(l, "mod_rows"), 1)
                    kind = KIND[units[at[s]][0]] if s in at else None
                    if kind == "norm":
                        norm_front(at[s])
                    if s - 1 in at and KIND[units[at[s - 1]][0]] == "norm":
                        norm_back(at[s - 1])
                    if kind == "rope":
                        rope(at[s])
                    if kind == "gate":
                        c, p, half, _ = units[at[s]]
                        g = {6: gf, 7: gb}[c][:, 2 * p:2 * p + 2, half * HC:(half + 1) * HC]
                        dve.wait_ge(S(l, "act_rel"), n_act[at[s]])
                        dve.scalar_tensor_tensor(g, g, 1.0, proj_bank(units[at[s]])[:, :]
                                                 .rearrange("p (a b) -> p a b", a=2), ALU.add, ALU.mult)\
                            .then_inc(S(l, "gate_rel"), 1)
                    if s in (1, 3, 4):
                        low_h(l, {1: 3, 3: 4, 4: 5}[s])
                    if s in splits:
                        low_wc(l, splits[s])
                meet(dve, "dve")

                link(dve.memset(q_pad[0][64:128, 0, :], 0.0))
                link(dve.memset(q_pad[0][0:64, 1, :], 0.0))
                link(dve.tensor_copy(q_pad[0][0:64, 0, :], qaT[0:64, 0, :]))
                dve.tensor_copy(q_pad[0][64:128, 1, :], qaT[64:128, 0, :]).then_inc(S(l, "qz_first"), 1)
                nu = na_units(l)

                def inverse_sum(n):
                    dve.wait_ge(S(l, "p_ready"), n + 1)
                    link(dve.reciprocal(rinv[:, n:n + 1], rsum[:, n:n + 1]))
                    if n >= 2:
                        dve.wait_ge(S(l, "pt_done"), n - 1)
                    dve.tensor_scalar(diag[n % 2], ident[:, :], rinv[:, n:n + 1], None, ALU.mult)\
                        .then_inc(S(l, "diag_ready"), 1)

                for n, (hp, j, e, ranges, _, ty) in enumerate(nu):
                    h = 2 * hp + e
                    b = PS[S_BANKS[n % 4]]
                    w = sum(k for _, k in ranges)
                    dve.wait_ge(S(l, "s_done"), n + 1)
                    if ty is not None:
                        if j == 0:
                            dve.wait_ge(S(l, "bias_ready"), h + 1)
                        link(dve.tensor_tensor(b[:, 0:KSPAN], b[:, 0:KSPAN], bias[h][:, ty, :], ALU.add))
                    if n >= 4:
                        dve.wait_ge(S(l, "p_ready"), n - 3)
                    dve.tensor_reduce(negmax[:, n % 4:n % 4 + 1], b[:, 0:w], AX.X, ALU.max, negate=True)\
                        .then_inc(S(l, "nm_ready"), 1)
                    if n >= 1:
                        inverse_sum(n - 1)
                inverse_sum(len(nu) - 1)
                meet(dve, "dve")

                groups = ret_groups(l)

                def head_norm(g, part):
                    r, lat, qts, kts = groups[g]
                    n = len(qts)
                    d = part % 2
                    if part == 0:
                        dve.wait_ge(S(l, "w_used_r"), ret_end(l, g))
                    if part == 2:
                        dve.wait_ge(S(l, "hrstd_ready"), g + 1)
                    o = [ret_bank(g, d)[:, i * P:(i + 1) * P] for i in range(n)]
                    u = [d * 4 + i for i in range(n)]
                    if part < 2:
                        for i in range(n):
                            ins = dve.bn_stats(bnst[:, u[i] * 6:u[i] * 6 + 6], o[i])
                        link(ins)
                        for i in range(n):
                            ins = dve.bn_aggr(mv[:, u[i] * 2:u[i] * 2 + 2], bnst[:, u[i] * 6:u[i] * 6 + 6])
                        link(ins)
                    else:
                        if d == 0 and g:
                            dve.wait_ge(S(l, "ret_norm"), g)
                        for i in range(n):
                            ins = dve.tensor_scalar(ofb[d][:, i * P:(i + 1) * P], o[i], mv[:, 2 * u[i]:2 * u[i] + 1],
                                                    hrstd[:, u[i]:u[i] + 1], ALU.subtract, ALU.mult)
                        ins.then_inc(S(l, "head_normed"), 1)
                    if part == 1:
                        dve.tensor_scalar(hvar, mv.rearrange("p (a b) -> p a b", b=2)[:, :, 1], RET_EPS, 4.0,
                                          ALU.add, ALU.mult).then_inc(S(l, "hvar_ready"), 1)
                    if part >= 2 and g >= len(groups) - last_groups(l):
                        v, gate, out = normed(groups[g], d)
                        dve.wait_ge(S(l, "head_normed"), 2 * g + d + 1)
                        link(dve.tensor_tensor(v, v, gate, ALU.mult))
                        if part == 3:
                            dve.tensor_tensor(out, normed(groups[g], 0)[0], v, ALU.add).then_inc(S(l, "ret_norm"), 1)

                link(dve.memset(mv, 0.0))
                for m, (g, a, r, qts, kt, _) in enumerate(ret_steps(l)):
                    w = len(qts) * P
                    for d in range(2):
                        dve.wait_ge(S(l, "st_done"), m + 1)
                        dve.wait_ge(S(l, "dec_ready"), 2 * m + d + 1)
                        if m >= 3:
                            dve.wait_ge(S(l, "w_used_r"), m - 2)
                        dve.tensor_tensor(Wd[m % 3][:, d, 0:w], PS[m % 2][:, 0:w], dec[(2 * m + d) % 4][:, 0:w],
                                          ALU.mult).then_inc(S(l, "w_mult"), 1)
                    behind = last_groups(l)
                    first = g - g % behind
                    slot = a if g == first else NT + a
                    if behind == 1:
                        slot = a - 1
                    if first and 0 <= slot < 4 * behind:
                        head_norm(first - behind + slot // 4, slot % 4)
                for x in range(len(groups) - last_groups(l), len(groups)):
                    for part in range(4):
                        head_norm(x, part)

                nt = tiles(l)
                dve.wait_ge(S(l, "g_in"), 80)
                for n in (0, 2):
                    link(dve.scalar_tensor_tensor(bc[n][:, :], bc[n][:, :], 1.0, normw2, ALU.add, ALU.mult))
                dve.wait_ge(S(l, "gate_in"), 32)

                def ffn_row(t):
                    a, b = (0, 1) if t < LAT else (2, 3)
                    dve.wait_ge(S(l, "g_rs"), t + 1)
                    link(dve.scalar_tensor_tensor(hrow2[t], X[:, t, :], rstd[:, t:t + 1], bc[a][:, :],
                                                  ALU.mult, ALU.mult))
                    dve.tensor_tensor(hrow2[t], hrow2[t], bc[b][:, :], ALU.add).then_inc(S(l, "g_row"), 1)

                for n in range(2 * nt):
                    c, t = divmod(n, nt)
                    dve.wait_ge(S(l, "op_done"), n + 1)
                    link(dve.tensor_tensor(otmp[n % 2], PS[OUT_BANKS[n % 4]][:, :],
                                           mix_gate[0 if t < LAT else 1][:, c * CH:(c + 1) * CH], ALU.mult))
                    xs = X[:, t, c * CH:(c + 1) * CH]
                    dve.tensor_tensor(xs, xs, otmp[n % 2], ALU.add).then_inc(S(l, "x_upd"), 1)
                    if c == 1:
                        if t >= 1:
                            ffn_row(t - 1)
                        dve.wait_ge(S(l, "g_ss"), t + 1)
                        dve.tensor_scalar(msq[:, t:t + 1], ss[:, t:t + 1], 1.0 / D, EPS, ALU.mult, ALU.add)\
                            .then_inc(S(l, "g_ms"), 1)
                ffn_row(nt - 1)
                route(l)
                meet(dve, "dve")

                n_pairs = dve.value_load(ints[0:1, 79:80], min_val=NE // 2, max_val=NBLK // 2 - 1)

                def low(dst, src, hi, ready):
                    dve.tensor_tensor(dst, src, hi.bitcast(F32), ALU.subtract).then_inc(S(l, ready), 1)

                def low_x(half):
                    o = slice(4 * half, 4 * half + 4)
                    low(x_lo[:, o, :], PS[half][:, :].rearrange("p (a b) -> p a b", a=4), x_hi[:, o, :], "xlo_ready")

                for half in range(2):
                    dve.wait_ge(S(l, "xhi_ready"), half + 1)
                    low_x(half)
                with dve.Fori(0, n_pairs) as i:
                    for s in range(2):
                        b = 2 * i + s

                        def low_w(u):
                            dve.wait_ge(S(l, "whi_ready"), b * UNITS + u + 1)
                            low(w_lo[u % 3][:, :, :], raw(s, u), w_hi[u % 3][:, :, :], "wlo_ready")

                        for u in range(8):
                            low_w(u)
                        dve.wait_ge(S(l, "th_ready"), b + 1)
                        dve.scalar_tensor_tensor(act, th, 1.0, PS[2][:, :], ALU.add, ALU.mult)\
                            .then_inc(S(l, "gate_step"), 1)
                        dve.wait_ge(S(l, "gate_step"), b + 1)
                        dve.wait_ge(S(l, "w_used"), b * UNITS + 8 + 3)
                        dve.scalar_tensor_tensor(act, act, 0.5, PS[3][:, :], ALU.mult, ALU.mult)\
                            .then_inc(S(l, "a_ready"), 1)
                        low_w(8)
                        dve.wait_ge(S(l, "ahi_ready"), b + 1)
                        low(a_lo[:, :, :], PS[4][:, :].rearrange("p (a b) -> p a b", a=4), a_hi[:, :, :], "alo_ready")
                        low_w(9)
                        dve.wait_ge(S(l, "xhi_ready"), 2 * b + 3)
                        low_x(0)
                        dve.wait_ge(S(l, "xhi_ready"), 2 * b + 4)
                        low_x(1)
                        low_w(10)
                        low_w(11)
                meet(dve, "dve")

                if l < DEPTH - 1:
                    dve.wait_ge(cleared, 1)
                    dve.drain()
                    dve.wait_ge(S(l, "next_in"), 80)
                    scale_norm_weight((0, 1))
                dve.wait_ge(S(l, "gb_in"), 32)
                for t in range(nt):
                    v = y1[t]
                    dve.wait_ge(S(l, "z_first"), t + 1)
                    link(dve.scalar_tensor_tensor(v, y2[t], wgt[:, 2 * t + 1:2 * t + 2], v, ALU.mult, ALU.add))
                    dve.tensor_tensor(v, v, ffn_gate[0 if t < LAT else 1], ALU.mult).then_inc(S(l, "z_gated"), 1)
                    if l < DEPTH - 1:
                        front(l + 1, t)
                    else:
                        dve.wait_ge(S(l, "z_gated"), t + 1)
                        dve.tensor_tensor(X[:, t, :], X[:, t, :], v, ALU.add).then_inc(S(l, "comb_done"), 1)
                if l < DEPTH - 1:
                    front_end(l + 1)


def _constants():
    f = np.float32
    tok = np.arange(SEQ)
    col, row = tok // ROWS, tok % ROWS
    time = row * COLS + col
    freqs = 10000.0 ** (-np.arange(32, dtype=np.float64) / 32)
    ang = np.stack([row[:, None] * freqs, col[:, None] * freqs], axis=1)
    cos = np.repeat(np.cos(ang)[:, :, None, :], 2, axis=2).reshape(LAT, P, RD)
    sin = np.sin(ang).reshape(LAT, P, 64)
    ct = np.arange(CTX)
    fwd = np.concatenate([np.where(time[None] >= time[:, None], time[None] - time[:, None], BIG),
                          time[None] + CTX - ct[:, None]])
    bwd = np.concatenate([np.where(time[None] <= time[:, None], time[:, None] - time[None], BIG),
                          ct[:, None] + SEQ - time[None]])
    cf = np.where(ct[None] >= ct[:, None], ct[None] - ct[:, None], BIG)
    delta = np.stack([fwd, bwd]).reshape(2, NT, P, SEQ).transpose(2, 0, 1, 3)
    dctx = np.stack([cf, cf.T]).reshape(2, 2, P, CTX).transpose(2, 0, 1, 3)
    mask = np.zeros((P, 3, KSPAN))
    for ty, j in ((0, 0), (1, 1), (2, 3)):
        qcol = j * QBLK + np.arange(QBLK)
        c0 = np.clip(qcol - WIN_W // 2, 0, COLS - WIN_W)
        kcol = KSTART[j] + np.arange(KBLK)
        ok = (kcol[None] >= c0[:, None]) & (kcol[None] < c0[:, None] + WIN_W)
        mask[:, ty] = np.repeat(np.repeat(np.where(ok, 0.0, -BIG), ROWS, 0), ROWS, 1)
    return {
        "ident": np.eye(P, dtype=f), "upper": np.triu(np.ones((P, P), f), 1),
        "cos_t": cos.transpose(1, 0, 2).astype(f), "sin_t": sin.transpose(1, 0, 2).astype(f),
        "delta": np.stack([delta[:, :, 3 * i:3 * i + 3].transpose(0, 2, 1, 3) for i in range(2)]).astype(f),
        "delta_ctx": dctx.astype(f), "na_mask": mask.astype(f),
        "rev8": (NG - np.arange(NG)).astype(f), "rev32": (NE - np.arange(NE)).astype(f),
        "ovidx": np.arange(NOV).astype(f), "first_blocks": np.arange(NE, dtype=np.int32),
        "assign_ids": (np.arange(2 * NT)[None] * P + np.arange(P)[:, None] - NO_ROW).astype(f),
        "numbers": np.concatenate([np.arange(P), np.arange(NBLK)]).astype(f),
    }


def kernel(**inputs):
    import concourse.bacc as bacc
    from concourse.bass_utils import run_bass_kernel_spmd

    x = {k: np.asarray(v) for k, v in inputs.items()}
    arrays = {n: x[n] for n in ("ada_w", "norm_mix_w", "norm_ffn_w", "na_q_norm", "na_k_norm",
                                "ret_decay", "w_out", "router_w", "router_bias", "exp_w_gate", "exp_w_up",
                                "exp_w_down")}
    arrays["x"] = x["x"][0].reshape(ROWS, COLS, D).transpose(1, 0, 2).reshape(SEQ, D)
    arrays["ctx"] = x["ctx"][0]
    arrays["cc"] = np.stack([x["c"][0], x["c_ctx"]], -1).reshape(KD, P, 2).transpose(1, 0, 2).reshape(P, 2 * KD)
    rpb = x["na_rpb"]
    win = np.stack([rpb[:, :, ROWS - 1 - q:2 * ROWS - 1 - q, :] for q in range(ROWS)], 2).transpose(0, 1, 2, 4, 3)
    win = np.pad(win, ((0, 0), (0, 0), (0, 0), (V_PAD, V_PAD), (0, 0)))
    win = np.stack([np.stack([win[:, :, :, (o := V_PAD + WIN_W - 1 + b - q):o + KBLK] for b in BIAS_START], 3)
                    for q in range(QBLK)], 2)
    arrays["rpb"] = win.reshape(DEPTH, NAH, P, 3, KSPAN)
    arrays["w_in"] = x["w_in"].reshape(DEPTH, 2, 4, P, 16, HC).transpose(0, 4, 1, 3, 2, 5)\
        .reshape(DEPTH, N_STEPS, P, 4, HC)
    ada_b = np.zeros((DEPTH, 3, 4, 32, CH), np.float32)
    ada_b[:, :, :, 0:2] = x["ada_b"].reshape(DEPTH, 3, 4, 1, CH)
    arrays["ada_b"] = ada_b.reshape(DEPTH * 3, P, CH)
    arrays.update(_constants())
    arrays = {n: np.ascontiguousarray(a) for n, a in arrays.items()}
    nc = bacc.Bacc("TRN2", target_bir_lowering=False, num_devices=1)
    aps = {n: nc.dram_tensor(f"in_{n}", a.shape, mybir.dt.from_np(a.dtype), kind="ExternalInput").ap()
           for n, a in arrays.items()}
    aps["out"] = nc.dram_tensor("out_x", (SEQ, D), F32, kind="ExternalOutput").ap()
    build(nc, aps)
    r = run_bass_kernel_spmd(nc, [{f"in_{n}": a for n, a in arrays.items()}], core_ids=[0])
    out = r.results[0]["out_x"]
    return out.reshape(COLS, ROWS, D).transpose(1, 0, 2).reshape(1, SEQ, D)
```
